# Optimizing a Trainium2 kernel written in Bass

```python
import math
import jax
import jax.numpy as jnp
from jax import lax
import numpy as np

D_MODEL = 1024
BATCH = 1
SEQ = 512
DEPTH = 2

F32 = jnp.float32
N_BRANCH = 4
ROPE_THETA = 500000.0
NORM_EPS = 1e-6
Q_BLOCK = 128
NEG_INF = -1e30

GDN_HEADS = 4
GDN_DK = 64
GDN_DV = 64
GDN_CONV = 4
GDN_CHUNK = 64
MLA_HEADS = 4
MLA_Q_LORA = 256
MLA_KV_LORA = 128
MLA_NOPE = 64
MLA_ROPE = 32
MLA_DV = 64
RWKV_HEADS = 4
RWKV_DH = 64
RWKV_DECAY_LORA = 64
RWKV_AAA_LORA = 64
RWKV_GATE_LORA = 128
RWKV_GN_EPS = 64e-5
DSA_HEADS = 4
DSA_DH = 64
IDX_HEADS = 8
IDX_DH = 64
IDX_TOPK_MAX = 256
D_FF = 4 * D_MODEL

GDN_QKV = 2 * GDN_HEADS * GDN_DK + GDN_HEADS * GDN_DV
GDN_SPLITS = (GDN_QKV, GDN_HEADS, GDN_HEADS, GDN_HEADS * GDN_DV)
MLA_SPLITS = (MLA_Q_LORA, MLA_KV_LORA, MLA_ROPE)
RWKV_W = RWKV_HEADS * RWKV_DH
RWKV_SPLITS = (RWKV_W, RWKV_W, RWKV_W, RWKV_DECAY_LORA, RWKV_AAA_LORA, RWKV_GATE_LORA)
DSA_W = DSA_HEADS * DSA_DH
DSA_SPLITS = (IDX_HEADS * IDX_DH, IDX_DH, IDX_HEADS, DSA_W, DSA_W, DSA_W)
GATE_SPLITS = (D_MODEL,) * N_BRANCH
SLAB_SPLITS = (sum(GDN_SPLITS), sum(MLA_SPLITS), sum(RWKV_SPLITS), sum(DSA_SPLITS), sum(GATE_SPLITS))
N_IN = sum(SLAB_SPLITS)
GDN_W = GDN_HEADS * GDN_DV
MLA_W = MLA_HEADS * MLA_DV
RWKV_IN = sum(RWKV_SPLITS)

kernel_name = "hybrid_gdn_mla_rwkv7_dsa_trunk"

def _split(t, sizes):
    return jnp.split(t, np.cumsum(sizes)[:-1].tolist(), axis=-1)

def rms_norm(x, g, eps=NORM_EPS):
    x32 = x.astype(F32)
    y = x32 * lax.rsqrt(jnp.mean(x32 * x32, axis=-1, keepdims=True) + eps)
    return (y * g.astype(F32)).astype(x.dtype)

def l2_normalize(x, eps=1e-6):
    x32 = x.astype(F32)
    return x32 * lax.rsqrt(jnp.sum(x32 * x32, axis=-1, keepdims=True) + eps)

def rotary_tables(positions, rot_dims):
    inv_freq = ROPE_THETA ** (-jnp.arange(0, rot_dims, 2, dtype=F32) / rot_dims)
    ang = positions.astype(F32)[..., None] * inv_freq
    return jnp.cos(ang), jnp.sin(ang)

def apply_rotary(x, cos, sin):
    half = cos.shape[-1]
    if x.ndim == 4:
        cos, sin = cos[:, :, None, :], sin[:, :, None, :]
    x1 = x[..., :half].astype(F32)
    x2 = x[..., half:2 * half].astype(F32)
    rot = jnp.concatenate([x1 * cos - x2 * sin, x2 * cos + x1 * sin], axis=-1).astype(x.dtype)
    return jnp.concatenate([rot, x[..., 2 * half:]], axis=-1)

def causal_depthwise_conv(x, w):
    k, c = w.shape
    return lax.conv_general_dilated(x, w[:, None, :].astype(x.dtype), window_strides=(1,),
                                    padding=[(k - 1, 0)], dimension_numbers=('NWC', 'WIO', 'NWC'),
                                    feature_group_count=c)

def token_shift(x):
    return jnp.pad(x, ((0, 0), (1, 0), (0, 0)))[:, :-1]

def gated_delta_rule_chunked(q, k, v, g, beta):
    b, t, h, dk = q.shape
    dv = v.shape[-1]
    c = GDN_CHUNK
    n = t // c

    def to_chunks(a):
        a = a.reshape((b, n, c, h) + a.shape[3:])
        return jnp.moveaxis(a, (1, 3), (0, 2))

    q = to_chunks(q * dk ** -0.5)
    k = to_chunks(k)
    v = to_chunks(v)
    g = to_chunks(g)
    beta = to_chunks(beta)
    gc = jnp.cumsum(g, axis=-1)
    incl = jnp.tril(jnp.ones((c, c), bool))
    strict = jnp.tril(jnp.ones((c, c), bool), -1)
    decay = jnp.exp(jnp.where(incl, gc[..., :, None] - gc[..., None, :], -jnp.inf))
    k_beta = k * beta[..., None]
    v_beta = v * beta[..., None]
    m = jnp.where(strict, jnp.einsum('nbhcd,nbhsd->nbhcs', k_beta, k) * decay, 0.0)
    eye = jnp.eye(c, dtype=m.dtype)
    t_inv = lax.linalg.triangular_solve(eye + m, jnp.broadcast_to(eye, m.shape),
                                        left_side=True, lower=True)
    u = t_inv @ v_beta
    w = t_inv @ (k_beta * jnp.exp(gc)[..., None])
    a_intra = jnp.einsum('nbhcd,nbhsd->nbhcs', q, k) * decay
    q_dec = q * jnp.exp(gc)[..., None]
    k_dec = k * jnp.exp(gc[..., -1:] - gc)[..., None]
    g_last = jnp.exp(gc[..., -1])

    def step(state, xs):
        q_d, k_d, u_c, w_c, a_c, gl = xs
        v_new = u_c - w_c @ state
        o = q_d @ state + a_c @ v_new
        state = state * gl[..., None, None] + jnp.swapaxes(k_d, -1, -2) @ v_new
        return state, o

    s0 = jnp.zeros((b, h, dk, dv), F32)
    _, o = lax.scan(step, s0, (q_dec, k_dec, u, w, a_intra, g_last))
    return jnp.moveaxis(o, (0, 2), (1, 3)).reshape(b, t, h, dv)

def gdn_mixer(p, conv_w, a_log, dt_bias, norm_g):
    b, s, _ = p.shape
    qkv, a, beta_logit, z = _split(p, GDN_SPLITS)
    qkv = jax.nn.silu(causal_depthwise_conv(qkv, conv_w)).astype(F32)
    q, k, v = _split(qkv, (GDN_HEADS * GDN_DK, GDN_HEADS * GDN_DK, GDN_HEADS * GDN_DV))
    q = l2_normalize(q.reshape(b, s, GDN_HEADS, GDN_DK))
    k = l2_normalize(k.reshape(b, s, GDN_HEADS, GDN_DK))
    v = v.reshape(b, s, GDN_HEADS, GDN_DV)
    beta = jax.nn.sigmoid(beta_logit.astype(F32))
    g = -jnp.exp(a_log.astype(F32)) * jax.nn.softplus(a.astype(F32) + dt_bias.astype(F32))
    o = gated_delta_rule_chunked(q, k, v, g, beta)
    o = rms_norm(o, norm_g) * jax.nn.silu(z.astype(F32).reshape(b, s, GDN_HEADS, GDN_DV))
    return o.reshape(b, s, GDN_W).astype(p.dtype)

def causal_block_attention(q, k, v, scale):
    b, s, h, _ = q.shape
    key_pos = jnp.arange(s)

    def block(i):
        start = i * Q_BLOCK
        qb = lax.dynamic_slice_in_dim(q, start, Q_BLOCK, axis=1)
        sc = jnp.einsum('bqhd,bkhd->bhqk', qb, k, preferred_element_type=F32) * scale
        q_pos = start + jnp.arange(Q_BLOCK)
        sc = jnp.where(key_pos[None, :] <= q_pos[:, None], sc, NEG_INF)
        pr = jax.nn.softmax(sc, axis=-1)
        return jnp.einsum('bhqk,bkhd->bqhd', pr.astype(v.dtype), v)

    o = lax.map(block, jnp.arange(s // Q_BLOCK))
    return jnp.moveaxis(o, 0, 1).reshape(b, s, h, v.shape[-1])

def mla_mixer(p, rope, q_norm_g, kv_norm_g, w_uq, w_ukv):
    b, s, _ = p.shape
    c_q, c_kv, k_rope = _split(p, MLA_SPLITS)
    q = (rms_norm(c_q, q_norm_g) @ w_uq).reshape(b, s, MLA_HEADS, MLA_NOPE + MLA_ROPE)
    q = jnp.concatenate([q[..., :MLA_NOPE], apply_rotary(q[..., MLA_NOPE:], *rope)], axis=-1)
    kv = (rms_norm(c_kv, kv_norm_g) @ w_ukv).reshape(b, s, MLA_HEADS, MLA_NOPE + MLA_DV)
    k_nope, v = kv[..., :MLA_NOPE], kv[..., MLA_NOPE:]
    k_rope = apply_rotary(k_rope, *rope)
    k = jnp.concatenate([k_nope, jnp.broadcast_to(k_rope[:, :, None, :], (b, s, MLA_HEADS, MLA_ROPE))], axis=-1)
    o = causal_block_attention(q, k, v, (MLA_NOPE + MLA_ROPE) ** -0.5)
    return o.reshape(b, s, MLA_W)

def rwkv7_scan(r, w, k, v, kk, a):
    b, t, h, n = r.shape

    def step(state, xs):
        r_t, w_t, k_t, v_t, kk_t, a_t = xs
        sa = jnp.einsum('bhvk,bhk->bhv', state, -kk_t)
        state = (state * w_t[:, :, None, :] + sa[..., None] * (kk_t * a_t)[:, :, None, :]
                 + v_t[..., None] * k_t[:, :, None, :])
        return state, jnp.einsum('bhvk,bhk->bhv', state, r_t)

    xs = tuple(jnp.moveaxis(z, 1, 0) for z in (r, w, k, v, kk, a))
    _, o = lax.scan(step, jnp.zeros((b, h, n, n), F32), xs)
    return jnp.moveaxis(o, 0, 1)

def rwkv7_mixer(p, mu, w0, w_w2, a0, w_a2, w_g2, k_k, k_a, r_k, ln_w, ln_b):
    b, s, _ = p.shape
    p = p + (token_shift(p) - p) * mu
    r, k, v, xw, xa, xg = _split(p.astype(F32), RWKV_SPLITS)
    w_log = -jax.nn.softplus(-(w0.astype(F32) + jnp.tanh(xw) @ w_w2.astype(F32))) - 0.5
    decay = jnp.exp(-jnp.exp(w_log))
    a = jax.nn.sigmoid(a0.astype(F32) + xa @ w_a2.astype(F32))
    g = jax.nn.sigmoid(xg) @ w_g2.astype(F32)
    heads = lambda z: z.reshape(b, s, RWKV_HEADS, RWKV_DH)
    kk = l2_normalize(heads(k * k_k.astype(F32)))
    k = k * (1.0 + (a - 1.0) * k_a.astype(F32))
    r, k, v, a, decay = heads(r), heads(k), heads(v), heads(a), heads(decay)
    o = rwkv7_scan(r, decay, k, v, kk, a)
    mean = jnp.mean(o, axis=-1, keepdims=True)
    var = jnp.mean(jnp.square(o - mean), axis=-1, keepdims=True)
    o = ((o - mean) * lax.rsqrt(var + RWKV_GN_EPS)).reshape(b, s, RWKV_W) * ln_w.astype(F32) + ln_b.astype(F32)
    bonus = jnp.sum(r * k * r_k.astype(F32), axis=-1, keepdims=True) * v
    o = (o + bonus.reshape(b, s, RWKV_W)) * g
    return o.astype(p.dtype)

def dsa_mixer(p, rope_idx, rope_att):
    b, s, _ = p.shape
    iq, ik, iw, q, k, v = _split(p, DSA_SPLITS)
    iq = apply_rotary(iq.reshape(b, s, IDX_HEADS, IDX_DH), *rope_idx)
    ik = apply_rotary(ik, *rope_idx)
    iw = iw.astype(F32) * (IDX_HEADS ** -0.5 * IDX_DH ** -0.5)
    q = apply_rotary(q.reshape(b, s, DSA_HEADS, DSA_DH), *rope_att)
    k = apply_rotary(k.reshape(b, s, DSA_HEADS, DSA_DH), *rope_att)
    v = v.reshape(b, s, DSA_HEADS, DSA_DH)
    n_sel = min(IDX_TOPK_MAX, s // 4)
    key_pos = jnp.arange(s)
    gather = jax.vmap(lambda tb, ib: tb[ib])

    def block(i):
        start = i * Q_BLOCK
        q_pos = start + jnp.arange(Q_BLOCK)
        iqb = lax.dynamic_slice_in_dim(iq, start, Q_BLOCK, axis=1)
        iwb = lax.dynamic_slice_in_dim(iw, start, Q_BLOCK, axis=1)
        qb = lax.dynamic_slice_in_dim(q, start, Q_BLOCK, axis=1)
        logits = jnp.einsum('bqhd,bsd->bqhs', iqb, ik, preferred_element_type=F32)
        score = jnp.einsum('bqhs,bqh->bqs', jax.nn.relu(logits), iwb)
        score = jnp.where(key_pos[None, None, :] <= q_pos[None, :, None], score, -jnp.inf)
        _, sel = lax.top_k(score, n_sel)
        valid = sel <= q_pos[None, :, None]
        k_sel = gather(k, sel)
        v_sel = gather(v, sel)
        sc = jnp.einsum('bqhd,bqkhd->bqhk', qb, k_sel, preferred_element_type=F32) * DSA_DH ** -0.5
        sc = jnp.where(valid[:, :, None, :], sc, NEG_INF)
        pr = jax.nn.softmax(sc, axis=-1)
        return jnp.einsum('bqhk,bqkhd->bqhd', pr.astype(v.dtype), v_sel)

    o = lax.map(block, jnp.arange(s // Q_BLOCK))
    return jnp.moveaxis(o, 0, 1).reshape(b, s, DSA_W)

def setup_inputs(seed: int = 0) -> dict:
    key = jax.random.key(seed)
    ks = iter(jax.random.split(key, 48))
    nrm = lambda shape, scale: scale * jax.random.normal(next(ks), shape, F32)
    gain = lambda shape: 1.0 + 0.02 * jax.random.normal(next(ks), shape, F32)
    unif = lambda shape, lo, hi: jax.random.uniform(next(ks), shape, F32, lo, hi)
    L = DEPTH
    x = jax.random.normal(next(ks), (BATCH, SEQ, D_MODEL), F32)
    positions = (jax.random.randint(next(ks), (BATCH, 1), 0, 1024, dtype=jnp.int32)
                 + jnp.arange(SEQ, dtype=jnp.int32)[None, :])
    dt = jnp.exp(unif((L, GDN_HEADS), math.log(1e-3), math.log(1e-1)))
    return {
        "x": x,
        "positions": positions,
        "mix_norm_g": gain((L, D_MODEL)),
        "w_in": nrm((L, D_MODEL, N_IN), D_MODEL ** -0.5),
        "gdn_conv_w": nrm((L, GDN_CONV, GDN_QKV), GDN_CONV ** -0.5),
        "gdn_a_log": jnp.log(unif((L, GDN_HEADS), 1.0, 16.0)),
        "gdn_dt_bias": dt + jnp.log(-jnp.expm1(-dt)),
        "gdn_norm_g": gain((L, GDN_DV)),
        "mla_q_norm_g": gain((L, MLA_Q_LORA)),
        "mla_kv_norm_g": gain((L, MLA_KV_LORA)),
        "mla_w_uq": nrm((L, MLA_Q_LORA, MLA_HEADS * (MLA_NOPE + MLA_ROPE)), MLA_Q_LORA ** -0.5),
        "mla_w_ukv": nrm((L, MLA_KV_LORA, MLA_HEADS * (MLA_NOPE + MLA_DV)), MLA_KV_LORA ** -0.5),
        "rwkv_mu": unif((L, RWKV_IN), 0.0, 1.0),
        "rwkv_w0": unif((L, RWKV_W), -6.0, -1.0),
        "rwkv_w_w2": nrm((L, RWKV_DECAY_LORA, RWKV_W), 0.5 * RWKV_DECAY_LORA ** -0.5),
        "rwkv_a0": nrm((L, RWKV_W), 0.1),
        "rwkv_w_a2": nrm((L, RWKV_AAA_LORA, RWKV_W), 0.5 * RWKV_AAA_LORA ** -0.5),
        "rwkv_w_g2": nrm((L, RWKV_GATE_LORA, RWKV_W), RWKV_GATE_LORA ** -0.5),
        "rwkv_k_k": 0.85 + nrm((L, RWKV_W), 0.02),
        "rwkv_k_a": 1.0 + nrm((L, RWKV_W), 0.02),
        "rwkv_r_k": nrm((L, RWKV_HEADS, RWKV_DH), 0.1),
        "rwkv_ln_w": gain((L, RWKV_W)),
        "rwkv_ln_b": nrm((L, RWKV_W), 0.02),
        "w_out_gdn": nrm((L, GDN_W, D_MODEL), GDN_W ** -0.5),
        "w_out_mla": nrm((L, MLA_W, D_MODEL), MLA_W ** -0.5),
        "w_out_rwkv": nrm((L, RWKV_W, D_MODEL), RWKV_W ** -0.5),
        "w_out_dsa": nrm((L, DSA_W, D_MODEL), DSA_W ** -0.5),
        "w_o": nrm((L, D_MODEL, D_MODEL), D_MODEL ** -0.5),
        "mlp_norm_g": gain((L, D_MODEL)),
        "w_up": nrm((L, D_MODEL, D_FF), D_MODEL ** -0.5),
        "w_down": nrm((L, D_FF, D_MODEL), D_FF ** -0.5),
        "final_norm_g": gain((D_MODEL,)),
    }

def reference(x, positions, mix_norm_g, w_in, gdn_conv_w, gdn_a_log, gdn_dt_bias, gdn_norm_g,
              mla_q_norm_g, mla_kv_norm_g, mla_w_uq, mla_w_ukv,
              rwkv_mu, rwkv_w0, rwkv_w_w2, rwkv_a0, rwkv_w_a2, rwkv_w_g2, rwkv_k_k, rwkv_k_a,
              rwkv_r_k, rwkv_ln_w, rwkv_ln_b,
              w_out_gdn, w_out_mla, w_out_rwkv, w_out_dsa, w_o,
              mlp_norm_g, w_up, w_down, final_norm_g):
    rope_mla = rotary_tables(positions, MLA_ROPE)
    rope_idx = rotary_tables(positions, IDX_DH // 4)
    rope_att = rotary_tables(positions, DSA_DH // 4)
    for l in range(DEPTH):
        h = rms_norm(x, mix_norm_g[l])
        p_gdn, p_mla, p_rwkv, p_dsa, p_gate = _split(h @ w_in[l], SLAB_SPLITS)
        y_a = gdn_mixer(p_gdn, gdn_conv_w[l], gdn_a_log[l], gdn_dt_bias[l], gdn_norm_g[l]) @ w_out_gdn[l]
        y_b = mla_mixer(p_mla, rope_mla, mla_q_norm_g[l], mla_kv_norm_g[l], mla_w_uq[l], mla_w_ukv[l]) @ w_out_mla[l]
        y_c = rwkv7_mixer(p_rwkv, rwkv_mu[l], rwkv_w0[l], rwkv_w_w2[l], rwkv_a0[l], rwkv_w_a2[l],
                          rwkv_w_g2[l], rwkv_k_k[l], rwkv_k_a[l], rwkv_r_k[l], rwkv_ln_w[l],
                          rwkv_ln_b[l]) @ w_out_rwkv[l]
        y_d = dsa_mixer(p_dsa, rope_idx, rope_att) @ w_out_dsa[l]
        g_a, g_b, g_c, g_d = _split(jax.nn.sigmoid(p_gate.astype(F32)).astype(x.dtype), GATE_SPLITS)
        merged = g_a * y_a + g_b * y_b + g_c * y_c + g_d * y_d
        x = x + merged @ w_o[l]
        hm = rms_norm(x, mlp_norm_g[l])
        x = x + jnp.square(jax.nn.relu(hm @ w_up[l])) @ w_down[l]
    return rms_norm(x, final_norm_g)


_drawn_inputs = setup_inputs


def setup_inputs(seed=0):
    import zlib

    import numpy as np

    out = dict(_drawn_inputs(seed))
    spreads = {}
    factors = {'gdn_norm_g': 6.436,
     'mla_q_norm_g': 8.0,
     'mla_kv_norm_g': 8.0,
     'rwkv_w_w2': 4.985,
     'rwkv_a0': 3.296,
     'rwkv_k_k': 5.692,
     'rwkv_k_a': 5.347,
     'rwkv_ln_w': 6.966,
     'rwkv_ln_b': 6.436,
     'final_norm_g': 2.909}
    for name, (base, spread) in spreads.items():
        noise = np.random.default_rng([zlib.crc32(name.encode()), seed]).standard_normal(out[name].shape)
        drawn = base * np.exp(spread * noise) if base else spread * noise
        out[name] = jnp.asarray(drawn.astype(out[name].dtype))
    for name, factor in factors.items():
        out[name] = (out[name] * factor).astype(out[name].dtype)
    return out
```

```python
from contextlib import ExitStack

import numpy as np

import concourse.bass as bass
from concourse import mybir

ALU = mybir.AluOpType
ACT = mybir.ActivationFunctionType
F32 = mybir.dt.float32
I32 = mybir.dt.int32
AX_X = mybir.AxisListType.X

P = 128
T = 512
D = 1024
L = 2
KT = D // P
TT = T // P
C = 64
NC = T // C
H = 4
M = TT * H
FF = 4096
EPS = 1e-6
GN_EPS = 64e-5
TOPK = 128
NEG = -1e30
DECAY = float(np.exp(-0.5))
MAGIC = 12582912.0
TWO_PI = (6.28125, 0.0019350051879882812, 3.0199159819e-07)
LEVELS = (1, 2, 4, 8, 16, 32)

GDN0, MLA0, RWK0, DSA0, GATE0 = 0, 1032, 1448, 2472, 3824

UW = 256
SLOT = 10 * UW
RING = 3


def unit_list():
    u = [("rw", i) for i in range(4)] + [("misc", 0)]
    u += [("gd", i) for i in range(4)]
    u += [("merge", 2, i) for i in range(4)]
    u += [("ds", i) for i in range(5)]
    u += [("merge", 0, i) for i in range(4)]
    u += [("cq", 0)]
    u += [("merge", 3, i) for i in range(4)]
    u += [("merge", 1, i) for i in range(4)]
    u += [("wo", i) for i in range(4)]
    u += [("up", i) for i in range(16)]
    u += [("down", j, kb) for j in range(4) for kb in range(4)]
    return u


UNITS = unit_list()
NU = len(UNITS)

CONST = {}


def _constants():
    n = np.arange(P)
    blk = n[:, None] // C == n[None, :] // C
    parts = [
        ("ident", np.eye(P)),
        ("ones", np.ones((P, P))),
        ("blocks", blk),
        ("upto", blk & (n[:, None] <= n[None, :])),
        ("before", blk & (n[:, None] < n[None, :])),
        ("after", blk & (n[:, None] > n[None, :])),
        ("eye_c", (n[:, None] % C) == np.arange(C)[None, :]),
    ]
    i, j = (n % C)[:, None], np.arange(C)[None, :]
    for s in LEVELS:
        parts.append((f"level{s}", (i // (2 * s) == j // (2 * s)) & (i % (2 * s) >= s) & (j % (2 * s) < s)))
    parts.append(("causal", np.where(n[None, :] <= n[:, None], 0.0, NEG)))

    def rotate(dims, start, width):
        r = np.zeros((P, P))
        for b in range(start, P, width):
            for e in range(dims // 2):
                if b + dims <= P:
                    r[b + dims // 2 + e, b + e] = -1.0
                    r[b + e, b + dims // 2 + e] = 1.0
        return r

    rot_m = np.zeros((P, P))
    rot_m[64:96, 64:96] = rotate(32, 0, P)[:32, :32]
    rot_d = rotate(16, 0, C)
    dup = np.zeros((P, P))
    dup[:C, :] = (np.arange(C)[:, None] == (n % C)[None, :])
    parts += [("rot_m", rot_m), ("rot_d", rot_d), ("dup", dup), ("dup_rot", dup @ rot_d)]
    fm = np.zeros(P, np.float32)
    inv_m = (np.float32(500000.0) ** (-np.arange(0, 32, 2, dtype=np.float32) / np.float32(32))).astype(np.float32)
    fm[64:80] = inv_m
    fm[80:96] = inv_m
    fd = np.zeros(P, np.float32)
    inv_d = (np.float32(500000.0) ** (-np.arange(0, 16, 2, dtype=np.float32) / np.float32(16))).astype(np.float32)
    for b in (0, C):
        fd[b:b + 8] = inv_d
        fd[b + 8:b + 16] = inv_d
    parts += [("freq_d", fd[:, None]), ("freq_m", fm[:, None])]
    at, cols = 0, []
    for name, a in parts:
        a = np.asarray(a, np.float32)
        CONST[name] = (at, a.shape[1])
        at += a.shape[1]
        cols.append(a)
    return np.ascontiguousarray(np.concatenate(cols, axis=1))


CONST_ARRAY = _constants()
NCONST = CONST_ARRAY.shape[1]

PAR = {}
_at = 0
for _n, _w in (("mix_g", 8), ("mlp_g", 8), ("fin_g", 8), ("conv", 24), ("mu", 8), ("w0", 2), ("a0", 2), ("k_k", 2),
               ("k_a", 2), ("r_k", 2), ("ln_w", 2), ("ln_b", 2), ("gdn_g", 1), ("q_g", 2), ("kv_g", 1),
               ("a_log", 4), ("dt", 4), ("wa2", 256), ("g2", 256), ("uq", 768), ("ukv", 512)):
    PAR[_n] = (_at, _w)
    _at += _w
NPAR = _at


def build(nc, x_in, pos_in, wstream, par_in, const_in, tabs, out):
    ctx = ExitStack()
    with ctx:
        def sb(name, shape, dt=F32):
            return ctx.enter_context(nc.sbuf_tensor(name, shape, dt))

        def sem(name):
            return ctx.enter_context(nc.semaphore(name))

        xT = sb("xT", [P, KT, T])
        hT = sb("hT", [P, KT, T])
        mg = sb("mg", [P, KT, T])
        ring = sb("ring", [P, RING, SLOT])
        consts = sb("consts", [P, NCONST])
        par = sb("par", [P, NPAR])
        yo = sb("yo", [P, 2, 2, T])
        misc = sb("misc", [P, 3, T])
        sg = sb("sg", [P, 2, T])
        s_z = sb("s_z", [P, 2, 2, C])
        un_z = sb("un_z", [P, 2, 4 * C])
        pc = sb("pc", [P, 2, NC])
        ab = sb("ab", [P, TT, 16])
        gsm = sb("gsm", [P, 6, M])
        m8 = sb("m8", [P, 8])
        sml = sb("sml", [P, 16])
        AQ = 45
        arena = sb("arena", [P, AQ * T])

        def ar(q, shape, at=0):
            n = int(np.prod(shape))
            v = arena[:, q * T + at:q * T + at + n]
            if len(shape) == 1:
                return v
            names = " ".join("abcd"[:len(shape)])
            return v.rearrange(f"p ({names}) -> p {names}", **{k: s for k, s in zip("abcd", shape)})

        def cst(name):
            a, w = CONST[name]
            return consts[:, a:a + w]

        def pr(name, i=None):
            a, w = PAR[name]
            return par[:, a:a + w] if i is None else par[:, a + i:a + i + 1]

        bank_a = [ctx.enter_context(nc.psum_tensor(f"bank_a{i}", [P, T], F32)) for i in range(4)]
        bank_v = [ctx.enter_context(nc.psum_tensor(f"bank_v{i}", [P, T], F32)) for i in range(4)]

        S, per = {}, {}

        def ev(name, n):
            S[name] = sem(name)
            per[name] = n

        a_full = sem("a_full")
        v_full = sem("v_full")
        w_here = [sem(f"w_here{i}") for i in range(RING)]
        w_used = sem("w_used")
        const_here = sem("const_here")
        par_here = sem("par_here")
        x_here = sem("x_here")
        pos_here = sem("pos_here")
        tab_out = sem("tab_out")
        tab_d_here = sem("tab_d_here")
        tab_m_here = sem("tab_m_here")
        out_done = sem("out_done")
        dve_step = sem("dve_step")
        act_step = sem("act_step")
        for name, n in (
            ("n_sq", 2), ("n_var", 2), ("n_rec", 2), ("n_rs", 2), ("n_h", 16),
            ("x_t", 0), ("o_tok", 0), ("tab", 0), ("tab_sin", 0), ("tab_arg", 0), ("init", 0),
            ("r_in", 8), ("r_zero", 1), ("r_mix", 8), ("r_act", 2), ("r_lora", 6), ("r_cum", 1), ("r_dec", 3),
            ("r_ex", 1), ("r_sq", 1), ("r_l2", 2), ("r_l2r", 1), ("r_l2s", 1), ("r_bsq", 2), ("r_bon", 2), ("r_feat", 4),
            ("r_tok", 8), ("r_mat", 16), ("r_y", 12), ("r_ybd", 12), ("r_t", 10), ("r_x", 12), ("r_xbd", 12),
            ("r_eye", 1), ("r_xi", 1), ("r_wt", 2), ("r_y1", 2), ("r_u", 2), ("r_ws", NC), ("r_s", NC), ("r_o", NC),
            ("r_mean", 2), ("r_sq2", 1), ("r_gv", 2), ("r_gr", 1), ("r_gs", 1), ("r_out", 1),
            ("g_pad", 1), ("g_in", 6), ("g_z", 2), ("g_conv", 6), ("g_sig", 1), ("g_silu", 1), ("g_sq", 1), ("g_l2", 4),
            ("g_l2r", 1), ("g_l2s", 1), ("g_qk", 1), ("g_t1", 1), ("g_t2", 1), ("g_g", 2), ("g_feat", 6), ("g_gc", 1),
            ("g_row", 4), ("g_d", 4), ("g_dm", 4), ("g_prep", 2),
            ("g_tok", 6), ("g_mat", 8), ("g_y", 12), ("g_ybd", 12), ("g_t", 10), ("g_x", 12), ("g_xbd", 12),
            ("g_eye", 1), ("g_xi", 1), ("g_wt", 2), ("g_u", 2), ("g_ws", NC), ("g_s", NC), ("g_o", NC),
            ("g_sq2", 1), ("g_gv", 2), ("g_gr", 1), ("g_gs", 1), ("g_out", 1),
            ("misc_in", 3), ("ab_in", 1),
            ("d_in", 8), ("d_v", 2), ("d_ik", 2), ("d_rot", 8), ("d_sc", 24), ("d_acc", 24), ("d_bias", 4),
            ("d_ss", 16), ("d_p", 16), ("d_pn", 16), ("d_pt", 16), ("d_o", 16), ("d_kz", 2),
            ("m_in", 2), ("m_sq", 1), ("m_nv", 2), ("m_rec", 1), ("m_rs", 1), ("m_c", 1), ("m_q", 4), ("m_k", 4), ("m_v", 2),
            ("m_rot", 4), ("m_kr", 4), ("m_krb", 1),
            ("m_bias", 1),
            ("m_ss", 16), ("m_p", 16), ("m_pn", 16), ("m_pt", 16), ("m_o", 16),
            ("mg_sig", 32), ("mg_done", 32), ("wo_done", 8), ("up_relu", 32), ("up_done", 32), ("g_zs", 1), ("r_s0", 1), ("g_s0", 1), ("down_done", 8),
        ):
            ev(name, n)

        def at(l, name, k):
            return l * per[name] + k

        class Banks:

            def __init__(self):
                self.used = {"a": 0, "v": 0}
                self.reader = {"a": [(const_here, 16)] * 4, "v": [(const_here, 16)] * 4}
                self.counts = {}

            def next(self, pool, done):
                i = self.used[pool] % 4
                self.used[pool] += 1
                sem_, value = self.reader[pool][i]
                self.counts[done] = self.counts.get(done, 0) + 1
                self.reader[pool][i] = (S[done], self.counts[done])
                return (bank_a if pool == "a" else bank_v)[i], sem_, value

        class Filled:

            def __init__(self, banks):
                self.n, self.banks = 0, banks

            def next(self):
                self.n += 1
                return self.n

            def bank(self):
                return self.banks[(self.n - 1) % 4]

        block = ctx.enter_context(nc.Block())

        R = dict(
            rw=ar(0, (8, T + 1)), rm=ar(9, (8, T)), sw=ar(0, (2, T)), a=ar(2, (2, T)), g=ar(4, (2, T)), cs=ar(6, (2, T)),
            p=ar(17, (2, T)), pi=ar(19, (2, T)), pe=ar(21, (2, T)), kk=ar(23, (2, T)), tmp=ar(25, (2, T)),
            rt=ar(27, (2, T)), et=ar(29, (2, T)), bz=ar(31, (2, 2, T)), kz=ar(35, (2, 2, T)),
            bh=ar(39, (2, T)), kh=ar(41, (2, T)), bon=ar(43, (2, T)),
            e_tok=ar(17, (TT, 256)), v_tok=ar(19, (TT, 256)), b_tok=ar(21, (TT, 256)), k_tokz=ar(23, (TT, 2, 256)),
            u=ar(9, (M, P)), ark=ar(0, (2 * M, C)), akk=ar(39, (M, P)),
            x_bd=ar(31, (M, P)), y_bd=ar(35, (M, P)), t_c=ar(29, (M, C)), x_c=ar(6, (M, C)), y_c=ar(15, (M, C)),
            wt=ar(29, (2, T)), y1=ar(15, (TT, 256)), up=ar(6, (TT, 256)), o=ar(9, (2, T)), sq=ar(11, (2, T)),
        )
        R["arb"] = mg[:, 0:4, :].rearrange("p a (b c) -> p (a b) c", c=P)
        R["ark"] = ar(0, (M, P))
        G = dict(
            ci=ar(0, (6, T + 3)), co=ar(7, (6, T)), z=ar(13, (2, T)), sig=ar(15, (6, T)), sq=ar(0, (4, T)), rs=ar(15, (4, T)),
            egc=ar(15, (2, T)), ers=ar(17, (2, T)), beta=ar(19, (2, T)), kb=ar(0, (2, T)), rt=ar(2, (2, T)), et=ar(4, (2, T)),
            bh=ar(21, (2, T)), vb=ar(23, (2, T)), kz=ar(25, (2, 2, T)), d=ar(29, (M, P)), u=ar(33, (M, P)), arb=ar(37, (M, P)),
            e_tok=ar(41, (TT, 256)), v_tok=ar(43, (TT, 256)), b_tok=ar(17, (TT, 256)),
            x_bd=ar(25, (M, P)), y_bd=ar(29, (M, P)), t_c=ar(0, (M, C)), x_c=ar(4, (M, C)), y_c=ar(19, (M, C)),
            wt=ar(0, (2, T)), up=ar(4, (TT, 256)), o=ar(7, (2, T)), sq2=ar(9, (2, T)),
            g_wide=ar(41, (M * C,)), b_wide=ar(43, (M * C,)),
        )
        Dv = dict(
            iq=ar(0, (4, T)), q=ar(4, (2, T)), k=ar(6, (2, T)), v=ar(8, (TT, 256)), tab=ar(10, (2, T)),
            ikz=ar(12, (2, T)), kz=ar(14, (2, 2, T)), tmp=ar(18, (T,)), rl=ar(19, (2, T)), sc=ar(21, (T,)), wk=ar(22, (T,)),
            gt=ar(23, (T,)), eq=ar(24, (T,)), cum=ar(25, (T,)), bias=ar(26, (TT, T)),
            ss=ar(30, (2, T)), pt=ar(32, (2, TT, P)),
        )
        Mv = dict(
            cq=ar(0, (2, T)), sq=ar(2, (3, T)), rs=ar(5, (2, T)), q=ar(7, (4, T)), k=ar(11, (4, T)), v=ar(15, (TT, 256)),
            tab=ar(17, (2, T)), tmp=ar(19, (T,)), bias=ar(20, (T,)), kr=ar(21, (T,)),
            ss=ar(30, (2, T)), pt=ar(32, (2, TT, P)),
        )
        xin = ar(0, (TT, D))
        xout = ar(0, (TT, D))
        up_act = ar(0, (FF // P, T))
        POS = dict(i=ar(20, (T,)).bitcast(I32), f=ar(21, (T,)), ang=ar(22, (T,)), k=ar(23, (T,)), sin=ar(24, (2, T)), cos=ar(26, (2, T)),
                   red=ar(28, (2, T)))
        rotors = ("d", "m")

        @block.sync
        def _(sp):
            sp.dma_start(xin, x_in.rearrange("(t p) d -> p t d", p=P)).then_inc(x_here, 16)
            sp.dma_start(consts[:], const_in).then_inc(const_here, 16)
            sp.dma_start(POS["i"], pos_in.partition_broadcast(P)).then_inc(pos_here, 16)
            for g in range(L * NU):
                u = g % NU
                if g >= RING:
                    sp.wait_ge(w_used, g - RING + 2)
                kts = 10 if UNITS[u][0] == "merge" else 8
                sp.dma_start(ring[:, g % RING, 0:kts * UW], wstream[g, :, 0:kts * UW]).then_inc(w_here[g % RING], 16)
            sp.wait_ge(S["o_tok"], 8)
            sp.dma_start(out.rearrange("(t p) d -> p t d", p=P), xout).then_inc(out_done, 16)
            sp.wait_ge(out_done, 16)

        @block.gpsimd
        def _(pool):
            for i in range(2):
                pool.wait_ge(S["tab"], i + 1)
                pool.dma_start(tabs[i, 0], POS["cos"][:, i, :]).then_inc(tab_out, 16)
                pool.dma_start(tabs[i, 1], POS["sin"][:, i, :]).then_inc(tab_out, 16)
            pool.wait_ge(tab_out, 64)
            for l in range(L):
                if l > 0:
                    pool.wait_ge(S["n_h"], at(l - 1, "n_h", 16))
                pool.dma_start(par[:], par_in[l]).then_inc(par_here, 16)
                pool.wait_ge(S["g_out"], at(l, "g_out", 1))
                pool.dma_start(Dv["tab"], tabs[0].rearrange("k p t -> p k t")).then_inc(tab_d_here, 16)
                pool.wait_ge(S["d_o"], at(l, "d_o", 16))
                pool.dma_start(Mv["tab"], tabs[1].rearrange("k p t -> p k t")).then_inc(tab_m_here, 16)

        @block.tensor
        def _(pe):
            mm = nc.tensor.matmul
            banks = Banks()
            unit = [0]

            def begin_unit(want, l):
                g = unit[0]
                assert UNITS[g % NU] == want and g // NU == l, (UNITS[g % NU], want)
                unit[0] += 1
                pe.wait_ge(w_here[g % RING], 16 * (g // RING + 1))
                return ring[:, g % RING, :].rearrange("p (k n) -> p k n", n=UW), [True]

            def used(ins, first):
                if first[0]:
                    ins.then_inc(w_used, 1)
                    first[0] = False

            def feat_group(w, first, col, n, rhs, pool, done, part=0):
                b, reader, emptied = banks.next(pool, done)
                pe.wait_ge(reader, emptied)
                for k in range(KT):
                    ins = mm(b[part:part + n, :], w[:, k, col:col + n], rhs[:, k, :], start=k == 0, stop=k == KT - 1)
                    used(ins, first)
                ins.then_inc(a_full if pool == "a" else v_full, 1)

            def norm_sum(n):
                b, reader, emptied = banks.next("v", "n_var")
                pe.wait_ge(reader, emptied)
                pe.wait_ge(S["n_sq"], n + 1)
                for k in range(KT):
                    ins = mm(b[:], cst("ones"), hT[:, k, :], start=k == 0, stop=k == KT - 1)
                ins.then_inc(v_full, 1)

            def merge(l, br, slot, i):
                w, first = begin_unit(("merge", br, i), l)
                for j in range(2):
                    b, reader, emptied = banks.next("v", "mg_done")
                    pe.wait_ge(reader, emptied)
                    for k in range(2):
                        ins = mm(b[:], w[:, 8 + k, j * P:(j + 1) * P], yo[:, slot, k, :], start=k == 0, stop=k == 1)
                        used(ins, first)
                    ins.then_inc(v_full, 1)
                    feat_group(w, first, j * P, P, hT, "a", "mg_sig")

            def transposes(srcs, x):
                for s in srcs:
                    for half in range(2):
                        b, reader, emptied = banks.next("a", x + "_tok")
                        pe.wait_ge(reader, emptied)
                        for t2 in range(2):
                            for f in range(2):
                                c = t2 * 256 + f * P
                                t = 2 * half + t2
                                ins = nc.tensor.transpose(b[:, c:c + P], s[:, f, t * P:(t + 1) * P], cst("ident"))
                        ins.then_inc(a_full, 1)

            def pair_matrices(lz, rhs, x):
                for t in range(TT):
                    b, reader, emptied = banks.next("v", x + "_mat")
                    pe.wait_ge(reader, emptied)
                    for h in range(H):
                        ins = mm(b[:, h * P:(h + 1) * P], lz[:, h // 2, h % 2, t * P:(t + 1) * P],
                                 rhs[:, h // 2, t * P:(t + 1) * P], start=True, stop=True)
                    ins.then_inc(v_full, 1)

            def small_products(pool, done, half, lhs, rhs):
                b, reader, emptied = banks.next(pool, done)
                pe.wait_ge(reader, emptied)
                for i in range(8):
                    m = 8 * half + i
                    ins = mm(b[:, i * C:(i + 1) * C], lhs[:, m, :], rhs(m), start=True, stop=True)
                ins.then_inc(v_full if pool == "v" else a_full, 1)

            def invert(l, x, V, fill):
                pe.wait_ge(S[x + "_eye"], at(l, x + "_eye", 1))
                for n, s in enumerate(LEVELS):
                    for half in range(2):
                        if n:
                            pe.wait_ge(S[x + "_t"], at(l, x + "_t", 2 * (n - 1) + half + 1))
                        small_products("v", x + "_y", half, V["u"], lambda m: V["t_c"][:, m, :])
                    for half in range(2):
                        if n < len(LEVELS) - 1:
                            pe.wait_ge(S[x + "_y"], at(l, x + "_y", 2 * n + half + 1))
                            if n:
                                pe.wait_ge(S[x + "_xbd"], at(l, x + "_xbd", 2 * (n - 1) + half + 1))
                            elif half == 0:
                                pe.wait_ge(S[x + "_xi"], at(l, x + "_xi", 1))
                            small_products("v", x + "_t", half, V["x_bd"], lambda m: V["y_c"][:, m, :])
                    for half in range(2):
                        pe.wait_ge(S[x + "_ybd"], at(l, x + "_ybd", 2 * n + half + 1))
                        if n:
                            pe.wait_ge(S[x + "_x"], at(l, x + "_x", 2 * (n - 1) + half + 1))
                        small_products("v", x + "_x", half, V["y_bd"], lambda m: V["x_c"][:, m, :])
                    if n % 2 == 1:
                        fill()
                pe.wait_ge(S[x + "_xbd"], at(l, x + "_xbd", 2 * len(LEVELS)))

            def through(l, x, V, rhs):
                for f in range(2):
                    b, reader, emptied = banks.next("a", x + "_wt")
                    pe.wait_ge(reader, emptied)
                    for t in range(TT):
                        for hp in range(2):
                            h = 2 * f + hp
                            ins = mm(b[hp * C:(hp + 1) * C, t * P:(t + 1) * P], V["e_tok"][:, t, h * C:(h + 1) * C],
                                     V["x_bd"][:, t * H + h, :], start=True, stop=True)
                    ins.then_inc(a_full, 1)
                for half in range(2):
                    small_products("a", x + "_u", half, V["x_bd"],
                                   lambda m: rhs[:, m // H, (m % H) * C:(m % H + 1) * C])

            def scan(l, x, V, fill):
                pe.wait_ge(S[x + "_s0"], at(l, x + "_s0", 1))
                pe.wait_ge(S[x + "_wt"], at(l, x + "_wt", 2))
                for c in range(NC):
                    t, par_ = divmod(c, 2)
                    rows = slice(par_ * C, (par_ + 1) * C)
                    if c:
                        pe.wait_ge(S[x + "_s"], at(l, x + "_s", c))
                    b, reader, emptied = banks.next("v", x + "_ws")
                    pe.wait_ge(reader, emptied)
                    for f in range(2):
                        ins = mm(b[rows, f * P:(f + 1) * P], V["wt"][:, f, c * C:(c + 1) * C],
                                 s_z[:, f, :, :], start=True, stop=True)
                    ins.then_inc(v_full, 1)
                    bo, reader, emptied = banks.next("a", x + "_o")
                    pe.wait_ge(reader, emptied)
                    bs, reader, emptied = banks.next("v", x + "_s")
                    pe.wait_ge(reader, emptied)
                    pe.wait_ge(S[x + "_ws"], at(l, x + "_ws", c + 1))
                    for h in range(H):
                        f, hp = divmod(h, 2)
                        dst = bo[hp * C:(hp + 1) * C, f * C:(f + 1) * C]
                        hc = slice(h * C, (h + 1) * C)
                        mm(dst, s_z[:, f, hp, :], V["rt"][:, f, c * C:(c + 1) * C], start=True, stop=False)
                        if "ark" in V:
                            mm(dst, V["v_tok"][:, t, hc], V["ark"][:, t * H + h, rows], start=False, stop=False)
                        ins = mm(dst, un_z[:, par_, hc], V["arb"][:, t * H + h, rows], start=False, stop=True)
                    ins.then_inc(a_full, 1)
                    for h in range(H):
                        f, hp = divmod(h, 2)
                        dst = bs[hp * C:(hp + 1) * C, f * C:(f + 1) * C]
                        hc = slice(h * C, (h + 1) * C)
                        if "ark" in V:
                            mm(dst, V["k_tokz"][:, t, par_, hc], V["v_tok"][:, t, hc], start=True, stop=False)
                        ins = mm(dst, V["b_tok"][:, t, hc], un_z[:, par_, hc], start="ark" not in V, stop=True)
                    ins.then_inc(v_full, 1)
                    if c in (1, 4):
                        fill()

            def block_sums(l, need, k, src, tiles, done):
                pe.wait_ge(S[need], at(l, need, k))
                for i in range(tiles):
                    b, reader, emptied = banks.next("v", done)
                    pe.wait_ge(reader, emptied)
                    mm(b[:], cst("blocks"), src[:, i, :], start=True, stop=True).then_inc(v_full, 1)

            def attention(l, x, q_of, k_of, v, scores_need):
                steps = [(qt, h) for qt in range(TT) for h in range(H)]
                for i in range(len(steps) + 2):
                    if i < len(steps):
                        qt, h = steps[i]
                        b, reader, emptied = banks.next("v", x + "_ss")
                        pe.wait_ge(reader, emptied)
                        scores_need(qt)
                        mm(b[:, 0:(qt + 1) * P], q_of(h, qt), k_of(h, (qt + 1) * P), start=True, stop=True).then_inc(v_full, 1)
                    if 1 <= i <= len(steps):
                        qt, h = steps[i - 1]
                        b, reader, emptied = banks.next("a", x + "_pt")
                        pe.wait_ge(reader, emptied)
                        pe.wait_ge(S[x + "_pn"], at(l, x + "_pn", i))
                        for k in range(qt + 1):
                            ins = nc.tensor.transpose(b[:, k * P:(k + 1) * P], V_ss(x)[:, (i - 1) % 2, k * P:(k + 1) * P], cst("ident"))
                        ins.then_inc(a_full, 1)
                    if i >= 2:
                        qt, h = steps[i - 2]
                        b, reader, emptied = banks.next("v", x + "_o")
                        pe.wait_ge(reader, emptied)
                        pe.wait_ge(S[x + "_pt"], at(l, x + "_pt", i - 1))
                        rows = slice((h % 2) * C, (h % 2 + 1) * C)
                        for k in range(qt + 1):
                            ins = mm(b[rows, 0:P], v[:, k, h * C:(h + 1) * C], V_pt(x)[:, (i - 2) % 2, k, :],
                                     start=k == 0, stop=k == qt)
                        ins.then_inc(v_full, 1)

            def V_ss(x):
                return (Dv if x == "d" else Mv)["ss"]

            def V_pt(x):
                return (Dv if x == "d" else Mv)["pt"]

            pe.wait_ge(x_here, 16)
            pe.wait_ge(const_here, 16)
            for k in range(KT):
                b, reader, emptied = banks.next("v", "x_t")
                pe.wait_ge(reader, emptied)
                for t in range(TT):
                    ins = nc.tensor.transpose(b[:, t * P:(t + 1) * P], xin[:, t, k * P:(k + 1) * P], cst("ident"))
                ins.then_inc(v_full, 1)

            for l in range(L):
                norm_sum(2 * l)
                for i in range(4):
                    w, first = begin_unit(("rw", i), l)
                    for j in range(2):
                        if i == 0 and j == 0:
                            pe.wait_ge(S["n_h"], at(l, "n_h", 8))
                        feat_group(w, first, j * P, P, hT, "a", "r_in")
                w, first = begin_unit(("misc", 0), l)
                feat_group(w, first, 0, P, hT, "a", "misc_in")
                feat_group(w, first, P, 32, hT, "a", "misc_in", part=64)
                feat_group(w, first, P + 32, 64, hT, "a", "misc_in")
                b, reader, emptied = banks.next("a", "ab_in")
                pe.wait_ge(reader, emptied)
                for t in range(TT):
                    for k in range(KT):
                        ins = mm(b[:, t * 16:(t + 1) * 16], hT[:, k, t * P:(t + 1) * P], w[:, k, 224:240],
                                 start=k == 0, stop=k == KT - 1)
                ins.then_inc(a_full, 1)
                pe.wait_ge(S["r_act"], at(l, "r_act", 2))
                for f in range(2):
                    b, reader, emptied = banks.next("a", "r_lora")
                    pe.wait_ge(reader, emptied)
                    mm(b[:], pr("wa2")[0:64, f * P:(f + 1) * P], R["rm"][0:64, 6, :], start=True, stop=True).then_inc(a_full, 1)
                for f in range(2):
                    b, reader, emptied = banks.next("a", "r_lora")
                    pe.wait_ge(reader, emptied)
                    mm(b[:], pr("wa2")[64:128, f * P:(f + 1) * P], R["rm"][64:128, 6, :], start=True, stop=True).then_inc(a_full, 1)
                for f in range(2):
                    b, reader, emptied = banks.next("a", "r_lora")
                    pe.wait_ge(reader, emptied)
                    mm(b[:], pr("g2")[:, f * P:(f + 1) * P], R["rm"][:, 7, :], start=True, stop=True).then_inc(a_full, 1)
                block_sums(l, "r_sq", 1, R["tmp"], 2, "r_l2")
                block_sums(l, "r_bsq", 2, R["tmp"], 2, "r_bon")
                pe.wait_ge(S["r_feat"], at(l, "r_feat", 4))
                transposes((R["et"], R["rm"][:, 4:6, :], R["bh"], R["kh"]), "r")
                pair_matrices(R["bz"], R["et"], "r")
                pair_matrices(R["kz"], R["et"], "r")
                pair_matrices(R["kz"], R["rt"], "r")
                pair_matrices(R["bz"], R["rt"], "r")
                invert(l, "r", R, lambda: None)
                pe.wait_ge(S["r_tok"], at(l, "r_tok", 8))
                for half in range(2):
                    small_products("v", "r_y1", half, R["akk"], lambda m: R["v_tok"][:, m // H, (m % H) * C:(m % H + 1) * C])
                pe.wait_ge(S["r_y1"], at(l, "r_y1", 2))
                through(l, "r", R, R["y1"])
                scan(l, "r", R, lambda: None)
                block_sums(l, "r_o", NC, R["o"], 2, "r_mean")
                block_sums(l, "r_sq2", 1, R["sq"], 2, "r_gv")

                pe.wait_ge(S["r_out"], at(l, "r_out", 1))
                for i in range(4):
                    w, first = begin_unit(("gd", i), l)
                    for j in range(2):
                        feat_group(w, first, j * P, P, hT, "a", "g_in" if i < 3 else "g_z")
                todo = list(range(4))

                def fill_r():
                    if todo:
                        merge(l, 2, 0, todo.pop(0))

                block_sums(l, "g_sq", 1, G["sq"], 4, "g_l2")
                fill_r()
                pe.wait_ge(S["g_g"], at(l, "g_g", 2))
                for src, rhs in (("g", "upto"), ("g", "after"), ("b", "ident")):
                    for f in range(2):
                        b, reader, emptied = banks.next("a", "g_feat")
                        pe.wait_ge(reader, emptied)
                        for t in range(TT):
                            m = t * H + 2 * f
                            wide = G["g_wide" if src == "g" else "b_wide"][:, m * C:(m + 2) * C]
                            ins = mm(b[:, t * P:(t + 1) * P], wide, cst(rhs), start=True, stop=True)
                        ins.then_inc(a_full, 1)
                b, reader, emptied = banks.next("v", "g_gc")
                pe.wait_ge(reader, emptied)
                mm(b[:, 0:M], cst("upto"), gsm[:, 4, :], start=True, stop=True).then_inc(v_full, 1)
                for t in range(TT):
                    b, reader, emptied = banks.next("v", "g_row")
                    pe.wait_ge(reader, emptied)
                    for h in range(H):
                        ins = mm(b[:, h * P:(h + 1) * P], gsm[:, 4, t * H + h:t * H + h + 1].to_broadcast([P, P]), cst("upto"),
                                 start=True, stop=True)
                    ins.then_inc(v_full, 1)
                pe.wait_ge(S["g_prep"], at(l, "g_prep", 2))
                transposes((G["et"], G["vb"], G["bh"]), "g")
                pair_matrices(G["kz"], G["kb"], "g")
                pair_matrices(G["kz"], G["co"][:, 0:2, :], "g")
                invert(l, "g", G, fill_r)
                pe.wait_ge(S["g_tok"], at(l, "g_tok", 6))
                through(l, "g", G, G["v_tok"])
                scan(l, "g", G, fill_r)
                block_sums(l, "g_sq2", 1, G["sq2"], 2, "g_gv")
                assert not todo

                pe.wait_ge(S["g_out"], at(l, "g_out", 1))
                for i in range(4):
                    w, first = begin_unit(("ds", i), l)
                    for j in range(2):
                        feat_group(w, first, j * P, P, hT, "a", "d_in")
                w, first = begin_unit(("ds", 4), l)
                for half in range(2):
                    b, reader, emptied = banks.next("a", "d_v")
                    pe.wait_ge(reader, emptied)
                    for t2 in range(2):
                        t = 2 * half + t2
                        for k in range(KT):
                            ins = mm(b[:, t2 * UW:(t2 + 1) * UW], hT[:, k, t * P:(t + 1) * P], w[:, k, :], start=k == 0, stop=k == KT - 1)
                            used(ins, first)
                    ins.then_inc(a_full, 1)
                for nm in ("dup", "dup_rot"):
                    b, reader, emptied = banks.next("v", "d_ik")
                    pe.wait_ge(reader, emptied)
                    mm(b[:], cst(nm), misc[:, 2, :], start=True, stop=True).then_inc(v_full, 1)
                for i in range(8):
                    src = Dv["iq"][:, i, :] if i < 4 else Dv["q"][:, i - 4, :] if i < 6 else Dv["k"][:, i - 6, :]
                    b, reader, emptied = banks.next("v", "d_rot")
                    pe.wait_ge(reader, emptied)
                    pe.wait_ge(S["d_in"], at(l, "d_in", i + 1))
                    mm(b[:], cst("rot_d"), src, start=True, stop=True).then_inc(v_full, 1)
                pe.wait_ge(S["d_rot"], at(l, "d_rot", 8))
                pe.wait_ge(S["d_kz"], at(l, "d_kz", 2))
                for qt in range(1, TT):
                    for h in range(8):
                        b, reader, emptied = banks.next("a", "d_sc")
                        pe.wait_ge(reader, emptied)
                        mm(b[:, 0:(qt + 1) * P], Dv["iq"][:, h // 2, qt * P:(qt + 1) * P], Dv["ikz"][:, h % 2, 0:(qt + 1) * P],
                           start=True, stop=True).then_inc(a_full, 1)
                    merge(l, 0, 1, qt - 1)
                merge(l, 0, 1, 3)
                attention(l, "d", lambda h, qt: Dv["q"][:, h // 2, qt * P:(qt + 1) * P],
                          lambda h, n: Dv["kz"][:, h // 2, h % 2, 0:n], Dv["v"], lambda qt: None)

                pe.wait_ge(S["d_o"], at(l, "d_o", 16))
                w, first = begin_unit(("cq", 0), l)
                for j in range(2):
                    feat_group(w, first, j * P, P, hT, "a", "m_in")
                merge(l, 3, 0, 0)
                pe.wait_ge(S["m_sq"], at(l, "m_sq", 1))
                b, reader, emptied = banks.next("v", "m_nv")
                pe.wait_ge(reader, emptied)
                for k in range(2):
                    ins = mm(b[:], cst("ones"), Mv["sq"][:, k, :], start=k == 0, stop=k == 1)
                ins.then_inc(v_full, 1)
                b, reader, emptied = banks.next("v", "m_nv")
                pe.wait_ge(reader, emptied)
                mm(b[:], cst("ones"), Mv["sq"][:, 2, :], start=True, stop=True).then_inc(v_full, 1)
                merge(l, 3, 0, 1)
                pe.wait_ge(S["m_c"], at(l, "m_c", 1))
                for h in range(H):
                    b, reader, emptied = banks.next("a", "m_q")
                    pe.wait_ge(reader, emptied)
                    for k in range(2):
                        ins = mm(b[0:96, :], pr("uq")[:, k * 384 + h * 96:k * 384 + (h + 1) * 96], Mv["cq"][:, k, :], start=k == 0, stop=k == 1)
                    ins.then_inc(a_full, 1)
                for h in range(H):
                    b, reader, emptied = banks.next("a", "m_k")
                    pe.wait_ge(reader, emptied)
                    mm(b[0:64, :], pr("ukv")[:, h * P:h * P + C], misc[:, 0, :], start=True, stop=True).then_inc(a_full, 1)
                for half in range(2):
                    b, reader, emptied = banks.next("a", "m_v")
                    pe.wait_ge(reader, emptied)
                    for t2 in range(2):
                        t = 2 * half + t2
                        ins = mm(b[:, t2 * UW:(t2 + 1) * UW], misc[:, 0, t * P:(t + 1) * P],
                                 pr("ukv").rearrange("p (h n) -> p h n", n=P)[:, :, C:P], start=True, stop=True)
                    ins.then_inc(a_full, 1)
                b, reader, emptied = banks.next("v", "m_krb")
                pe.wait_ge(reader, emptied)
                mm(b[0:96, :], cst("rot_m")[64:96, 0:96], misc[64:96, 1, :], start=True, stop=True).then_inc(v_full, 1)
                for h in range(H):
                    b, reader, emptied = banks.next("v", "m_rot")
                    pe.wait_ge(reader, emptied)
                    pe.wait_ge(S["m_q"], at(l, "m_q", h + 1))
                    mm(b[0:96, :], cst("rot_m")[0:96, 0:96], Mv["q"][0:96, h, :], start=True, stop=True).then_inc(v_full, 1)
                merge(l, 3, 0, 2)
                merge(l, 3, 0, 3)
                pe.wait_ge(S["m_rot"], at(l, "m_rot", 4))
                pe.wait_ge(S["m_kr"], at(l, "m_kr", 4))
                pe.wait_ge(S["m_k"], at(l, "m_k", 4))
                pe.wait_ge(S["m_v"], at(l, "m_v", 2))
                attention(l, "m", lambda h, qt: Mv["q"][0:96, h, qt * P:(qt + 1) * P],
                          lambda h, n: Mv["k"][0:96, h, 0:n], Mv["v"], lambda qt: None)
                pe.wait_ge(S["m_o"], at(l, "m_o", 16))
                for i in range(4):
                    merge(l, 1, 1, i)

                pe.wait_ge(S["mg_done"], at(l, "mg_done", 32))
                for i in range(4):
                    w, first = begin_unit(("wo", i), l)
                    for j in range(2):
                        feat_group(w, first, j * P, P, mg, "v", "wo_done")
                norm_sum(2 * l + 1)
                for i in range(16):
                    w, first = begin_unit(("up", i), l)
                    for j in range(2):
                        if i == 0 and j == 0:
                            pe.wait_ge(S["n_h"], at(l, "n_h", 16))
                        feat_group(w, first, j * P, P, hT, "a", "up_relu")
                for i in range(4):
                    b0, reader, emptied = banks.next("v", "down_done")
                    pe.wait_ge(reader, emptied)
                    b1, reader, emptied = banks.next("v", "down_done")
                    pe.wait_ge(reader, emptied)
                    pair = (b0, b1)
                    for kb in range(4):
                        w, first = begin_unit(("down", i, kb), l)
                        for j in range(2):
                            for k in range(KT):
                                if i == 0 and j == 0:
                                    pe.wait_ge(S["up_done"], at(l, "up_done", kb * KT + k + 1))
                                ins = mm(pair[j][:], w[:, k, j * P:(j + 1) * P], up_act[:, kb * KT + k, :],
                                         start=kb == 0 and k == 0, stop=kb == 3 and k == KT - 1)
                                used(ins, first)
                            if kb == 3:
                                ins.then_inc(v_full, 1)
            norm_sum(2 * L)
            for t in range(TT):
                for half in range(2):
                    b, reader, emptied = banks.next("a", "o_tok")
                    pe.wait_ge(reader, emptied)
                    if t == 0 and half == 0:
                        pe.wait_ge(S["n_h"], 16 * L + 8)
                    for k in range(4):
                        ins = nc.tensor.transpose(b[:, k * P:(k + 1) * P], hT[:, 4 * half + k, t * P:(t + 1) * P], cst("ident"))
                    ins.then_inc(a_full, 1)

        @block.scalar
        def _(act):
            act_fn = nc.scalar.activation
            filled = Filled(bank_a)

            def invert(l, x, V, fill):
                act.wait_ge(S[x + "_eye"], at(l, x + "_eye", 1))
                for p in range(2):
                    rows = slice(p * C, (p + 1) * C)
                    last = act_fn(V["x_bd"][rows, :, p * C:(p + 1) * C], V["x_c"][rows, :, :], ACT.Copy)
                last.then_inc(S[x + "_xi"], 1)
                for n in range(len(LEVELS)):
                    for half in range(2):
                        ms = slice(8 * half, 8 * half + 8)
                        act.wait_ge(S[x + "_y"], at(l, x + "_y", 2 * n + half + 1))
                        if n:
                            act.wait_ge(S[x + "_x"], at(l, x + "_x", 2 * (n - 1) + half + 1))
                        for p in range(2):
                            rows = slice(p * C, (p + 1) * C)
                            last = act_fn(V["y_bd"][rows, ms, p * C:(p + 1) * C], V["y_c"][rows, ms, :], ACT.Copy)
                        last.then_inc(S[x + "_ybd"], 1)
                    for half in range(2):
                        ms = slice(8 * half, 8 * half + 8)
                        act.wait_ge(S[x + "_x"], at(l, x + "_x", 2 * n + half + 1))
                        if n < len(LEVELS) - 1:
                            act.wait_ge(S[x + "_t"], at(l, x + "_t", 2 * n + half + 1))
                        for p in range(2):
                            rows = slice(p * C, (p + 1) * C)
                            last = act_fn(V["x_bd"][rows, ms, p * C:(p + 1) * C], V["x_c"][rows, ms, :], ACT.Copy)
                        last.then_inc(S[x + "_xbd"], 1)
                    if n % 2 == 1:
                        fill()

            def tok(l, x, V, names):
                for nm in names:
                    for half in range(2):
                        act.wait_ge(a_full, filled.next())
                        b = filled.bank()
                        if nm == "k_tokz":
                            for p in range(2):
                                rows = slice(p * C, (p + 1) * C)
                                last = act_fn(V[nm][rows, 2 * half:2 * half + 2, p, :],
                                              b[rows, :].rearrange("p (t n) -> p t n", n=256), ACT.Copy)
                        else:
                            last = act_fn(V[nm][:, 2 * half:2 * half + 2, :], b[:].rearrange("p (t n) -> p t n", n=256), ACT.Copy)
                        last.then_inc(S[x + "_tok"], 1)

            def after_inverse(l, x, V):
                for f in range(2):
                    act.wait_ge(a_full, filled.next())
                    b = filled.bank()
                    act_fn(V["wt"][:, f, :], b[:], ACT.Copy).then_inc(S[x + "_wt"], 1)
                for half in range(2):
                    act.wait_ge(a_full, filled.next())
                    b = filled.bank()
                    act_fn(V["up"][:, 2 * half:2 * half + 2, :], b[:].rearrange("p (t n) -> p t n", n=256), ACT.Copy).then_inc(S[x + "_u"], 1)

            def outputs(l, x, V, cs):
                for c in cs:
                    act.wait_ge(a_full, filled.next())
                    b = filled.bank()
                    act_fn(V["o"][:, :, c * C:(c + 1) * C], b[:, 0:P].rearrange("p (f n) -> p f n", n=C), ACT.Copy).then_inc(S[x + "_o"], 1)

            sigs = [0]

            def merge_sig(l):
                for _ in range(2):
                    act.wait_ge(a_full, filled.next())
                    b = filled.bank()
                    n = sigs[0]
                    if n >= 2:
                        act.wait_ge(S["mg_done"], n - 1)
                    act_fn(sg[:, n % 2, :], b[:], ACT.Sigmoid).then_inc(S["mg_sig"], 1)
                    sigs[0] += 1

            def norm_root(n):
                act.wait_ge(S["n_rec"], n + 1)
                act_fn(sg[:, 0, :], sg[:, 0, :], ACT.Sqrt).then_inc(S["n_rs"], 1)

            def attention(l, x, V):
                steps = [(qt, h) for qt in range(TT) for h in range(H)]
                for i in range(len(steps) + 1):
                    if i < len(steps):
                        qt, h = steps[i]
                        n = (qt + 1) * P
                        act.wait_ge(S[x + "_ss"], at(l, x + "_ss", i + 1))
                        act_fn(V["ss"][:, i % 2, 0:n], V["ss"][:, i % 2, 0:n], ACT.Exp, bias=sml[:, i % 2:i % 2 + 1], accum_out=sml[:, 2 + i % 2:3 + i % 2]).then_inc(S[x + "_p"], 1)
                    if i >= 1:
                        qt, h = steps[i - 1]
                        act.wait_ge(a_full, filled.next())
                        b = filled.bank()
                        if i >= 3:
                            act.wait_ge(S[x + "_o"], at(l, x + "_o", i - 2))
                        act_fn(V["pt"][:, (i - 1) % 2, 0:qt + 1, :], b[:, 0:(qt + 1) * P].rearrange("p (k n) -> p k n", n=P), ACT.Copy).then_inc(S[x + "_pt"], 1)

            for i in range(2):
                act.wait_ge(S["tab_arg"], i + 1)
                act_fn(POS["sin"][:, i, :], POS["red"][:, i, :], ACT.Sin)
                act_fn(POS["cos"][:, i, :], POS["red"][:, i, :], ACT.Sin, scale=0.5).then_inc(S["tab_sin"], 1)

            for l in range(L):
                norm_root(2 * l)
                if l == 0:
                    act.wait_ge(tab_out, 64)
                for i in range(8):
                    act.wait_ge(a_full, filled.next())
                    b = filled.bank()
                    act_fn(R["rw"][:, i, 1:T + 1], b[:], ACT.Copy).then_inc(S["r_in"], 1)
                act.wait_ge(a_full, filled.next())
                b = filled.bank()
                act_fn(misc[:, 0, :], b[:], ACT.Copy).then_inc(S["misc_in"], 1)
                act.wait_ge(a_full, filled.next())
                b = filled.bank()
                act_fn(misc[64:96, 1, :], b[64:96, :], ACT.Copy).then_inc(S["misc_in"], 1)
                act.wait_ge(a_full, filled.next())
                b = filled.bank()
                act_fn(misc[0:64, 2, :], b[0:64, :], ACT.Copy).then_inc(S["misc_in"], 1)
                act.wait_ge(a_full, filled.next())
                b = filled.bank()
                act_fn(ab[:, :, :], b[:, 0:64].rearrange("p (t n) -> p t n", n=16), ACT.Copy).then_inc(S["ab_in"], 1)
                act.wait_ge(S["r_mix"], at(l, "r_mix", 8))
                act_fn(R["rm"][0:64, 6, :], R["rm"][0:64, 6, :], ACT.Tanh).then_inc(S["r_act"], 1)
                act_fn(R["rm"][:, 7, :], R["rm"][:, 7, :], ACT.Sigmoid).then_inc(S["r_act"], 1)
                act.wait_ge(par_here, 16 * (l + 1))
                for nm, bias in (("sw", "w0"), ("a", "a0"), ("g", None)):
                    for f in range(2):
                        act.wait_ge(a_full, filled.next())
                        b = filled.bank()
                        if bias:
                            act_fn(R[nm][:, f, :], b[:], ACT.Sigmoid, bias=pr(bias, f)).then_inc(S["r_lora"], 1)
                        else:
                            act_fn(R[nm][:, f, :], b[:], ACT.Copy).then_inc(S["r_lora"], 1)
                act.wait_ge(S["r_cum"], at(l, "r_cum", 1))
                act_fn(R["p"], R["cs"], ACT.Exp, scale=-DECAY).then_inc(S["r_dec"], 1)
                act_fn(R["pi"], R["cs"], ACT.Exp, scale=DECAY).then_inc(S["r_dec"], 1)
                act.wait_ge(S["r_ex"], at(l, "r_ex", 1))
                act_fn(R["pe"], R["sw"], ACT.Exp, scale=-DECAY).then_inc(S["r_dec"], 1)
                act.wait_ge(S["r_l2r"], at(l, "r_l2r", 1))
                act_fn(R["tmp"], R["tmp"], ACT.Sqrt).then_inc(S["r_l2s"], 1)
                act.wait_ge(S["r_feat"], at(l, "r_feat", 4))
                tok(l, "r", R, ("e_tok", "v_tok", "b_tok", "k_tokz"))
                invert(l, "r", R, lambda: None)
                after_inverse(l, "r", R)
                outputs(l, "r", R, range(NC))
                act.wait_ge(S["r_gr"], at(l, "r_gr", 1))
                act_fn(R["sq"], R["sq"], ACT.Sqrt).then_inc(S["r_gs"], 1)

                for i in range(6):
                    act.wait_ge(a_full, filled.next())
                    b = filled.bank()
                    if i == 0:
                        act.wait_ge(S["g_pad"], at(l, "g_pad", 1))
                    act_fn(G["ci"][:, i, 3:T + 3], b[:], ACT.Copy).then_inc(S["g_in"], 1)
                for i in range(2):
                    act.wait_ge(a_full, filled.next())
                    b = filled.bank()
                    act_fn(G["z"][:, i, :], b[:], ACT.Copy).then_inc(S["g_z"], 1)
                act.wait_ge(S["g_t1"], at(l, "g_t1", 1))
                act_fn(gsm[:, 1, :], gsm[:, 1, :], ACT.Exp).then_inc(act_step, 1)
                act_fn(sml[:, 8:12], pr("a_log"), ACT.Exp).then_inc(S["g_t2"], 1)
                act.wait_ge(act_step, 2 * l + 1)
                act_fn(gsm[:, 1, :], gsm[:, 1, :], ACT.Ln, bias=1.0).then_inc(act_step, 1)
                act.wait_ge(act_step, 2 * l + 2)
                act.wait_ge(S["g_conv"], at(l, "g_conv", 6))
                act_fn(gsm[:, 5, :], ab[:, :, 4:8], ACT.Sigmoid)
                act_fn(G["sig"], G["co"], ACT.Sigmoid).then_inc(S["g_sig"], 1)
                act_fn(G["bh"], G["z"], ACT.Sigmoid).then_inc(S["g_zs"], 1)
                act.wait_ge(S["g_l2r"], at(l, "g_l2r", 1))
                act_fn(G["rs"], G["rs"], ACT.Sqrt).then_inc(S["g_l2s"], 1)
                merge_sig(l)
                act.wait_ge(S["g_qk"], at(l, "g_qk", 1))
                for i in range(6):
                    act.wait_ge(a_full, filled.next())
                    b = filled.bank()
                    f = i % 2
                    dst = (G["egc"], G["ers"], G["beta"])[i // 2][:, f, :]
                    act_fn(dst, b[:], ACT.Exp if i < 4 else ACT.Copy).then_inc(S["g_feat"], 1)
                for t in range(TT):
                    act.wait_ge(S["g_row"], at(l, "g_row", t + 1))
                    act_fn(G["d"][:, t * H:(t + 1) * H, :], G["d"][:, t * H:(t + 1) * H, :], ACT.Exp).then_inc(S["g_d"], 1)
                act.wait_ge(S["g_prep"], at(l, "g_prep", 2))
                tok(l, "g", G, ("e_tok", "v_tok", "b_tok"))
                invert(l, "g", G, lambda: merge_sig(l))
                after_inverse(l, "g", G)
                outputs(l, "g", G, range(0, 8))
                act.wait_ge(S["g_gr"], at(l, "g_gr", 1))
                act_fn(G["sq2"], G["sq2"], ACT.Sqrt).then_inc(S["g_gs"], 1)

                act.wait_ge(S["g_out"], at(l, "g_out", 1))
                for i in range(8):
                    act.wait_ge(a_full, filled.next())
                    b = filled.bank()
                    dst = Dv["iq"][:, i, :] if i < 4 else Dv["q"][:, i - 4, :] if i < 6 else Dv["k"][:, i - 6, :]
                    act_fn(dst, b[:], ACT.Copy).then_inc(S["d_in"], 1)
                for half in range(2):
                    act.wait_ge(a_full, filled.next())
                    b = filled.bank()
                    act_fn(Dv["v"][:, 2 * half:2 * half + 2, :], b[:].rearrange("p (t n) -> p t n", n=256), ACT.Copy).then_inc(S["d_v"], 1)
                i = 0
                for qt in range(1, TT):
                    n = (qt + 1) * P
                    for h in range(8):
                        act.wait_ge(a_full, filled.next())
                        b = filled.bank()
                        if i >= 2:
                            act.wait_ge(S["d_acc"], at(l, "d_acc", i - 1))
                        act_fn(Dv["rl"][:, i % 2, 0:n], b[:, 0:n], ACT.Relu).then_inc(S["d_sc"], 1)
                        i += 1
                    merge_sig(l)
                merge_sig(l)
                attention(l, "d", Dv)

                act.wait_ge(S["d_o"], at(l, "d_o", 16))
                for j in range(2):
                    act.wait_ge(a_full, filled.next())
                    b = filled.bank()
                    act_fn(Mv["cq"][:, j, :], b[:], ACT.Copy).then_inc(S["m_in"], 1)
                merge_sig(l)
                act.wait_ge(S["m_rec"], at(l, "m_rec", 1))
                act_fn(Mv["rs"], Mv["rs"], ACT.Sqrt).then_inc(S["m_rs"], 1)
                merge_sig(l)
                for h in range(H):
                    act.wait_ge(a_full, filled.next())
                    b = filled.bank()
                    act_fn(Mv["q"][0:96, h, :], b[0:96, :], ACT.Copy).then_inc(S["m_q"], 1)
                for h in range(H):
                    act.wait_ge(a_full, filled.next())
                    b = filled.bank()
                    act_fn(Mv["k"][0:64, h, :], b[0:64, :], ACT.Copy).then_inc(S["m_k"], 1)
                for half in range(2):
                    act.wait_ge(a_full, filled.next())
                    b = filled.bank()
                    act_fn(Mv["v"][:, 2 * half:2 * half + 2, :], b[:].rearrange("p (t n) -> p t n", n=256), ACT.Copy).then_inc(S["m_v"], 1)
                merge_sig(l)
                merge_sig(l)
                attention(l, "m", Mv)
                for _ in range(4):
                    merge_sig(l)
                norm_root(2 * l + 1)
                for i in range(32):
                    act.wait_ge(a_full, filled.next())
                    b = filled.bank()
                    act_fn(up_act[:, i, :], b[:], ACT.Relu).then_inc(S["up_relu"], 1)
            norm_root(2 * L)
            for t in range(TT):
                for half in range(2):
                    act.wait_ge(a_full, filled.next())
                    b = filled.bank()
                    act_fn(xout[:, t, half * T:(half + 1) * T], b[:], ACT.Copy).then_inc(S["o_tok"], 1)

        @block.vector
        def _(dve):
            v = nc.vector
            filled = Filled(bank_v)
            counts = {}

            def reached(name):
                counts[name] = counts.get(name, 0) + 1
                return counts[name]

            def link(ins):
                ins.then_inc(dve_step, 1)
                dve.wait_ge(dve_step, reached("step"))

            def tt(out_, a, b, op):
                link(v.tensor_tensor(out_, a, b, op))

            def ts(out_, a, s1, s2, op0, op1=ALU.bypass):
                link(v.tensor_scalar(out_, a, s1, s2, op0, op1))

            def stt(out_, a, s, b, op0, op1):
                link(v.scalar_tensor_tensor(out_, a, s, b, op0, op1))

            MUL, ADD, SUB = ALU.mult, ALU.add, ALU.subtract
            hm = (cst("blocks")[:, 0:1], cst("blocks")[:, C:C + 1])

            def norm(n, gain):
                v.tensor_tensor(hT[:], xT[:], xT[:], MUL).then_inc(S["n_sq"], 1)
                dve.wait_ge(S["n_sq"], reached("n_sq"))
                dve.wait_ge(v_full, filled.next())
                b = filled.bank()
                v.tensor_scalar(sg[:, 0, :], b[:], 1.0 / D, EPS, MUL, ADD).then_inc(S["n_var"], 1)
                dve.wait_ge(S["n_var"], reached("n_var"))
                v.reciprocal(sg[:, 0, :], sg[:, 0, :]).then_inc(S["n_rec"], 1)
                dve.wait_ge(S["n_rec"], reached("n_rec"))
                dve.wait_ge(S["n_rs"], n + 1)
                for k in range(KT):
                    v.scalar_tensor_tensor(hT[:, k, :], xT[:, k, :], pr(gain, k), sg[:, 0, :], MUL, MUL).then_inc(S["n_h"], 1)
                    dve.wait_ge(S["n_h"], reached("n_h"))

            def bank3(b, n):
                return b[:].rearrange("p (m n) -> p m n", n=n)

            def masked(x, dst, mask, count):
                for t in range(TT):
                    dve.wait_ge(v_full, filled.next())
                    b = filled.bank()
                    m = mask(t)
                    v.tensor_tensor(dst[:, t * H:(t + 1) * H, :], bank3(b, P), m, MUL).then_inc(S[x + "_mat"], 1)
                    dve.wait_ge(S[x + "_mat"], reached(x + "_mat"))

            def invert(l, x, V, fill):
                link(v.memset(V["x_bd"], 0.0))
                link(v.memset(V["y_bd"], 0.0))
                eye = cst("eye_c").unsqueeze(1).to_broadcast([P, M, C])
                link(v.tensor_copy(V["t_c"], eye))
                v.tensor_copy(V["x_c"], eye).then_inc(S[x + "_eye"], 1)
                dve.wait_ge(S[x + "_eye"], reached(x + "_eye"))
                for n, s in enumerate(LEVELS):
                    lev = cst(f"level{s}").unsqueeze(1).to_broadcast([P, 8, C])
                    for half in range(2):
                        ms = slice(8 * half, 8 * half + 8)
                        dve.wait_ge(v_full, filled.next())
                        b = filled.bank()
                        v.tensor_tensor(V["y_c"][:, ms, :], bank3(b, C), lev, MUL).then_inc(S[x + "_y"], 1)
                        dve.wait_ge(S[x + "_y"], reached(x + "_y"))
                    if n < len(LEVELS) - 1:
                        for half in range(2):
                            ms = slice(8 * half, 8 * half + 8)
                            dve.wait_ge(v_full, filled.next())
                            b = filled.bank()
                            v.tensor_tensor(V["t_c"][:, ms, :], V["t_c"][:, ms, :], bank3(b, C), SUB).then_inc(S[x + "_t"], 1)
                            dve.wait_ge(S[x + "_t"], reached(x + "_t"))
                    for half in range(2):
                        ms = slice(8 * half, 8 * half + 8)
                        dve.wait_ge(v_full, filled.next())
                        b = filled.bank()
                        if n:
                            dve.wait_ge(S[x + "_xbd"], at(l, x + "_xbd", 2 * (n - 1) + half + 1))
                        v.tensor_tensor(V["x_c"][:, ms, :], V["x_c"][:, ms, :], bank3(b, C), SUB).then_inc(S[x + "_x"], 1)
                        dve.wait_ge(S[x + "_x"], reached(x + "_x"))
                    if n % 2 == 1:
                        fill()

            def scan(l, x, V, fill):
                v.memset(s_z[:], 0.0).then_inc(S[x + "_s0"], 1)
                dve.wait_ge(S[x + "_s0"], reached(x + "_s0"))
                dve.wait_ge(S[x + "_u"], at(l, x + "_u", 2))
                for c in range(NC):
                    t, par_ = divmod(c, 2)
                    rows = slice(par_ * C, (par_ + 1) * C)
                    dve.wait_ge(v_full, filled.next())
                    b = filled.bank()
                    v.tensor_tensor(un_z[rows, par_, :], V["up"][rows, t, :], b[rows, 0:4 * C], SUB).then_inc(S[x + "_ws"], 1)
                    dve.wait_ge(S[x + "_ws"], reached(x + "_ws"))
                    dve.wait_ge(v_full, filled.next())
                    b = filled.bank()
                    for h in range(H):
                        f, hp = divmod(h, 2)
                        hr = slice(hp * C, (hp + 1) * C)
                        ins = v.scalar_tensor_tensor(out=s_z[hr, f, hp, :], in0=s_z[hr, f, hp, :], scalar=pc[hr, f, c:c + 1],
                                                     in1=b[hr, f * C:(f + 1) * C], op0=MUL, op1=ADD)
                    ins.then_inc(S[x + "_s"], 1)
                    dve.wait_ge(S[x + "_s"], reached(x + "_s"))
                    if c in (1, 4):
                        fill()

            merged = [0]

            def merge(l, first=False):
                for _ in range(2):
                    n = merged[0]
                    m = n % 8
                    dve.wait_ge(v_full, filled.next())
                    b = filled.bank()
                    dve.wait_ge(S["mg_sig"], n + 1)
                    s = sg[:, n % 2, :]
                    if first:
                        v.tensor_tensor(mg[:, m, :], b[:], s, MUL).then_inc(S["mg_done"], 1)
                        dve.wait_ge(S["mg_done"], reached("mg_done"))
                    else:
                        tt(s, b[:], s, MUL)
                        v.tensor_tensor(mg[:, m, :], mg[:, m, :], s, ADD).then_inc(S["mg_done"], 1)
                        dve.wait_ge(S["mg_done"], reached("mg_done"))
                    merged[0] += 1

            def attention(l, x, V, scale, bias, slot):
                steps = [(qt, h) for qt in range(TT) for h in range(H)]
                for i in range(len(steps) + 2):
                    if i < len(steps):
                        qt, h = steps[i]
                        n = (qt + 1) * P
                        dve.wait_ge(v_full, filled.next())
                        b = filled.bank()
                        if i >= 2:
                            dve.wait_ge(S[x + "_pt"], at(l, x + "_pt", i - 1))
                        ss = V["ss"][:, i % 2, 0:n]
                        stt(ss, b[:, 0:n], scale, bias(qt), MUL, ADD)
                        v.tensor_reduce(sml[:, i % 2:i % 2 + 1], ss, AX_X, ALU.max, negate=True).then_inc(S[x + "_ss"], 1)
                        dve.wait_ge(S[x + "_ss"], reached(x + "_ss"))
                    if 1 <= i <= len(steps):
                        j = i - 1
                        qt, h = steps[j]
                        n = (qt + 1) * P
                        dve.wait_ge(S[x + "_p"], at(l, x + "_p", j + 1))
                        link(v.reciprocal(sml[:, 4 + j % 2:5 + j % 2], sml[:, 2 + j % 2:3 + j % 2]))
                        ss = V["ss"][:, j % 2, 0:n]
                        v.tensor_scalar(ss, ss, sml[:, 4 + j % 2:5 + j % 2], None, MUL).then_inc(S[x + "_pn"], 1)
                        dve.wait_ge(S[x + "_pn"], reached(x + "_pn"))
                    if i >= 2:
                        qt, h = steps[i - 2]
                        dve.wait_ge(v_full, filled.next())
                        b = filled.bank()
                        rows = slice((h % 2) * C, (h % 2 + 1) * C)
                        v.tensor_copy(yo[rows, slot, h // 2, qt * P:(qt + 1) * P], b[rows, 0:P]).then_inc(S[x + "_o"], 1)
                        dve.wait_ge(S[x + "_o"], reached(x + "_o"))

            link(v.memset(un_z[:], 0.0))
            link(v.memset(misc[:], 0.0))
            dve.wait_ge(const_here, 16)
            for k in range(KT):
                dve.wait_ge(v_full, filled.next())
                b = filled.bank()
                v.tensor_copy(xT[:, k, :], b[:]).then_inc(S["x_t"], 1)
                dve.wait_ge(S["x_t"], reached("x_t"))
            dve.wait_ge(pos_here, 16)
            link(v.tensor_copy(POS["f"], POS["i"]))
            for i, nm in enumerate(rotors):
                ts(POS["ang"], POS["f"], cst("freq_" + nm), None, MUL)
                ts(POS["k"], POS["ang"], float(1.0 / (2.0 * np.pi)), MAGIC, MUL, ADD)
                ts(POS["k"], POS["k"], MAGIC, None, SUB)
                red = POS["red"][:, i, :]
                stt(red, POS["k"], -TWO_PI[0], POS["ang"], MUL, ADD)
                stt(red, POS["k"], -TWO_PI[1], red, MUL, ADD)
                stt(red, POS["k"], -TWO_PI[2], red, MUL, ADD)
                v.tensor_scalar(red, red, 3.1415925, -3.1415925, ALU.min, ALU.max).then_inc(S["tab_arg"], 1)
                dve.wait_ge(S["tab_arg"], reached("tab_arg"))
            for i in range(2):
                dve.wait_ge(S["tab_sin"], i + 1)
                cos = POS["cos"][:, i, :]
                tt(cos, cos, cos, MUL)
                v.tensor_scalar(cos, cos, -2.0, 1.0, MUL, ADD).then_inc(S["tab"], 1)
                dve.wait_ge(S["tab"], reached("tab"))

            for l in range(L):
                dve.wait_ge(par_here, 16 * (l + 1))
                norm(2 * l, "mix_g")
                if l == 0:
                    dve.wait_ge(tab_out, 64)
                v.memset(R["rw"][:, :, 0:1], 0.0).then_inc(S["r_zero"], 1)
                dve.wait_ge(S["r_zero"], reached("r_zero"))
                ts(sml[:, 12:14], pr("k_a"), -1.0, 1.0, MUL, ADD)
                dve.wait_ge(S["r_in"], at(l, "r_in", 8))
                tt(R["rm"], R["rw"][:, :, 0:T], R["rw"][:, :, 1:T + 1], SUB)
                for i in range(8):
                    v.scalar_tensor_tensor(R["rm"][:, i, :], R["rm"][:, i, :], pr("mu", i), R["rw"][:, i, 1:T + 1], MUL, ADD).then_inc(S["r_mix"], 1)
                    dve.wait_ge(S["r_mix"], reached("r_mix"))
                r_, k_, v_ = R["rm"][:, 0:2, :], R["rm"][:, 2:4, :], R["rm"][:, 4:6, :]
                for f in range(2):
                    ts(R["kk"][:, f, :], k_[:, f, :], pr("k_k", f), None, MUL)
                v.tensor_tensor(R["tmp"], R["kk"], R["kk"], MUL).then_inc(S["r_sq"], 1)
                dve.wait_ge(S["r_sq"], reached("r_sq"))
                dve.wait_ge(S["r_lora"], at(l, "r_lora", 2))
                for f in range(2):
                    for c in range(NC):
                        cs = slice(c * C, (c + 1) * C)
                        ins = v.tensor_tensor_scan(R["cs"][:, f, cs], cst("ones")[:, 0:C], R["sw"][:, f, cs], 0.0, MUL, ADD)
                ins.then_inc(S["r_cum"], 1)
                dve.wait_ge(S["r_cum"], reached("r_cum"))
                v.tensor_tensor(R["sw"], R["cs"], R["sw"], SUB).then_inc(S["r_ex"], 1)
                dve.wait_ge(S["r_ex"], reached("r_ex"))
                for f in range(2):
                    dve.wait_ge(v_full, filled.next())
                    b = filled.bank()
                    v.tensor_scalar(R["tmp"][:, f, :], b[:], EPS, None, ADD).then_inc(S["r_l2"], 1)
                    dve.wait_ge(S["r_l2"], reached("r_l2"))
                v.reciprocal(R["tmp"], R["tmp"]).then_inc(S["r_l2r"], 1)
                dve.wait_ge(S["r_l2r"], reached("r_l2r"))
                dve.wait_ge(S["r_l2s"], at(l, "r_l2s", 1))
                tt(R["kk"], R["kk"], R["tmp"], MUL)
                dve.wait_ge(S["r_lora"], at(l, "r_lora", 4))
                for f in range(2):
                    ts(R["tmp"][:, f, :], R["a"][:, f, :], pr("k_a", f), sml[:, 12 + f:13 + f], MUL, ADD)
                tt(k_, k_, R["tmp"], MUL)
                for f in range(2):
                    v.scalar_tensor_tensor(R["tmp"][:, f, :], k_[:, f, :], pr("r_k", f), r_[:, f, :], MUL, MUL).then_inc(S["r_bsq"], 1)
                    dve.wait_ge(S["r_bsq"], reached("r_bsq"))
                for f in range(2):
                    dve.wait_ge(v_full, filled.next())
                    b = filled.bank()
                    v.tensor_tensor(R["bon"][:, f, :], b[:], v_[:, f, :], MUL).then_inc(S["r_bon"], 1)
                    dve.wait_ge(S["r_bon"], reached("r_bon"))
                dve.wait_ge(S["r_dec"], at(l, "r_dec", 3))
                link(v.tensor_copy(pc[:], R["p"].rearrange("p f (c k) -> p f c k", k=C)[:, :, :, C - 1]))
                tt(R["et"], R["pe"], R["kk"], MUL)
                tt(R["rt"], R["p"], r_, MUL)
                tt(R["tmp"], R["kk"], R["a"], MUL)
                for hp in range(2):
                    stt(R["bz"][:, :, hp, :], R["pi"], hm[hp], R["tmp"], MUL, MUL)
                    stt(R["kz"][:, :, hp, :], R["pi"], hm[hp], k_, MUL, MUL)
                tt(R["bh"], R["tmp"], R["pi"], MUL)
                tt(R["kh"], k_, R["pi"], MUL)
                link(v.memset(R["k_tokz"], 0.0))
                for nm in ("bh", "kh"):
                    for f in range(2):
                        y = R[nm][:, f, :].rearrange("p (c k) -> p c k", k=C)
                        v.tensor_tensor(y, y, pc[:, f, :].unsqueeze(2).to_broadcast([P, NC, C]), MUL).then_inc(S["r_feat"], 1)
                        dve.wait_ge(S["r_feat"], reached("r_feat"))
                before = cst("before").unsqueeze(1).to_broadcast([P, H, P])
                upto = cst("upto").unsqueeze(1).to_broadcast([P, H, P])
                masked("r", R["u"], lambda t: before, 4)
                dve.wait_ge(S["r_tok"], at(l, "r_tok", 8))
                masked("r", R["akk"], lambda t: before, 4)
                masked("r", R["ark"], lambda t: upto, 4)
                masked("r", R["arb"], lambda t: upto, 4)
                invert(l, "r", R, lambda: None)
                for half in range(2):
                    dve.wait_ge(v_full, filled.next())
                    b = filled.bank()
                    v.tensor_scalar(R["y1"][:, 2 * half:2 * half + 2, :], bank3(b, 256), -1.0, None, MUL).then_inc(S["r_y1"], 1)
                    dve.wait_ge(S["r_y1"], reached("r_y1"))
                scan(l, "r", R, lambda: None)
                for f in range(2):
                    dve.wait_ge(v_full, filled.next())
                    b = filled.bank()
                    v.scalar_tensor_tensor(R["o"][:, f, :], b[:], -1.0 / C, R["o"][:, f, :], MUL, ADD).then_inc(S["r_mean"], 1)
                    dve.wait_ge(S["r_mean"], reached("r_mean"))
                v.tensor_tensor(R["sq"], R["o"], R["o"], MUL).then_inc(S["r_sq2"], 1)
                dve.wait_ge(S["r_sq2"], reached("r_sq2"))
                for f in range(2):
                    dve.wait_ge(v_full, filled.next())
                    b = filled.bank()
                    v.tensor_scalar(R["sq"][:, f, :], b[:], 1.0 / C, GN_EPS, MUL, ADD).then_inc(S["r_gv"], 1)
                    dve.wait_ge(S["r_gv"], reached("r_gv"))
                v.reciprocal(R["sq"], R["sq"]).then_inc(S["r_gr"], 1)
                dve.wait_ge(S["r_gr"], reached("r_gr"))
                dve.wait_ge(S["r_gs"], at(l, "r_gs", 1))
                tt(R["o"], R["o"], R["sq"], MUL)
                for f in range(2):
                    ts(R["o"][:, f, :], R["o"][:, f, :], pr("ln_w", f), pr("ln_b", f), MUL, ADD)
                tt(R["o"], R["o"], R["bon"], ADD)
                v.tensor_tensor(yo[:, 0, :, :], R["o"], R["g"], MUL).then_inc(S["r_out"], 1)
                dve.wait_ge(S["r_out"], reached("r_out"))

                v.memset(G["ci"][:, :, 0:3], 0.0).then_inc(S["g_pad"], 1)
                dve.wait_ge(S["g_pad"], reached("g_pad"))
                dve.wait_ge(S["ab_in"], at(l, "ab_in", 1))
                th = lambda i: gsm[:, i, :].rearrange("p (t h) -> p t h", h=H)
                tt(th(0), ab[:, :, 0:4], pr("dt").unsqueeze(1).to_broadcast([P, TT, H]), ADD)
                v.scalar_tensor_tensor(gsm[:, 1, :], gsm[:, 0, :], -1.0, gsm[:, 0, :], MUL, ALU.min).then_inc(S["g_t1"], 1)
                dve.wait_ge(S["g_t1"], reached("g_t1"))
                ts(ab[:, :, 8:16], ab[:, :, 8:16], float((8 * 64) ** -0.5), None, MUL)
                for i in range(6):
                    dve.wait_ge(S["g_in"], at(l, "g_in", i + 1))
                    ts(G["co"][:, i, :], G["ci"][:, i, 0:T], pr("conv", 4 * i), None, MUL)
                    for j in range(1, 3):
                        stt(G["co"][:, i, :], G["ci"][:, i, j:j + T], pr("conv", 4 * i + j), G["co"][:, i, :], MUL, ADD)
                    v.scalar_tensor_tensor(G["co"][:, i, :], G["ci"][:, i, 3:3 + T], pr("conv", 4 * i + 3), G["co"][:, i, :], MUL, ADD).then_inc(S["g_conv"], 1)
                    dve.wait_ge(S["g_conv"], reached("g_conv"))
                dve.wait_ge(S["g_sig"], at(l, "g_sig", 1))
                tt(G["co"], G["co"], G["sig"], MUL)
                v.tensor_tensor(G["sq"], G["co"][:, 0:4, :], G["co"][:, 0:4, :], MUL).then_inc(S["g_sq"], 1)
                dve.wait_ge(S["g_sq"], reached("g_sq"))
                stt(gsm[:, 2, :], gsm[:, 0, :], 0.0, gsm[:, 1, :], ALU.max, ADD)
                stt(th(4), th(2), -1.0, sml[:, 8:12].unsqueeze(1).to_broadcast([P, TT, H]), MUL, MUL)
                for i, nm in ((4, "g_wide"), (5, "b_wide")):
                    v.tensor_copy(G[nm].rearrange("p (m n) -> p m n", n=C), gsm[:, i, :].unsqueeze(2).to_broadcast([P, M, C])).then_inc(S["g_g"], 1)
                    dve.wait_ge(S["g_g"], reached("g_g"))
                dve.wait_ge(S["g_zs"], at(l, "g_zs", 1))
                tt(G["z"], G["z"], G["bh"], MUL)
                for i in range(4):
                    dve.wait_ge(v_full, filled.next())
                    b = filled.bank()
                    v.tensor_scalar(G["rs"][:, i, :], b[:], EPS, None, ADD).then_inc(S["g_l2"], 1)
                    dve.wait_ge(S["g_l2"], reached("g_l2"))
                v.reciprocal(G["rs"], G["rs"]).then_inc(S["g_l2r"], 1)
                dve.wait_ge(S["g_l2r"], reached("g_l2r"))
                dve.wait_ge(S["g_l2s"], at(l, "g_l2s", 1))
                stt(G["co"][:, 0:2, :], G["co"][:, 0:2, :], C ** -0.5, G["rs"][:, 0:2, :], MUL, MUL)
                v.tensor_tensor(G["co"][:, 2:4, :], G["co"][:, 2:4, :], G["rs"][:, 2:4, :], MUL).then_inc(S["g_qk"], 1)
                dve.wait_ge(S["g_qk"], reached("g_qk"))
                q_, k_, v_ = G["co"][:, 0:2, :], G["co"][:, 2:4, :], G["co"][:, 4:6, :]
                merge(l, True)
                dve.wait_ge(v_full, filled.next())
                b = filled.bank()
                v.tensor_copy(gsm[:, 3, :], b[:, 0:M]).then_inc(S["g_gc"], 1)
                dve.wait_ge(S["g_gc"], reached("g_gc"))
                for t in range(TT):
                    dve.wait_ge(v_full, filled.next())
                    b = filled.bank()
                    for h in range(H):
                        m = t * H + h
                        ins = v.tensor_scalar(G["d"][:, m, :], b[:, h * P:(h + 1) * P], gsm[:, 3, m:m + 1], 0.0, SUB, ALU.min)
                    ins.then_inc(S["g_row"], 1)
                    dve.wait_ge(S["g_row"], reached("g_row"))
                for t in range(TT):
                    dve.wait_ge(S["g_d"], at(l, "g_d", t + 1))
                    v.tensor_tensor(G["d"][:, t * H:(t + 1) * H, :], G["d"][:, t * H:(t + 1) * H, :], upto, MUL).then_inc(S["g_dm"], 1)
                    dve.wait_ge(S["g_dm"], reached("g_dm"))
                dve.wait_ge(S["g_feat"], at(l, "g_feat", 6))
                link(v.tensor_copy(pc[:], G["egc"].rearrange("p f (c k) -> p f c k", k=C)[:, :, :, C - 1]))
                tt(G["kb"], k_, G["beta"], MUL)
                tt(G["rt"], q_, G["egc"], MUL)
                tt(G["et"], G["kb"], G["egc"], MUL)
                tt(G["bh"], k_, G["ers"], MUL)
                tt(G["vb"], v_, G["beta"], MUL)
                for hp in range(2):
                    v.tensor_scalar(G["kz"][:, :, hp, :], k_, hm[hp], None, MUL).then_inc(S["g_prep"], 1)
                    dve.wait_ge(S["g_prep"], reached("g_prep"))
                masked("g", G["u"], lambda t: G["d"][:, t * H:(t + 1) * H, :], 4)
                masked("g", G["arb"], lambda t: G["d"][:, t * H:(t + 1) * H, :], 4)
                dve.wait_ge(S["g_tok"], at(l, "g_tok", 6))
                invert(l, "g", G, lambda: merge(l, True))
                scan(l, "g", G, lambda: None)
                dve.wait_ge(S["g_o"], at(l, "g_o", NC))
                v.tensor_tensor(G["sq2"], G["o"], G["o"], MUL).then_inc(S["g_sq2"], 1)
                dve.wait_ge(S["g_sq2"], reached("g_sq2"))
                for f in range(2):
                    dve.wait_ge(v_full, filled.next())
                    b = filled.bank()
                    v.tensor_scalar(G["sq2"][:, f, :], b[:], 1.0 / C, EPS, MUL, ADD).then_inc(S["g_gv"], 1)
                    dve.wait_ge(S["g_gv"], reached("g_gv"))
                v.reciprocal(G["sq2"], G["sq2"]).then_inc(S["g_gr"], 1)
                dve.wait_ge(S["g_gr"], reached("g_gr"))
                dve.wait_ge(S["g_gs"], at(l, "g_gs", 1))
                stt(G["o"], G["o"], pr("gdn_g", 0), G["sq2"], MUL, MUL)
                v.tensor_tensor(yo[:, 1, :, :], G["o"], G["z"], MUL).then_inc(S["g_out"], 1)
                dve.wait_ge(S["g_out"], reached("g_out"))

                dve.wait_ge(tab_d_here, 16 * (l + 1))
                cos, sin = Dv["tab"][:, 0, :], Dv["tab"][:, 1, :]
                link(v.memset(Dv["ikz"], 0.0))
                dve.wait_ge(v_full, filled.next())
                b = filled.bank()
                for hp in range(2):
                    hr = slice(hp * C, (hp + 1) * C)
                    ins = v.tensor_tensor(Dv["ikz"][hr, hp, :], b[hr, :], cos[hr, :], MUL)
                ins.then_inc(S["d_ik"], 1)
                dve.wait_ge(S["d_ik"], reached("d_ik"))
                dve.wait_ge(v_full, filled.next())
                b = filled.bank()
                v.tensor_tensor(Dv["tmp"], b[:], sin, MUL).then_inc(S["d_ik"], 1)
                dve.wait_ge(S["d_ik"], reached("d_ik"))
                for hp in range(2):
                    hr = slice(hp * C, (hp + 1) * C)
                    tt(Dv["ikz"][hr, hp, :], Dv["ikz"][hr, hp, :], Dv["tmp"][hr, :], ADD)
                for i in range(8):
                    x_ = Dv["iq"][:, i, :] if i < 4 else Dv["q"][:, i - 4, :] if i < 6 else Dv["k"][:, i - 6, :]
                    dve.wait_ge(v_full, filled.next())
                    b = filled.bank()
                    tt(Dv["tmp"], b[:], sin, MUL)
                    tt(x_, x_, cos, MUL)
                    v.tensor_tensor(x_, x_, Dv["tmp"], ADD).then_inc(S["d_rot"], 1)
                    dve.wait_ge(S["d_rot"], reached("d_rot"))
                for hp in range(2):
                    v.tensor_scalar(Dv["kz"][:, :, hp, :], Dv["k"], hm[hp], None, MUL).then_inc(S["d_kz"], 1)
                    dve.wait_ge(S["d_kz"], reached("d_kz"))
                i = 0
                for qt in range(1, TT):
                    n = (qt + 1) * P
                    sc, wk, gt, eq, cum = (Dv[x_][:, 0:n] for x_ in ("sc", "wk", "gt", "eq", "cum"))
                    for h in range(8):
                        dve.wait_ge(S["d_sc"], at(l, "d_sc", i + 1))
                        iw, rl = ab[:, qt, 8 + h:9 + h], Dv["rl"][:, i % 2, 0:n]
                        if h == 0:
                            v.tensor_scalar(sc, rl, iw, None, MUL).then_inc(S["d_acc"], 1)
                            dve.wait_ge(S["d_acc"], reached("d_acc"))
                        else:
                            v.scalar_tensor_tensor(sc, rl, iw, sc, MUL, ADD).then_inc(S["d_acc"], 1)
                            dve.wait_ge(S["d_acc"], reached("d_acc"))
                        i += 1
                    tt(sc[:, qt * P:n], sc[:, qt * P:n], cst("causal"), ADD)
                    src = sc
                    for r in range(TOPK // 8):
                        link(v.max(m8[:], src))
                        if r < TOPK // 8 - 1:
                            link(v.match_replace(wk, m8[:], src, -3e38))
                            src = wk
                    ts(gt, sc, m8[:, 7:8], None, ALU.is_gt)
                    link(v.tensor_reduce(sml[:, 6:7], gt, AX_X, ADD))
                    ts(sml[:, 7:8], sml[:, 6:7], -1.0, float(TOPK), MUL, ADD)
                    ts(eq, sc, m8[:, 7:8], None, ALU.is_equal)
                    link(v.tensor_tensor_scan(cum, eq, eq, 0.0, ADD, ALU.max))
                    stt(eq, cum, sml[:, 7:8], eq, ALU.is_le, MUL)
                    tt(gt, gt, eq, ADD)
                    v.tensor_scalar(Dv["bias"][:, qt, 0:n], gt, -NEG, NEG, MUL, ADD).then_inc(S["d_bias"], 1)
                    dve.wait_ge(S["d_bias"], reached("d_bias"))
                    merge(l)
                merge(l)
                attention(l, "d", Dv, C ** -0.5, lambda qt: Dv["bias"][:, qt, 0:(qt + 1) * P] if qt else cst("causal"), 0)

                dve.wait_ge(tab_m_here, 16 * (l + 1))
                rp = slice(64, 96)
                cos, sin = Mv["tab"][rp, 0, :], Mv["tab"][rp, 1, :]
                link(v.memset(Mv["bias"], 0.0))
                v.tensor_copy(Mv["bias"][:, 3 * P:T], cst("causal")).then_inc(S["m_bias"], 1)
                dve.wait_ge(S["m_bias"], reached("m_bias"))
                dve.wait_ge(S["m_in"], at(l, "m_in", 2))
                tt(Mv["sq"][:, 0:2, :], Mv["cq"], Mv["cq"], MUL)
                v.tensor_tensor(Mv["sq"][:, 2, :], misc[:, 0, :], misc[:, 0, :], MUL).then_inc(S["m_sq"], 1)
                dve.wait_ge(S["m_sq"], reached("m_sq"))
                merge(l)
                dve.wait_ge(v_full, filled.next())
                b = filled.bank()
                v.tensor_scalar(Mv["rs"][:, 0, :], b[:], 1.0 / 256, EPS, MUL, ADD).then_inc(S["m_nv"], 1)
                dve.wait_ge(S["m_nv"], reached("m_nv"))
                dve.wait_ge(v_full, filled.next())
                b = filled.bank()
                v.tensor_scalar(Mv["rs"][:, 1, :], b[:], 1.0 / 128, EPS, MUL, ADD).then_inc(S["m_nv"], 1)
                dve.wait_ge(S["m_nv"], reached("m_nv"))
                v.reciprocal(Mv["rs"], Mv["rs"]).then_inc(S["m_rec"], 1)
                dve.wait_ge(S["m_rec"], reached("m_rec"))
                dve.wait_ge(S["m_rs"], at(l, "m_rs", 1))
                for f in range(2):
                    stt(Mv["cq"][:, f, :], Mv["cq"][:, f, :], pr("q_g", f), Mv["rs"][:, 0, :], MUL, MUL)
                v.scalar_tensor_tensor(misc[:, 0, :], misc[:, 0, :], pr("kv_g", 0), Mv["rs"][:, 1, :], MUL, MUL).then_inc(S["m_c"], 1)
                dve.wait_ge(S["m_c"], reached("m_c"))
                merge(l)
                dve.wait_ge(v_full, filled.next())
                b = filled.bank()
                v.tensor_tensor(Mv["tmp"][rp, :], b[rp, :], sin, MUL).then_inc(S["m_krb"], 1)
                dve.wait_ge(S["m_krb"], reached("m_krb"))
                tt(Mv["kr"][rp, :], misc[rp, 1, :], cos, MUL)
                for h in range(H):
                    v.tensor_tensor(Mv["k"][rp, h, :], Mv["kr"][rp, :], Mv["tmp"][rp, :], ADD).then_inc(S["m_kr"], 1)
                    dve.wait_ge(S["m_kr"], reached("m_kr"))
                for h in range(H):
                    dve.wait_ge(v_full, filled.next())
                    b = filled.bank()
                    tt(Mv["tmp"][rp, :], b[rp, :], sin, MUL)
                    x_ = Mv["q"][rp, h, :]
                    tt(x_, x_, cos, MUL)
                    v.tensor_tensor(x_, x_, Mv["tmp"][rp, :], ADD).then_inc(S["m_rot"], 1)
                    dve.wait_ge(S["m_rot"], reached("m_rot"))
                merge(l)
                merge(l)
                attention(l, "m", Mv, 96 ** -0.5, lambda qt: Mv["bias"][:, (3 - qt) * P:T], 1)
                for _ in range(4):
                    merge(l)
                for m in range(KT):
                    dve.wait_ge(v_full, filled.next())
                    b = filled.bank()
                    v.tensor_tensor(xT[:, m, :], xT[:, m, :], b[:], ADD).then_inc(S["wo_done"], 1)
                    dve.wait_ge(S["wo_done"], reached("wo_done"))
                norm(2 * l + 1, "mlp_g")
                for i in range(32):
                    dve.wait_ge(S["up_relu"], at(l, "up_relu", i + 1))
                    v.tensor_tensor(up_act[:, i, :], up_act[:, i, :], up_act[:, i, :], MUL).then_inc(S["up_done"], 1)
                    dve.wait_ge(S["up_done"], reached("up_done"))
                for m in range(KT):
                    dve.wait_ge(v_full, filled.next())
                    b = filled.bank()
                    v.tensor_tensor(xT[:, m, :], xT[:, m, :], b[:], ADD).then_inc(S["down_done"], 1)
                    dve.wait_ge(S["down_done"], reached("down_done"))
            norm(2 * L, "fin_g")


def stream_layout(w):
    out = np.zeros((L * NU, P, SLOT), np.float32)
    w_outs = [w["w_out_gdn"], w["w_out_mla"], w["w_out_rwkv"], w["w_out_dsa"]]

    def tiles(a):
        return a.reshape(-1, P, a.shape[1]).transpose(1, 0, 2)

    for l in range(L):
        wi = w["w_in"][l]
        for u, unit in enumerate(UNITS):
            dst = out[l * NU + u].reshape(P, 10, UW)
            kind, i = unit[0], unit[-1]
            if kind == "rw":
                dst[:, 0:8] = tiles(wi[:, RWK0 + UW * i:RWK0 + UW * (i + 1)])
            elif kind == "gd":
                c = GDN0 + UW * i if i < 3 else GDN0 + 776
                dst[:, 0:8] = tiles(wi[:, c:c + UW])
            elif kind == "misc":
                parts = ((MLA0 + 256, 128), (MLA0 + 384, 32), (DSA0 + 512, 64), (GDN0 + 768, 8), (DSA0 + 576, 8))
                at = 0
                for c, n in parts:
                    dst[:, 0:8, at:at + n] = tiles(wi[:, c:c + n])
                    at += n
            elif kind == "ds":
                c = DSA0 + (UW * i if i < 2 else 584 + UW * (i - 2))
                dst[:, 0:8] = tiles(wi[:, c:c + UW])
            elif kind == "cq":
                dst[:, 0:8] = tiles(wi[:, MLA0:MLA0 + UW])
            elif kind == "merge":
                br = unit[1]
                c = GATE0 + D * br + UW * i
                dst[:, 0:8] = tiles(wi[:, c:c + UW])
                dst[:, 8:10] = tiles(w_outs[br][l][:, UW * i:UW * (i + 1)])
            elif kind == "wo":
                dst[:, 0:8] = tiles(w["w_o"][l][:, UW * i:UW * (i + 1)])
            elif kind == "up":
                dst[:, 0:8] = tiles(w["w_up"][l][:, UW * i:UW * (i + 1)])
            else:
                j, kb = unit[1], unit[2]
                dst[:, 0:8] = tiles(w["w_down"][l][D * kb:D * (kb + 1), UW * j:UW * (j + 1)])
    return out


def par_layout(w):
    out = np.zeros((L, P, NPAR), np.float32)

    def put(l, name, a):
        at, n = PAR[name]
        out[l, :, at:at + n] = a

    for l in range(L):
        col = lambda a: a.reshape(-1, P).T
        put(l, "mix_g", col(w["mix_norm_g"][l]))
        put(l, "mlp_g", col(w["mlp_norm_g"][l]))
        put(l, "fin_g", col(w["final_norm_g"]))
        put(l, "conv", w["gdn_conv_w"][l].reshape(4, 6, P).transpose(2, 1, 0).reshape(P, 24))
        put(l, "mu", col(w["rwkv_mu"][l]))
        for name, key in (("w0", "rwkv_w0"), ("a0", "rwkv_a0"), ("k_k", "rwkv_k_k"), ("k_a", "rwkv_k_a"),
                          ("ln_w", "rwkv_ln_w"), ("ln_b", "rwkv_ln_b"), ("q_g", "mla_q_norm_g"), ("kv_g", "mla_kv_norm_g")):
            put(l, name, col(w[key][l]))
        put(l, "r_k", col(w["rwkv_r_k"][l].reshape(-1)))
        put(l, "gdn_g", np.concatenate([w["gdn_norm_g"][l]] * 2)[:, None])
        put(l, "a_log", np.broadcast_to(w["gdn_a_log"][l], (P, H)))
        put(l, "dt", np.broadcast_to(w["gdn_dt_bias"][l], (P, H)))
        put(l, "wa2", np.concatenate([w["rwkv_w_w2"][l], w["rwkv_w_a2"][l]]))
        put(l, "g2", w["rwkv_w_g2"][l])
        put(l, "uq", w["mla_w_uq"][l].reshape(2, P, 384).transpose(1, 0, 2).reshape(P, 768))
        put(l, "ukv", w["mla_w_ukv"][l])
    return out


def kernel(**inputs):
    import concourse.bacc as bacc
    from concourse.bass_utils import run_bass_kernel_spmd as run

    w = {k: np.asarray(a) for k, a in inputs.items()}
    arrays = {
        "in_x": np.ascontiguousarray(w["x"][0]),
        "in_pos": np.ascontiguousarray(w["positions"][0]),
        "in_w": stream_layout(w),
        "in_par": par_layout(w),
        "in_const": CONST_ARRAY,
    }
    nc = bacc.Bacc("TRN2", target_bir_lowering=False, num_devices=1)
    aps = [nc.dram_tensor(n, a.shape, mybir.dt.from_np(a.dtype), kind="ExternalInput").ap() for n, a in arrays.items()]
    tabs = nc.dram_tensor("tabs", (2, 2, P, T), F32, kind="Internal").ap()
    out = nc.dram_tensor("out_x", (T, D), F32, kind="ExternalOutput").ap()
    build(nc, *aps, tabs, out)
    r = run(nc, [arrays], core_ids=[0])
    return r.results[0]["out_x"].reshape(1, T, D)
```

```python
from contextlib import ExitStack

import numpy as np

import concourse.bass as bass
from concourse import mybir

ALU = mybir.AluOpType
ACT = mybir.ActivationFunctionType
F32 = mybir.dt.float32
F32R = mybir.dt.float32r
I32 = mybir.dt.int32
AX_X = mybir.AxisListType.X

P = 128
T = 512
D = 1024
L = 2
KT = D // P
TT = T // P
C = 64
NC = T // C
H = 4
M = TT * H
FF = 4096
EPS = 1e-6
GN_EPS = 64e-5
TOPK = 128
NEG = -1e30
DECAY = float(np.exp(-0.5))
MAGIC = 12582912.0
TWO_PI = (6.28125, 0.0019350051879882812, 3.0199159819e-07)
LEVELS = (2, 4, 8, 16, 32)

GDN0, MLA0, RWK0, DSA0, GATE0 = 0, 1032, 1448, 2472, 3824

SLOT = 10 * P
RING = 3
SPLIT = 2
QUARTERS = 4


def unit_list():
    u = [("rw", i) for i in range(8)] + [("misc", i) for i in range(2)]
    u += [("gd", i) for i in range(8)]
    u += [("merge", 2, i) for i in range(8)]
    u += [("ds", i) for i in range(10)]
    u += [("merge", 0, i) for i in range(8)]
    u += [("cq", i) for i in range(2)]
    u += [("merge", 3, i) for i in range(8)]
    u += [("merge", 1, i) for i in range(8)]
    u += [("wo", i) for i in range(8)]
    for q in range(QUARTERS + 1):
        if q < QUARTERS:
            u += [("up", 8 * q + i) for i in range(8)]
        if q >= 1:
            u += [("down", q - 1, i) for i in range(8)]
    return u


UNITS = unit_list()
NU = len(UNITS)

CONST = {}


def _constants():
    n = np.arange(P)
    blk = n[:, None] // C == n[None, :] // C
    parts = [
        ("ident", np.eye(P)),
        ("ones", np.ones((P, P))),
        ("blocks", blk),
        ("upto", blk & (n[:, None] <= n[None, :])),
        ("before", blk & (n[:, None] < n[None, :])),
        ("after", blk & (n[:, None] > n[None, :])),
    ]
    i, j = n[:, None], n[None, :]
    level = lambda s: (i // (2 * s) == j // (2 * s)) & (i % (2 * s) >= s) & (j % (2 * s) < s)
    parts.append(("first", -1.0 * level(1).T))
    for s in LEVELS:
        parts.append((f"level{s}", level(s)))
    parts.append(("causal", np.where(n[None, :] <= n[:, None], 0.0, NEG)))

    def rotate(dims, start, width):
        r = np.zeros((P, P))
        for b in range(start, P, width):
            for e in range(dims // 2):
                if b + dims <= P:
                    r[b + dims // 2 + e, b + e] = -1.0
                    r[b + e, b + dims // 2 + e] = 1.0
        return r

    rot_m = np.zeros((P, P))
    rot_m[64:96, 64:96] = rotate(32, 0, P)[:32, :32]
    rot_d = rotate(16, 0, C)
    dup = np.zeros((P, P))
    dup[:C, :] = (np.arange(C)[:, None] == (n % C)[None, :])
    parts += [("rot_m", rot_m), ("rot_d", rot_d), ("dup", dup), ("dup_rot", dup @ rot_d)]
    fm = np.zeros(P, np.float32)
    inv_m = (np.float32(500000.0) ** (-np.arange(0, 32, 2, dtype=np.float32) / np.float32(32))).astype(np.float32)
    fm[64:80] = inv_m
    fm[80:96] = inv_m
    fd = np.zeros(P, np.float32)
    inv_d = (np.float32(500000.0) ** (-np.arange(0, 16, 2, dtype=np.float32) / np.float32(16))).astype(np.float32)
    for b in (0, C):
        fd[b:b + 8] = inv_d
        fd[b + 8:b + 16] = inv_d
    parts += [("freq_d", fd[:, None]), ("freq_m", fm[:, None])]
    at, cols = 0, []
    for name, a in parts:
        a = np.asarray(a, np.float32)
        CONST[name] = (at, a.shape[1])
        at += a.shape[1]
        cols.append(a)
    return np.ascontiguousarray(np.concatenate(cols, axis=1))


CONST_ARRAY = _constants()
NCONST = CONST_ARRAY.shape[1]

PAR = {}
_at = 0
for _n, _w in (("mix_g", 8), ("mlp_g", 8), ("fin_g", 8), ("conv", 24), ("mu", 8), ("w0", 2), ("a0", 2), ("k_k", 2),
               ("k_a", 2), ("r_k", 2), ("ln_w", 2), ("ln_b", 2), ("gdn_g", 1), ("q_g", 2), ("kv_g", 1),
               ("a_log", 4), ("dt", 4), ("wa2", 256), ("g2", 256), ("uq", 768), ("ukv", 512)):
    PAR[_n] = (_at, _w)
    _at += _w
NPAR = _at


def build(nc, x_in, pos_in, wstream, par_in, const_in, tabs, x_dram, out):
    ctx = ExitStack()
    with ctx:
        def sb(name, shape, dt=F32):
            return ctx.enter_context(nc.sbuf_tensor(name, shape, dt))

        def sem(name):
            return ctx.enter_context(nc.semaphore(name))

        h_hi = sb("h_hi", [P, KT, T], F32R)
        h_lo = sb("h_lo", [P, KT, T], F32R)
        mg = sb("mg", [P, KT, T])
        ring = sb("ring", [P, RING, SLOT])
        w_hi = sb("w_hi", [P, SPLIT, KT, P], F32R)
        w_lo = sb("w_lo", [P, SPLIT, KT, P], F32R)
        consts = sb("consts", [P, NCONST])
        par = sb("par", [P, NPAR])
        yo = sb("yo", [P, 2, 2, T])
        misc = sb("misc", [P, 2, T])
        sg = sb("sg", [P, 2, T])
        s_z = sb("s_z", [P, 2, 2, C])
        un_z = sb("un_z", [P, 2, 4 * C])
        pc = sb("pc", [P, 2, NC])
        ab = sb("ab", [P, TT, 16])
        gsm = sb("gsm", [P, 6, M])
        m8 = sb("m8", [P, 8])
        sml = sb("sml", [P, 16])
        AQ = 45
        with nc.sbuf_tensor("arena", [P, AQ * T], F32) as arena:
            pass
        parts = sb("parts", [P, 4, KT, T], F32R)

        def ar(q, shape, at=0):
            n = int(np.prod(shape))
            v = arena[:, q * T + at:q * T + at + n]
            if len(shape) == 1:
                return v
            names = " ".join("abcd"[:len(shape)])
            return v.rearrange(f"p ({names}) -> p {names}", **{k: s for k, s in zip("abcd", shape)})

        xT = ar(AQ - KT, (KT, T))

        def cst(name):
            a, w = CONST[name]
            return consts[:, a:a + w]

        def pr(name, i=None):
            a, w = PAR[name]
            return par[:, a:a + w] if i is None else par[:, a + i:a + i + 1]

        bank_a = [ctx.enter_context(nc.psum_tensor(f"bank_a{i}", [P, T], F32)) for i in range(4)]
        bank_v = [ctx.enter_context(nc.psum_tensor(f"bank_v{i}", [P, T], F32)) for i in range(4)]

        S, per = {}, {}

        def ev(name, n):
            S[name] = sem(name)
            per[name] = n

        a_full = sem("a_full")
        v_full = sem("v_full")
        w_here = [sem(f"w_here{i}") for i in range(RING)]
        wout_used = sem("wout_used")
        x_away = sem("x_away")
        x_back = sem("x_back")
        const_here = sem("const_here")
        par_here = sem("par_here")
        x_here = sem("x_here")
        pos_here = sem("pos_here")
        tab_out = sem("tab_out")
        tab_d_here = sem("tab_d_here")
        tab_m_here = sem("tab_m_here")
        out_done = sem("out_done")
        dve_step = sem("dve_step")
        act_step = sem("act_step")
        for name, n in (
            ("split_hi", NU), ("split_lo", NU),
            ("n_sq", 16), ("n_var", 2), ("n_rec", 2), ("n_rs", 2), ("n_g", 16), ("n_hi", 16), ("n_h", 16),
            ("x_t", 0), ("o_tok", 0), ("tab", 0), ("tab_sin", 0), ("tab_arg", 0), ("init", 0),
            ("r_in", 8), ("r_zero", 1), ("r_mix", 8), ("r_act", 2), ("r_lora", 6), ("r_cum", 1), ("r_dec", 3),
            ("r_ex", 1), ("r_sq", 1), ("r_l2", 2), ("r_l2r", 1), ("r_l2s", 1), ("r_bsq", 2), ("r_bon", 2), ("r_feat", 4),
            ("r_tok", 8), ("r_mat", 16), ("r_x1", TT), ("r_ti", TT), ("r_y", 5 * TT), ("r_t", 4 * TT), ("r_x", 5 * TT),
            ("r_wt", 2), ("r_y1", TT), ("r_u", TT), ("r_ws", NC), ("r_s", NC), ("r_o", NC),
            ("r_mean", 2), ("r_sq2", 1), ("r_gv", 2), ("r_gr", 1), ("r_gs", 1), ("r_out", 1),
            ("g_pad", 1), ("g_in", 6), ("g_z", 2), ("g_conv", 6), ("g_sig", 1), ("g_silu", 1), ("g_sq", 1), ("g_l2", 4),
            ("g_l2r", 1), ("g_l2s", 1), ("g_qk", 1), ("g_t1", 1), ("g_t2", 1), ("g_g", 2), ("g_feat", 6), ("g_gc", 1),
            ("g_row", 4), ("g_d", 4), ("g_dm", 4), ("g_prep", 2),
            ("g_tok", 6), ("g_mat", 8), ("g_x1", TT), ("g_ti", TT), ("g_y", 5 * TT), ("g_t", 4 * TT), ("g_x", 5 * TT),
            ("g_wt", 2), ("g_u", TT), ("g_ws", NC), ("g_s", NC), ("g_o", NC),
            ("g_sq2", 1), ("g_gv", 2), ("g_gr", 1), ("g_gs", 1), ("g_out", 1),
            ("misc_in", 2), ("ab_in", 1),
            ("d_in", 8), ("d_vf", 2), ("d_v", 2), ("d_ik", 2), ("d_rot", 8), ("d_sc", 24), ("d_acc", 24), ("d_bias", 4),
            ("d_ss", 16), ("d_p", 16), ("d_pn", 16), ("d_pt", 16), ("d_o", 16), ("d_kz", 2),
            ("m_in", 2), ("m_sq", 1), ("m_nv", 2), ("m_rec", 1), ("m_rs", 1), ("m_c", 1), ("m_q", 4), ("m_k", 4), ("m_v", 2),
            ("m_rot", 4), ("m_kr", 4), ("m_krb", 1),
            ("m_bias", 1),
            ("m_ss", 16), ("m_p", 16), ("m_pn", 16), ("m_pt", 16), ("m_o", 16),
            ("mg_sig", 32), ("mg_done", 32), ("mg_hi", 8), ("mg_lo", 8), ("wo_done", 8), ("up_relu", 32), ("up_sq", 32), ("up_hi", 32), ("up_done", 32), ("g_zs", 1), ("r_s0", 1), ("g_s0", 1), ("down_done", 8 * QUARTERS),
        ):
            ev(name, n)

        def at(l, name, k):
            return l * per[name] + k

        class Banks:

            def __init__(self):
                self.used = {"a": 0, "v": 0}
                self.reader = {"a": [(const_here, 16)] * 4, "v": [(const_here, 16)] * 4}
                self.counts = {}

            def next(self, pool, done):
                i = self.used[pool] % 4
                self.used[pool] += 1
                sem_, value = self.reader[pool][i]
                self.counts[done] = self.counts.get(done, 0) + 1
                self.reader[pool][i] = (S[done], self.counts[done])
                return (bank_a if pool == "a" else bank_v)[i], sem_, value

        class Filled:

            def __init__(self, banks):
                self.n, self.banks = 0, banks

            def next(self):
                self.n += 1
                return self.n

            def bank(self):
                return self.banks[(self.n - 1) % 4]

        def own_half(view, parts, i):
            return view.rearrange("p (f x c) -> p f x c", f=2, x=parts)[:, :, i, :]

        def merges_to(g):
            return sum(UNITS[i % NU][0] == "merge" for i in range(g))

        block = ctx.enter_context(nc.Block())

        R = dict(
            rw=ar(0, (8, T + 1)), rm=ar(9, (8, T)), sw=ar(0, (2, T)), a=ar(2, (2, T)), g=ar(4, (2, T)), cs=ar(6, (2, T)),
            p=ar(17, (2, T)), pi=ar(19, (2, T)), pe=ar(21, (2, T)), kk=ar(23, (2, T)), tmp=ar(25, (2, T)),
            rt=ar(27, (2, T)), et=ar(29, (2, T)), bz=ar(31, (2, 2, T)), kz=ar(35, (2, 2, T)),
            bh=ar(39, (2, T)), kh=ar(41, (2, T)), bon=ar(43, (2, T)),
            e_tok=ar(17, (TT, 256)), v_tok=ar(19, (TT, 256)), b_tok=ar(21, (TT, 256)), k_tokz=ar(23, (TT, 2, 256)),
            u=ar(9, (M, P)), ark=ar(0, (2 * M, C)), akk=ar(39, (M, P)),
            x_bd=ar(31, (M, P)), y_bd=ar(35, (M, P)), t_bd=ar(13, (M, P)),
            wt=ar(29, (2, T)), y1=ar(15, (TT, 256)), up=ar(6, (TT, 256)), o=ar(9, (2, T)), sq=ar(11, (2, T)),
        )
        R["arb"] = mg[:, 0:4, :].rearrange("p a (b c) -> p (a b) c", c=P)
        R["ark"] = ar(0, (M, P))
        G = dict(
            ci=ar(0, (6, T + 3)), co=ar(7, (6, T)), z=ar(13, (2, T)), sig=ar(15, (6, T)), sq=ar(0, (4, T)), rs=ar(15, (4, T)),
            egc=ar(15, (2, T)), ers=ar(17, (2, T)), beta=ar(19, (2, T)), kb=ar(0, (2, T)), rt=ar(2, (2, T)), et=ar(4, (2, T)),
            bh=ar(21, (2, T)), vb=ar(23, (2, T)), kz=ar(25, (2, 2, T)), d=ar(29, (M, P)), u=ar(33, (M, P)), arb=ar(37, (M, P)),
            e_tok=ar(41, (TT, 256)), v_tok=ar(43, (TT, 256)), b_tok=ar(17, (TT, 256)),
            x_bd=ar(25, (M, P)), y_bd=ar(29, (M, P)), t_bd=ar(7, (M, P)),
            wt=ar(0, (2, T)), up=ar(4, (TT, 256)), o=ar(7, (2, T)), sq2=ar(9, (2, T)),
            g_wide=ar(41, (M * C,)), b_wide=ar(43, (M * C,)),
        )
        Dv = dict(
            iq=ar(0, (4, T)), q=ar(4, (2, T)), k=ar(6, (2, T)), v=ar(8, (TT, 256)), tab=ar(10, (2, T)),
            ikz=ar(12, (2, T)), kz=ar(14, (2, 2, T)), tmp=ar(18, (T,)), rl=ar(19, (2, T)), sc=ar(21, (T,)), wk=ar(22, (T,)),
            vf=ar(34, (2, T)), gt=ar(23, (T,)), eq=ar(24, (T,)), cum=ar(25, (T,)), bias=ar(26, (TT, T)),
            ss=ar(30, (2, T)), pt=ar(32, (2, TT, P)),
        )
        Mv = dict(
            cq=ar(0, (2, T)), sq=ar(2, (3, T)), rs=ar(5, (2, T)), q=ar(7, (4, T)), k=ar(11, (4, T)), v=ar(15, (TT, 256)),
            tab=ar(17, (2, T)), tmp=ar(19, (T,)), bias=ar(20, (T,)), kr=ar(21, (T,)),
            ss=ar(30, (2, T)), pt=ar(32, (2, TT, P)),
        )
        xin = ar(0, (TT, D))
        xout = ar(0, (TT, D))
        mg_hi, mg_lo = parts[:, 0], parts[:, 1]
        up_hi = [parts[:, 0], parts[:, 2]]
        up_lo = [parts[:, 1], parts[:, 3]]
        relu = ar(32, (2, T))
        relu2 = ar(34, (2, T))
        squares = [ar(8, (KT, T)), ar(16, (KT, T))]
        POS = dict(i=ar(20, (T,)).bitcast(I32), f=ar(21, (T,)), ang=ar(22, (T,)), k=ar(23, (T,)), sin=ar(24, (2, T)), cos=ar(26, (2, T)),
                   red=ar(28, (2, T)))
        rotors = ("d", "m")

        @block.sync
        def _(sp):
            sp.dma_start(xin, x_in.rearrange("(t p) d -> p t d", p=P)).then_inc(x_here, 16)
            sp.dma_start(consts[:], const_in).then_inc(const_here, 16)
            sp.dma_start(POS["i"], pos_in.partition_broadcast(P)).then_inc(pos_here, 16)
            for g in range(L * NU):
                l, u = divmod(g, NU)
                if g >= RING:
                    sp.wait_ge(S["split_lo"], g - RING + 1)
                    if UNITS[(g - RING) % NU][0] == "merge":
                        sp.wait_ge(wout_used, merges_to(g - RING + 1))
                kts = 10 if UNITS[u][0] == "merge" else 8
                sp.dma_start(ring[:, g % RING, 0:kts * P], wstream[g, :, 0:kts * P]).then_inc(w_here[g % RING], 16)
                if UNITS[u] == ("rw", 4):
                    if l == 0:
                        sp.wait_ge(S["x_t"], 8)
                    else:
                        sp.wait_ge(S["down_done"], at(l - 1, "down_done", 8 * QUARTERS))
                    sp.dma_start(x_dram, xT).then_inc(x_away, 16)
                if UNITS[u] == ("cq", 0):
                    sp.wait_ge(S["g_out"], at(l, "g_out", 1))
                    sp.wait_ge(x_away, 16 * (l + 1))
                    sp.dma_start(xT, x_dram).then_inc(x_back, 16)
            sp.wait_ge(S["o_tok"], 8)
            sp.dma_start(out.rearrange("(t p) d -> p t d", p=P), xout).then_inc(out_done, 16)
            sp.wait_ge(out_done, 16)

        @block.gpsimd
        def _(pool):
            pool.dma_start(par[:], par_in[0]).then_inc(par_here, 16)
            for g in range(L * NU):
                l, u = divmod(g, NU)
                pool.wait_ge(S["split_hi"], g + 1)
                for half in range(2):
                    ks = slice(4 * half, 4 * half + 4)
                    raw = ring[:, g % RING, 4 * half * P:4 * (half + 1) * P].rearrange("p (k n) -> p k n", n=P)
                    ins = nc.gpsimd.tensor_tensor(w_lo[:, g % SPLIT, ks, :], raw, w_hi[:, g % SPLIT, ks, :].bitcast(F32), ALU.subtract)
                ins.then_inc(S["split_lo"], 1)
                if g == 1:
                    for i in range(2):
                        pool.wait_ge(S["tab"], i + 1)
                        pool.dma_start(tabs[i, 0], POS["cos"][:, i, :]).then_inc(tab_out, 16)
                        pool.dma_start(tabs[i, 1], POS["sin"][:, i, :]).then_inc(tab_out, 16)
                if UNITS[u] == ("ds", 0):
                    pool.wait_ge(tab_out, 64)
                    pool.wait_ge(S["g_out"], at(l, "g_out", 1))
                    pool.dma_start(Dv["tab"], tabs[0].rearrange("k p t -> p k t")).then_inc(tab_d_here, 16)
                if UNITS[u] == ("cq", 0):
                    pool.wait_ge(S["d_o"], at(l, "d_o", 16))
                    pool.dma_start(Mv["tab"], tabs[1].rearrange("k p t -> p k t")).then_inc(tab_m_here, 16)
                if UNITS[u] == ("up", 2) and l + 1 < L:
                    pool.wait_ge(S["n_g"], at(l, "n_g", 16))
                    pool.dma_start(par[:], par_in[l + 1]).then_inc(par_here, 16)

        @block.tensor
        def _(pe):
            mm = nc.tensor.matmul
            banks = Banks()
            unit = [0]

            def begin_unit(want, l):
                g = unit[0]
                assert UNITS[g % NU] == want and g // NU == l, (UNITS[g % NU], want)
                unit[0] += 1
                pe.wait_ge(S["split_hi"], g + 1)
                return g

            def split_product(g, b, hi, lo, sem_name=None, k0=0):
                s = g % SPLIT
                for k in range(KT):
                    if sem_name:
                        pe.wait_ge(S[sem_name], k0 + k + 1)
                    mm(b[:], w_hi[:, s, k, :], hi[:, k, :], start=k == 0, stop=False)
                    mm(b[:], w_hi[:, s, k, :], lo[:, k, :], start=False, stop=False)
                pe.wait_ge(S["split_lo"], g + 1)
                for k in range(KT):
                    ins = mm(b[:], w_lo[:, s, k, :], hi[:, k, :], start=False, stop=k == KT - 1)
                return ins

            def feat_group(want, l, hi, lo, pool, done, sem_name=None, k0=0):
                g = begin_unit(want, l)
                b, reader, emptied = banks.next(pool, done)
                pe.wait_ge(reader, emptied)
                split_product(g, b, hi, lo, sem_name, k0).then_inc(a_full if pool == "a" else v_full, 1)

            def norm_sum(n):
                b, reader, emptied = banks.next("v", "n_var")
                pe.wait_ge(reader, emptied)
                for k in range(KT):
                    pe.wait_ge(S["n_sq"], n * KT + k + 1)
                    ins = mm(b[:], cst("ones"), squares[n % 2][:, k, :], start=k == 0, stop=k == KT - 1)
                ins.then_inc(v_full, 1)

            def merge(l, br, slot, i):
                for j in range(2):
                    g = begin_unit(("merge", br, 2 * i + j), l)
                    b, reader, emptied = banks.next("v", "mg_done")
                    pe.wait_ge(reader, emptied)
                    for k in range(2):
                        ins = mm(b[:], ring[:, g % RING, (KT + k) * P:(KT + k + 1) * P], yo[:, slot, k, :], start=k == 0, stop=k == 1)
                    ins.then_inc(v_full, 1)
                    b, reader, emptied = banks.next("a", "mg_sig")
                    pe.wait_ge(reader, emptied)
                    for k in range(KT):
                        ins = mm(b[:], w_hi[:, g % SPLIT, k, :], h_hi[:, k, :], start=k == 0, stop=False)
                        if k == 0:
                            ins.then_inc(wout_used, 1)
                        mm(b[:], w_hi[:, g % SPLIT, k, :], h_lo[:, k, :], start=False, stop=False)
                    pe.wait_ge(S["split_lo"], g + 1)
                    for k in range(KT):
                        ins = mm(b[:], w_lo[:, g % SPLIT, k, :], h_hi[:, k, :], start=False, stop=k == KT - 1)
                    ins.then_inc(a_full, 1)

            def transposes(srcs, x):
                for s in srcs:
                    for half in range(2):
                        b, reader, emptied = banks.next("a", x + "_tok")
                        pe.wait_ge(reader, emptied)
                        for t2 in range(2):
                            for f in range(2):
                                c = t2 * 256 + f * P
                                t = 2 * half + t2
                                ins = nc.tensor.transpose(b[:, c:c + P], s[:, f, t * P:(t + 1) * P], cst("ident"))
                        ins.then_inc(a_full, 1)

            def pair_matrices(lz, rhs, x):
                for t in range(TT):
                    b, reader, emptied = banks.next("v", x + "_mat")
                    pe.wait_ge(reader, emptied)
                    for h in range(H):
                        ins = mm(b[:, h * P:(h + 1) * P], lz[:, h // 2, h % 2, t * P:(t + 1) * P],
                                 rhs[:, h // 2, t * P:(t + 1) * P], start=True, stop=True)
                    ins.then_inc(v_full, 1)

            def block_products(pool, done, t, lhs, rhs):
                b, reader, emptied = banks.next(pool, done)
                pe.wait_ge(reader, emptied)
                for h in range(H):
                    m = t * H + h
                    ins = mm(b[:, h * P:(h + 1) * P], lhs[:, m, :], rhs(m), start=True, stop=True)
                ins.then_inc(v_full if pool == "v" else a_full, 1)

            def of_pair(src):
                return lambda m: src[:, m // H, (m % H) // 2 * P:((m % H) // 2 + 1) * P]

            def invert(l, x, V, fill):
                for t in range(TT):
                    b, reader, emptied = banks.next("a", x + "_ti")
                    pe.wait_ge(reader, emptied)
                    pe.wait_ge(S[x + "_x1"], at(l, x + "_x1", t + 1))
                    for h in range(H):
                        ins = nc.tensor.transpose(b[:, h * P:(h + 1) * P], V["x_bd"][:, t * H + h, :], cst("ident"))
                    ins.then_inc(a_full, 1)
                for n in range(len(LEVELS)):
                    for t in range(TT):
                        if n:
                            pe.wait_ge(S[x + "_t"], at(l, x + "_t", TT * (n - 1) + t + 1))
                        else:
                            pe.wait_ge(S[x + "_ti"], at(l, x + "_ti", t + 1))
                        block_products("v", x + "_y", t, V["u"], lambda m: V["t_bd"][:, m, :])
                    for t in range(TT):
                        pe.wait_ge(S[x + "_y"], at(l, x + "_y", TT * n + t + 1))
                        if n:
                            pe.wait_ge(S[x + "_x"], at(l, x + "_x", TT * (n - 1) + t + 1))
                        if n < len(LEVELS) - 1:
                            block_products("v", x + "_t", t, V["x_bd"], lambda m: V["y_bd"][:, m, :])
                    for t in range(TT):
                        block_products("v", x + "_x", t, V["y_bd"], lambda m: V["x_bd"][:, m, :])
                    fill(n)

            def through(l, x, V, rhs):
                pe.wait_ge(S[x + "_x"], at(l, x + "_x", TT * len(LEVELS)))
                for f in range(2):
                    b, reader, emptied = banks.next("a", x + "_wt")
                    pe.wait_ge(reader, emptied)
                    for t in range(TT):
                        for hp in range(2):
                            h = 2 * f + hp
                            ins = mm(b[hp * C:(hp + 1) * C, t * P:(t + 1) * P], V["e_tok"][:, t, h * C:(h + 1) * C],
                                     V["x_bd"][:, t * H + h, :], start=True, stop=True)
                    ins.then_inc(a_full, 1)
                for t in range(TT):
                    block_products("a", x + "_u", t, V["x_bd"], of_pair(rhs))

            def scan(l, x, V, fill):
                pe.wait_ge(S[x + "_s0"], at(l, x + "_s0", 1))
                pe.wait_ge(S[x + "_wt"], at(l, x + "_wt", 2))
                for c in range(NC):
                    t, par_ = divmod(c, 2)
                    rows = slice(par_ * C, (par_ + 1) * C)
                    if c:
                        pe.wait_ge(S[x + "_s"], at(l, x + "_s", c))
                    b, reader, emptied = banks.next("v", x + "_ws")
                    pe.wait_ge(reader, emptied)
                    for f in range(2):
                        ins = mm(b[rows, f * P:(f + 1) * P], V["wt"][:, f, c * C:(c + 1) * C],
                                 s_z[:, f, :, :], start=True, stop=True)
                    ins.then_inc(v_full, 1)
                    bo, reader, emptied = banks.next("a", x + "_o")
                    pe.wait_ge(reader, emptied)
                    bs, reader, emptied = banks.next("v", x + "_s")
                    pe.wait_ge(reader, emptied)
                    pe.wait_ge(S[x + "_ws"], at(l, x + "_ws", c + 1))
                    for h in range(H):
                        f, hp = divmod(h, 2)
                        dst = bo[hp * C:(hp + 1) * C, f * C:(f + 1) * C]
                        hc = slice(h * C, (h + 1) * C)
                        mm(dst, s_z[:, f, hp, :], V["rt"][:, f, c * C:(c + 1) * C], start=True, stop=False)
                        if "ark" in V:
                            mm(dst, V["v_tok"][:, t, hc], V["ark"][:, t * H + h, rows], start=False, stop=False)
                        ins = mm(dst, un_z[:, par_, hc], V["arb"][:, t * H + h, rows], start=False, stop=True)
                    ins.then_inc(a_full, 1)
                    for h in range(H):
                        f, hp = divmod(h, 2)
                        dst = bs[hp * C:(hp + 1) * C, f * C:(f + 1) * C]
                        hc = slice(h * C, (h + 1) * C)
                        if "ark" in V:
                            mm(dst, V["k_tokz"][:, t, par_, hc], V["v_tok"][:, t, hc], start=True, stop=False)
                        ins = mm(dst, V["b_tok"][:, t, hc], un_z[:, par_, hc], start="ark" not in V, stop=True)
                    ins.then_inc(v_full, 1)
                    if c in (1, 4):
                        fill()

            def block_sums(l, need, k, src, tiles, done):
                pe.wait_ge(S[need], at(l, need, k))
                for i in range(tiles):
                    b, reader, emptied = banks.next("v", done)
                    pe.wait_ge(reader, emptied)
                    mm(b[:], cst("blocks"), src[:, i, :], start=True, stop=True).then_inc(v_full, 1)

            def attention(l, x, q_of, k_of, v, scores_need):
                steps = [(qt, h) for qt in range(TT) for h in range(H)]
                for i in range(len(steps) + 2):
                    if i < len(steps):
                        qt, h = steps[i]
                        b, reader, emptied = banks.next("v", x + "_ss")
                        pe.wait_ge(reader, emptied)
                        scores_need(qt)
                        mm(b[:, 0:(qt + 1) * P], q_of(h, qt), k_of(h, (qt + 1) * P), start=True, stop=True).then_inc(v_full, 1)
                    if 1 <= i <= len(steps):
                        qt, h = steps[i - 1]
                        b, reader, emptied = banks.next("a", x + "_pt")
                        pe.wait_ge(reader, emptied)
                        pe.wait_ge(S[x + "_pn"], at(l, x + "_pn", i))
                        for k in range(qt + 1):
                            ins = nc.tensor.transpose(b[:, k * P:(k + 1) * P], V_ss(x)[:, (i - 1) % 2, k * P:(k + 1) * P], cst("ident"))
                        ins.then_inc(a_full, 1)
                    if i >= 2:
                        qt, h = steps[i - 2]
                        b, reader, emptied = banks.next("v", x + "_o")
                        pe.wait_ge(reader, emptied)
                        pe.wait_ge(S[x + "_pt"], at(l, x + "_pt", i - 1))
                        rows = slice((h % 2) * C, (h % 2 + 1) * C)
                        for k in range(qt + 1):
                            ins = mm(b[rows, 0:P], v[:, k, h * C:(h + 1) * C], V_pt(x)[:, (i - 2) % 2, k, :],
                                     start=k == 0, stop=k == qt)
                        ins.then_inc(v_full, 1)

            def V_ss(x):
                return (Dv if x == "d" else Mv)["ss"]

            def V_pt(x):
                return (Dv if x == "d" else Mv)["pt"]

            pe.wait_ge(x_here, 16)
            pe.wait_ge(const_here, 16)
            for k in range(KT):
                b, reader, emptied = banks.next("v", "x_t")
                pe.wait_ge(reader, emptied)
                for t in range(TT):
                    ins = nc.tensor.transpose(b[:, t * P:(t + 1) * P], xin[:, t, k * P:(k + 1) * P], cst("ident"))
                ins.then_inc(v_full, 1)

            for l in range(L):
                norm_sum(2 * l)
                for i in range(8):
                    if i == 0:
                        feat_group(("rw", i), l, h_hi, h_lo, "a", "r_in", "n_h", at(l, "n_h", 0))
                    else:
                        feat_group(("rw", i), l, h_hi, h_lo, "a", "r_in")
                for i in range(2):
                    feat_group(("misc", i), l, h_hi, h_lo, "a", "misc_in")
                b, reader, emptied = banks.next("a", "ab_in")
                pe.wait_ge(reader, emptied)
                pe.wait_ge(S["misc_in"], at(l, "misc_in", 2))
                for t in range(TT):
                    ins = nc.tensor.transpose(b[:, t * P:(t + 1) * P], misc[:, 1, t * P:(t + 1) * P], cst("ident"))
                ins.then_inc(a_full, 1)
                pe.wait_ge(S["r_act"], at(l, "r_act", 2))
                for f in range(2):
                    b, reader, emptied = banks.next("a", "r_lora")
                    pe.wait_ge(reader, emptied)
                    mm(b[:], pr("wa2")[0:64, f * P:(f + 1) * P], R["rm"][0:64, 6, :], start=True, stop=True).then_inc(a_full, 1)
                for f in range(2):
                    b, reader, emptied = banks.next("a", "r_lora")
                    pe.wait_ge(reader, emptied)
                    mm(b[:], pr("wa2")[64:128, f * P:(f + 1) * P], R["rm"][64:128, 6, :], start=True, stop=True).then_inc(a_full, 1)
                for f in range(2):
                    b, reader, emptied = banks.next("a", "r_lora")
                    pe.wait_ge(reader, emptied)
                    mm(b[:], pr("g2")[:, f * P:(f + 1) * P], R["rm"][:, 7, :], start=True, stop=True).then_inc(a_full, 1)
                block_sums(l, "r_sq", 1, R["tmp"], 2, "r_l2")
                block_sums(l, "r_bsq", 2, R["tmp"], 2, "r_bon")
                pe.wait_ge(S["r_feat"], at(l, "r_feat", 4))
                transposes((R["et"], R["rm"][:, 4:6, :], R["bh"], R["kh"]), "r")
                pair_matrices(R["bz"], R["et"], "r")
                pair_matrices(R["kz"], R["et"], "r")
                pair_matrices(R["kz"], R["rt"], "r")
                pair_matrices(R["bz"], R["rt"], "r")
                invert(l, "r", R, lambda n: None)
                pe.wait_ge(S["r_tok"], at(l, "r_tok", 8))
                for t in range(TT):
                    block_products("v", "r_y1", t, R["akk"], of_pair(R["v_tok"]))
                pe.wait_ge(S["r_y1"], at(l, "r_y1", TT))
                through(l, "r", R, R["y1"])
                scan(l, "r", R, lambda: None)
                block_sums(l, "r_o", NC, R["o"], 2, "r_mean")
                block_sums(l, "r_sq2", 1, R["sq"], 2, "r_gv")

                pe.wait_ge(S["r_out"], at(l, "r_out", 1))
                for i in range(8):
                    feat_group(("gd", i), l, h_hi, h_lo, "a", "g_in" if i < 6 else "g_z")
                todo = list(range(4))

                def fill_r():
                    if todo:
                        merge(l, 2, 0, todo.pop(0))

                block_sums(l, "g_sq", 1, G["sq"], 4, "g_l2")
                fill_r()
                pe.wait_ge(S["g_g"], at(l, "g_g", 2))
                for src, rhs in (("g", "upto"), ("g", "after"), ("b", "ident")):
                    for f in range(2):
                        b, reader, emptied = banks.next("a", "g_feat")
                        pe.wait_ge(reader, emptied)
                        for t in range(TT):
                            m = t * H + 2 * f
                            wide = G["g_wide" if src == "g" else "b_wide"][:, m * C:(m + 2) * C]
                            ins = mm(b[:, t * P:(t + 1) * P], wide, cst(rhs), start=True, stop=True)
                        ins.then_inc(a_full, 1)
                b, reader, emptied = banks.next("v", "g_gc")
                pe.wait_ge(reader, emptied)
                mm(b[:, 0:M], cst("upto"), gsm[:, 4, :], start=True, stop=True).then_inc(v_full, 1)
                for t in range(TT):
                    b, reader, emptied = banks.next("v", "g_row")
                    pe.wait_ge(reader, emptied)
                    for h in range(H):
                        ins = mm(b[:, h * P:(h + 1) * P], gsm[:, 4, t * H + h:t * H + h + 1].to_broadcast([P, P]), cst("upto"),
                                 start=True, stop=True)
                    ins.then_inc(v_full, 1)
                pe.wait_ge(S["g_prep"], at(l, "g_prep", 2))
                transposes((G["et"], G["vb"], G["bh"]), "g")
                pair_matrices(G["kz"], G["kb"], "g")
                pair_matrices(G["kz"], G["co"][:, 0:2, :], "g")
                invert(l, "g", G, lambda n: fill_r() if n < 3 else None)
                pe.wait_ge(S["g_tok"], at(l, "g_tok", 6))
                through(l, "g", G, G["v_tok"])
                scan(l, "g", G, fill_r)
                block_sums(l, "g_sq2", 1, G["sq2"], 2, "g_gv")
                assert not todo

                pe.wait_ge(S["g_out"], at(l, "g_out", 1))
                for i in range(10):
                    feat_group(("ds", i), l, h_hi, h_lo, "a", "d_in" if i < 8 else "d_vf")
                pe.wait_ge(S["d_vf"], at(l, "d_vf", 2))
                for half in range(2):
                    b, reader, emptied = banks.next("a", "d_v")
                    pe.wait_ge(reader, emptied)
                    for t2 in range(2):
                        for f in range(2):
                            t = 2 * half + t2
                            ins = nc.tensor.transpose(b[:, t2 * 256 + f * P:t2 * 256 + (f + 1) * P], Dv["vf"][:, f, t * P:(t + 1) * P], cst("ident"))
                    ins.then_inc(a_full, 1)
                for nm in ("dup", "dup_rot"):
                    b, reader, emptied = banks.next("v", "d_ik")
                    pe.wait_ge(reader, emptied)
                    mm(b[:], cst(nm), misc[:, 1, :], start=True, stop=True).then_inc(v_full, 1)
                for i in range(8):
                    src = Dv["iq"][:, i, :] if i < 4 else Dv["q"][:, i - 4, :] if i < 6 else Dv["k"][:, i - 6, :]
                    b, reader, emptied = banks.next("v", "d_rot")
                    pe.wait_ge(reader, emptied)
                    pe.wait_ge(S["d_in"], at(l, "d_in", i + 1))
                    mm(b[:], cst("rot_d"), src, start=True, stop=True).then_inc(v_full, 1)
                pe.wait_ge(S["d_rot"], at(l, "d_rot", 8))
                pe.wait_ge(S["d_kz"], at(l, "d_kz", 2))
                for qt in range(1, TT):
                    for h in range(8):
                        b, reader, emptied = banks.next("a", "d_sc")
                        pe.wait_ge(reader, emptied)
                        mm(b[:, 0:(qt + 1) * P], Dv["iq"][:, h // 2, qt * P:(qt + 1) * P], Dv["ikz"][:, h % 2, 0:(qt + 1) * P],
                           start=True, stop=True).then_inc(a_full, 1)
                    merge(l, 0, 1, qt - 1)
                merge(l, 0, 1, 3)
                attention(l, "d", lambda h, qt: Dv["q"][:, h // 2, qt * P:(qt + 1) * P],
                          lambda h, n: Dv["kz"][:, h // 2, h % 2, 0:n], Dv["v"], lambda qt: None)

                pe.wait_ge(S["d_o"], at(l, "d_o", 16))
                for i in range(2):
                    feat_group(("cq", i), l, h_hi, h_lo, "a", "m_in")
                merge(l, 3, 0, 0)
                pe.wait_ge(S["m_sq"], at(l, "m_sq", 1))
                b, reader, emptied = banks.next("v", "m_nv")
                pe.wait_ge(reader, emptied)
                for k in range(2):
                    ins = mm(b[:], cst("ones"), Mv["sq"][:, k, :], start=k == 0, stop=k == 1)
                ins.then_inc(v_full, 1)
                b, reader, emptied = banks.next("v", "m_nv")
                pe.wait_ge(reader, emptied)
                mm(b[:], cst("ones"), Mv["sq"][:, 2, :], start=True, stop=True).then_inc(v_full, 1)
                merge(l, 3, 0, 1)
                pe.wait_ge(S["m_c"], at(l, "m_c", 1))
                for h in range(H):
                    b, reader, emptied = banks.next("a", "m_q")
                    pe.wait_ge(reader, emptied)
                    for k in range(2):
                        ins = mm(b[0:96, :], pr("uq")[:, k * 384 + h * 96:k * 384 + (h + 1) * 96], Mv["cq"][:, k, :], start=k == 0, stop=k == 1)
                    ins.then_inc(a_full, 1)
                for h in range(H):
                    b, reader, emptied = banks.next("a", "m_k")
                    pe.wait_ge(reader, emptied)
                    mm(b[0:64, :], pr("ukv")[:, h * P:h * P + C], misc[:, 0, :], start=True, stop=True).then_inc(a_full, 1)
                for half in range(2):
                    b, reader, emptied = banks.next("a", "m_v")
                    pe.wait_ge(reader, emptied)
                    for t2 in range(2):
                        t = 2 * half + t2
                        ins = mm(b[:, t2 * 256:(t2 + 1) * 256], misc[:, 0, t * P:(t + 1) * P],
                                 pr("ukv").rearrange("p (h n) -> p h n", n=P)[:, :, C:P], start=True, stop=True)
                    ins.then_inc(a_full, 1)
                b, reader, emptied = banks.next("v", "m_krb")
                pe.wait_ge(reader, emptied)
                mm(b[0:96, :], cst("rot_m")[64:96, 0:96], misc[64:96, 1, :], start=True, stop=True).then_inc(v_full, 1)
                for h in range(H):
                    b, reader, emptied = banks.next("v", "m_rot")
                    pe.wait_ge(reader, emptied)
                    pe.wait_ge(S["m_q"], at(l, "m_q", h + 1))
                    mm(b[0:96, :], cst("rot_m")[0:96, 0:96], Mv["q"][0:96, h, :], start=True, stop=True).then_inc(v_full, 1)
                merge(l, 3, 0, 2)
                merge(l, 3, 0, 3)
                pe.wait_ge(S["m_rot"], at(l, "m_rot", 4))
                pe.wait_ge(S["m_kr"], at(l, "m_kr", 4))
                pe.wait_ge(S["m_k"], at(l, "m_k", 4))
                pe.wait_ge(S["m_v"], at(l, "m_v", 2))
                attention(l, "m", lambda h, qt: Mv["q"][0:96, h, qt * P:(qt + 1) * P],
                          lambda h, n: Mv["k"][0:96, h, 0:n], Mv["v"], lambda qt: None)
                pe.wait_ge(S["m_o"], at(l, "m_o", 16))
                for i in range(4):
                    merge(l, 1, 1, i)

                for i in range(8):
                    if i == 0:
                        feat_group(("wo", i), l, mg_hi, mg_lo, "v", "wo_done", "mg_lo", at(l, "mg_lo", 0))
                    else:
                        feat_group(("wo", i), l, mg_hi, mg_lo, "v", "wo_done")
                norm_sum(2 * l + 1)
                for q in range(QUARTERS + 1):
                    if q < QUARTERS:
                        for i in range(8):
                            if q == 0 and i == 0:
                                feat_group(("up", i), l, h_hi, h_lo, "a", "up_relu", "n_h", at(l, "n_h", 8))
                            else:
                                feat_group(("up", 8 * q + i), l, h_hi, h_lo, "a", "up_relu")
                    if q >= 1:
                        for i in range(8):
                            hi, lo = up_hi[(q - 1) % 2], up_lo[(q - 1) % 2]
                            if i == 0:
                                feat_group(("down", q - 1, i), l, hi, lo, "v", "down_done", "up_done", at(l, "up_done", 8 * (q - 1)))
                            else:
                                feat_group(("down", q - 1, i), l, hi, lo, "v", "down_done")
            norm_sum(2 * L)
            for t in range(TT):
                for half in range(2):
                    b, reader, emptied = banks.next("a", "o_tok")
                    pe.wait_ge(reader, emptied)
                    if t == 0 and half == 0:
                        pe.wait_ge(S["n_g"], 16 * L + 8)
                    for k in range(4):
                        ins = nc.tensor.transpose(b[:, k * P:(k + 1) * P], mg[:, 4 * half + k, t * P:(t + 1) * P], cst("ident"))
                    ins.then_inc(a_full, 1)

        @block.scalar
        def _(act):
            act_fn = nc.scalar.activation
            filled = Filled(bank_a)

            def invert(l, x, V, fill):
                for t in range(TT):
                    act.wait_ge(a_full, filled.next())
                    b = filled.bank()
                    act_fn(V["t_bd"][:, t * H:(t + 1) * H, :], b[:].rearrange("p (m n) -> p m n", n=P), ACT.Copy).then_inc(S[x + "_ti"], 1)
                for n in range(len(LEVELS)):
                    fill(n)

            def tok(l, x, V, names):
                for nm in names:
                    for half in range(2):
                        act.wait_ge(a_full, filled.next())
                        b = filled.bank()
                        if nm == "k_tokz":
                            for p in range(2):
                                rows = slice(p * C, (p + 1) * C)
                                last = act_fn(V[nm][rows, 2 * half:2 * half + 2, p, :],
                                              b[rows, :].rearrange("p (t n) -> p t n", n=256), ACT.Copy)
                        else:
                            last = act_fn(V[nm][:, 2 * half:2 * half + 2, :], b[:].rearrange("p (t n) -> p t n", n=256), ACT.Copy)
                        last.then_inc(S[x + "_tok"], 1)

            def after_inverse(l, x, V):
                for f in range(2):
                    act.wait_ge(a_full, filled.next())
                    b = filled.bank()
                    act_fn(V["wt"][:, f, :], b[:], ACT.Copy).then_inc(S[x + "_wt"], 1)
                for t in range(TT):
                    act.wait_ge(a_full, filled.next())
                    b = filled.bank()
                    for hp in range(2):
                        last = act_fn(own_half(V["up"][:, t, :], 2, hp), own_half(b[:], 4, 3 * hp), ACT.Copy)
                    last.then_inc(S[x + "_u"], 1)

            def outputs(l, x, V, cs):
                for c in cs:
                    act.wait_ge(a_full, filled.next())
                    b = filled.bank()
                    act_fn(V["o"][:, :, c * C:(c + 1) * C], b[:, 0:P].rearrange("p (f n) -> p f n", n=C), ACT.Copy).then_inc(S[x + "_o"], 1)

            sigs = [0]

            def merge_sig(l):
                for _ in range(2):
                    act.wait_ge(a_full, filled.next())
                    b = filled.bank()
                    n = sigs[0]
                    if n >= 2:
                        act.wait_ge(S["mg_done"], n - 1)
                    act_fn(sg[:, n % 2, :], b[:], ACT.Sigmoid).then_inc(S["mg_sig"], 1)
                    sigs[0] += 1
                    split_next()

            units = [0]

            def split_next():
                g = units[0]
                if g < L * NU:
                    act.wait_ge(w_here[g % RING], 16 * (g // RING + 1))
                    act_fn(w_hi[:, g % SPLIT, :, :], ring[:, g % RING, 0:KT * P].rearrange("p (k n) -> p k n", n=P),
                           ACT.Copy).then_inc(S["split_hi"], 1)
                    units[0] += 1

            def norm_squares(n, need, k0):
                for k in range(KT):
                    act.wait_ge(S[need], k0 + k + 1)
                    act_fn(squares[n % 2][:, k, :], xT[:, k, :], ACT.Square).then_inc(S["n_sq"], 1)

            def norm_root(n, parts=True):
                act.wait_ge(S["n_rec"], n + 1)
                act_fn(sg[:, 0, :], sg[:, 0, :], ACT.Sqrt).then_inc(S["n_rs"], 1)
                if parts:
                    for k in range(KT):
                        act.wait_ge(S["n_g"], n * KT + k + 1)
                        act_fn(h_hi[:, k, :], mg[:, k, :], ACT.Copy).then_inc(S["n_hi"], 1)

            def attention(l, x, V):
                steps = [(qt, h) for qt in range(TT) for h in range(H)]
                for i in range(len(steps) + 1):
                    if i < len(steps):
                        qt, h = steps[i]
                        n = (qt + 1) * P
                        act.wait_ge(S[x + "_ss"], at(l, x + "_ss", i + 1))
                        act_fn(V["ss"][:, i % 2, 0:n], V["ss"][:, i % 2, 0:n], ACT.Exp, bias=sml[:, i % 2:i % 2 + 1], accum_out=sml[:, 2 + i % 2:3 + i % 2]).then_inc(S[x + "_p"], 1)
                    if i >= 1:
                        qt, h = steps[i - 1]
                        act.wait_ge(a_full, filled.next())
                        b = filled.bank()
                        if i >= 3:
                            act.wait_ge(S[x + "_o"], at(l, x + "_o", i - 2))
                        act_fn(V["pt"][:, (i - 1) % 2, 0:qt + 1, :], b[:, 0:(qt + 1) * P].rearrange("p (k n) -> p k n", n=P), ACT.Copy).then_inc(S[x + "_pt"], 1)

            split_next()
            split_next()
            for i in range(2):
                act.wait_ge(S["tab_arg"], i + 1)
                act_fn(POS["sin"][:, i, :], POS["red"][:, i, :], ACT.Sin)
                act_fn(POS["cos"][:, i, :], POS["red"][:, i, :], ACT.Sin, scale=0.5).then_inc(S["tab_sin"], 1)

            for l in range(L):
                if l == 0:
                    norm_squares(0, "x_t", 0)
                norm_root(2 * l)
                if l == 0:
                    act.wait_ge(tab_out, 64)
                for i in range(8):
                    act.wait_ge(a_full, filled.next())
                    b = filled.bank()
                    act_fn(R["rw"][:, i, 1:T + 1], b[:], ACT.Copy).then_inc(S["r_in"], 1)
                    split_next()
                act.wait_ge(a_full, filled.next())
                b = filled.bank()
                act_fn(misc[:, 0, :], b[:], ACT.Copy).then_inc(S["misc_in"], 1)
                split_next()
                act.wait_ge(a_full, filled.next())
                b = filled.bank()
                act_fn(misc[:, 1, :], b[:], ACT.Copy).then_inc(S["misc_in"], 1)
                split_next()
                act.wait_ge(a_full, filled.next())
                b = filled.bank()
                act_fn(ab[:, :, :], b[:].rearrange("p (t n) -> p t n", n=P)[:, :, 96:112], ACT.Copy).then_inc(S["ab_in"], 1)
                act.wait_ge(S["r_mix"], at(l, "r_mix", 8))
                act_fn(R["rm"][0:64, 6, :], R["rm"][0:64, 6, :], ACT.Tanh).then_inc(S["r_act"], 1)
                act_fn(R["rm"][:, 7, :], R["rm"][:, 7, :], ACT.Sigmoid).then_inc(S["r_act"], 1)
                act.wait_ge(par_here, 16 * (l + 1))
                for nm, bias in (("sw", "w0"), ("a", "a0"), ("g", None)):
                    for f in range(2):
                        act.wait_ge(a_full, filled.next())
                        b = filled.bank()
                        if bias:
                            act_fn(R[nm][:, f, :], b[:], ACT.Sigmoid, bias=pr(bias, f)).then_inc(S["r_lora"], 1)
                        else:
                            act_fn(R[nm][:, f, :], b[:], ACT.Copy).then_inc(S["r_lora"], 1)
                act.wait_ge(S["r_cum"], at(l, "r_cum", 1))
                act_fn(R["p"], R["cs"], ACT.Exp, scale=-DECAY).then_inc(S["r_dec"], 1)
                act_fn(R["pi"], R["cs"], ACT.Exp, scale=DECAY).then_inc(S["r_dec"], 1)
                act.wait_ge(S["r_ex"], at(l, "r_ex", 1))
                act_fn(R["pe"], R["sw"], ACT.Exp, scale=-DECAY).then_inc(S["r_dec"], 1)
                act.wait_ge(S["r_l2r"], at(l, "r_l2r", 1))
                act_fn(R["tmp"], R["tmp"], ACT.Sqrt).then_inc(S["r_l2s"], 1)
                act.wait_ge(S["r_feat"], at(l, "r_feat", 4))
                tok(l, "r", R, ("e_tok", "v_tok", "b_tok", "k_tokz"))
                invert(l, "r", R, lambda n: None)
                after_inverse(l, "r", R)
                outputs(l, "r", R, range(NC))
                act.wait_ge(S["r_gr"], at(l, "r_gr", 1))
                act_fn(R["sq"], R["sq"], ACT.Sqrt).then_inc(S["r_gs"], 1)

                for i in range(6):
                    act.wait_ge(a_full, filled.next())
                    b = filled.bank()
                    if i == 0:
                        act.wait_ge(S["g_pad"], at(l, "g_pad", 1))
                    act_fn(G["ci"][:, i, 3:T + 3], b[:], ACT.Copy).then_inc(S["g_in"], 1)
                    split_next()
                for i in range(2):
                    act.wait_ge(a_full, filled.next())
                    b = filled.bank()
                    act_fn(G["z"][:, i, :], b[:], ACT.Copy).then_inc(S["g_z"], 1)
                    split_next()
                act.wait_ge(S["g_t1"], at(l, "g_t1", 1))
                act_fn(gsm[:, 1, :], gsm[:, 1, :], ACT.Exp).then_inc(act_step, 1)
                act_fn(sml[:, 8:12], pr("a_log"), ACT.Exp).then_inc(S["g_t2"], 1)
                act.wait_ge(act_step, 2 * l + 1)
                act_fn(gsm[:, 1, :], gsm[:, 1, :], ACT.Ln, bias=1.0).then_inc(act_step, 1)
                act.wait_ge(act_step, 2 * l + 2)
                act.wait_ge(S["g_conv"], at(l, "g_conv", 6))
                act_fn(gsm[:, 5, :], ab[:, :, 4:8], ACT.Sigmoid)
                act_fn(G["sig"], G["co"], ACT.Sigmoid).then_inc(S["g_sig"], 1)
                act_fn(G["bh"], G["z"], ACT.Sigmoid).then_inc(S["g_zs"], 1)
                act.wait_ge(S["g_l2r"], at(l, "g_l2r", 1))
                act_fn(G["rs"], G["rs"], ACT.Sqrt).then_inc(S["g_l2s"], 1)
                merge_sig(l)
                act.wait_ge(S["g_qk"], at(l, "g_qk", 1))
                for i in range(6):
                    act.wait_ge(a_full, filled.next())
                    b = filled.bank()
                    f = i % 2
                    dst = (G["egc"], G["ers"], G["beta"])[i // 2][:, f, :]
                    act_fn(dst, b[:], ACT.Exp if i < 4 else ACT.Copy).then_inc(S["g_feat"], 1)
                for t in range(TT):
                    act.wait_ge(S["g_row"], at(l, "g_row", t + 1))
                    act_fn(G["d"][:, t * H:(t + 1) * H, :], G["d"][:, t * H:(t + 1) * H, :], ACT.Exp).then_inc(S["g_d"], 1)
                act.wait_ge(S["g_prep"], at(l, "g_prep", 2))
                tok(l, "g", G, ("e_tok", "v_tok", "b_tok"))
                invert(l, "g", G, lambda n: merge_sig(l) if n < 3 else None)
                after_inverse(l, "g", G)
                outputs(l, "g", G, range(0, 8))
                act.wait_ge(S["g_gr"], at(l, "g_gr", 1))
                act_fn(G["sq2"], G["sq2"], ACT.Sqrt).then_inc(S["g_gs"], 1)

                act.wait_ge(S["g_out"], at(l, "g_out", 1))
                for i in range(8):
                    act.wait_ge(a_full, filled.next())
                    b = filled.bank()
                    dst = Dv["iq"][:, i, :] if i < 4 else Dv["q"][:, i - 4, :] if i < 6 else Dv["k"][:, i - 6, :]
                    act_fn(dst, b[:], ACT.Copy).then_inc(S["d_in"], 1)
                    split_next()
                for f in range(2):
                    act.wait_ge(a_full, filled.next())
                    b = filled.bank()
                    act_fn(Dv["vf"][:, f, :], b[:], ACT.Copy).then_inc(S["d_vf"], 1)
                    split_next()
                for half in range(2):
                    act.wait_ge(a_full, filled.next())
                    b = filled.bank()
                    act_fn(Dv["v"][:, 2 * half:2 * half + 2, :], b[:].rearrange("p (t n) -> p t n", n=256), ACT.Copy).then_inc(S["d_v"], 1)
                i = 0
                for qt in range(1, TT):
                    n = (qt + 1) * P
                    for h in range(8):
                        act.wait_ge(a_full, filled.next())
                        b = filled.bank()
                        if i >= 2:
                            act.wait_ge(S["d_acc"], at(l, "d_acc", i - 1))
                        act_fn(Dv["rl"][:, i % 2, 0:n], b[:, 0:n], ACT.Relu).then_inc(S["d_sc"], 1)
                        i += 1
                    merge_sig(l)
                merge_sig(l)
                attention(l, "d", Dv)

                act.wait_ge(S["d_o"], at(l, "d_o", 16))
                for j in range(2):
                    act.wait_ge(a_full, filled.next())
                    b = filled.bank()
                    act_fn(Mv["cq"][:, j, :], b[:], ACT.Copy).then_inc(S["m_in"], 1)
                    split_next()
                merge_sig(l)
                act.wait_ge(S["m_rec"], at(l, "m_rec", 1))
                act_fn(Mv["rs"], Mv["rs"], ACT.Sqrt).then_inc(S["m_rs"], 1)
                merge_sig(l)
                for h in range(H):
                    act.wait_ge(a_full, filled.next())
                    b = filled.bank()
                    act_fn(Mv["q"][0:96, h, :], b[0:96, :], ACT.Copy).then_inc(S["m_q"], 1)
                for h in range(H):
                    act.wait_ge(a_full, filled.next())
                    b = filled.bank()
                    act_fn(Mv["k"][0:64, h, :], b[0:64, :], ACT.Copy).then_inc(S["m_k"], 1)
                for half in range(2):
                    act.wait_ge(a_full, filled.next())
                    b = filled.bank()
                    act_fn(Mv["v"][:, 2 * half:2 * half + 2, :], b[:].rearrange("p (t n) -> p t n", n=256), ACT.Copy).then_inc(S["m_v"], 1)
                merge_sig(l)
                merge_sig(l)
                attention(l, "m", Mv)
                mg_tile = 0
                for _ in range(4):
                    merge_sig(l)
                    for m in range(mg_tile, mg_tile + 2):
                        act.wait_ge(S["mg_done"], at(l, "mg_done", 24 + m + 1))
                        act_fn(mg_hi[:, m, :], mg[:, m, :], ACT.Copy).then_inc(S["mg_hi"], 1)
                    mg_tile += 2
                act.wait_ge(x_back, 16 * (l + 1))
                for m in range(8):
                    act.wait_ge(S["wo_done"], at(l, "wo_done", m + 1))
                    split_next()
                    act_fn(squares[1][:, m, :], xT[:, m, :], ACT.Square).then_inc(S["n_sq"], 1)
                norm_root(2 * l + 1)
                for q in range(QUARTERS + 1):
                    if q < QUARTERS:
                        for i in range(8):
                            n = 8 * q + i
                            act.wait_ge(a_full, filled.next())
                            b = filled.bank()
                            if n >= 2:
                                act.wait_ge(S["up_sq"], at(l, "up_sq", n - 1))
                            act_fn(relu[:, n % 2, :], b[:], ACT.Relu).then_inc(S["up_relu"], 1)
                            act.wait_ge(S["up_relu"], at(l, "up_relu", n + 1))
                            act_fn(up_hi[q % 2][:, i, :], relu[:, n % 2, :], ACT.Square).then_inc(S["up_hi"], 1)
                            split_next()
                    if q >= 1:
                        for m in range(8):
                            act.wait_ge(S["down_done"], at(l, "down_done", 8 * (q - 1) + m + 1))
                            split_next()
                            if q == QUARTERS:
                                act_fn(squares[0][:, m, :], xT[:, m, :], ACT.Square).then_inc(S["n_sq"], 1)
            norm_root(2 * L, False)
            for t in range(TT):
                for half in range(2):
                    act.wait_ge(a_full, filled.next())
                    b = filled.bank()
                    act_fn(xout[:, t, half * T:(half + 1) * T], b[:], ACT.Copy).then_inc(S["o_tok"], 1)

        @block.vector
        def _(dve):
            v = nc.vector
            filled = Filled(bank_v)
            counts = {}

            def reached(name):
                counts[name] = counts.get(name, 0) + 1
                return counts[name]

            def link(ins):
                ins.then_inc(dve_step, 1)
                dve.wait_ge(dve_step, reached("step"))

            def tt(out_, a, b, op):
                link(v.tensor_tensor(out_, a, b, op))

            def ts(out_, a, s1, s2, op0, op1=ALU.bypass):
                link(v.tensor_scalar(out_, a, s1, s2, op0, op1))

            def stt(out_, a, s, b, op0, op1):
                link(v.scalar_tensor_tensor(out_, a, s, b, op0, op1))

            MUL, ADD, SUB = ALU.mult, ALU.add, ALU.subtract
            hm = (cst("blocks")[:, 0:1], cst("blocks")[:, C:C + 1])

            def norm(n, gain, parts=True):
                dve.wait_ge(v_full, filled.next())
                b = filled.bank()
                v.tensor_scalar(sg[:, 0, :], b[:], 1.0 / D, EPS, MUL, ADD).then_inc(S["n_var"], 1)
                dve.wait_ge(S["n_var"], reached("n_var"))
                v.reciprocal(sg[:, 0, :], sg[:, 0, :]).then_inc(S["n_rec"], 1)
                dve.wait_ge(S["n_rec"], reached("n_rec"))
                dve.wait_ge(S["n_rs"], n + 1)
                for k in range(KT + 1):
                    if k < KT:
                        v.scalar_tensor_tensor(mg[:, k, :], xT[:, k, :], pr(gain, k), sg[:, 0, :], MUL, MUL).then_inc(S["n_g"], 1)
                    if parts and k >= 1:
                        dve.wait_ge(S["n_hi"], n * KT + k)
                        v.tensor_tensor(h_lo[:, k - 1, :], mg[:, k - 1, :], h_hi[:, k - 1, :].bitcast(F32), SUB).then_inc(S["n_h"], 1)

            def bank3(b, n):
                return b[:].rearrange("p (m n) -> p m n", n=n)

            def masked(x, dst, mask, count):
                for t in range(TT):
                    dve.wait_ge(v_full, filled.next())
                    b = filled.bank()
                    m = mask(t)
                    v.tensor_tensor(dst[:, t * H:(t + 1) * H, :], bank3(b, P), m, MUL).then_inc(S[x + "_mat"], 1)
                    dve.wait_ge(S[x + "_mat"], reached(x + "_mat"))

            def invert(l, x, V, fill):
                first = cst("first").unsqueeze(1).to_broadcast([P, H, P])
                eye = cst("ident").unsqueeze(1).to_broadcast([P, H, P])
                for t in range(TT):
                    ms = slice(t * H, (t + 1) * H)
                    tt(V["x_bd"][:, ms, :], V["u"][:, ms, :], first, MUL)
                    v.tensor_tensor(V["x_bd"][:, ms, :], V["x_bd"][:, ms, :], eye, ADD).then_inc(S[x + "_x1"], 1)
                    dve.wait_ge(S[x + "_x1"], reached(x + "_x1"))
                for n, s in enumerate(LEVELS):
                    lev = cst(f"level{s}").unsqueeze(1).to_broadcast([P, H, P])
                    for t in range(TT):
                        dve.wait_ge(v_full, filled.next())
                        b = filled.bank()
                        v.tensor_tensor(V["y_bd"][:, t * H:(t + 1) * H, :], bank3(b, P), lev, MUL).then_inc(S[x + "_y"], 1)
                    if n < len(LEVELS) - 1:
                        for t in range(TT):
                            ms = slice(t * H, (t + 1) * H)
                            dve.wait_ge(v_full, filled.next())
                            b = filled.bank()
                            v.tensor_tensor(V["t_bd"][:, ms, :], V["t_bd"][:, ms, :], bank3(b, P), SUB).then_inc(S[x + "_t"], 1)
                    for t in range(TT):
                        ms = slice(t * H, (t + 1) * H)
                        dve.wait_ge(v_full, filled.next())
                        b = filled.bank()
                        v.tensor_tensor(V["x_bd"][:, ms, :], V["x_bd"][:, ms, :], bank3(b, P), SUB).then_inc(S[x + "_x"], 1)
                    fill(n)

            def scan(l, x, V, fill):
                v.memset(s_z[:], 0.0).then_inc(S[x + "_s0"], 1)
                dve.wait_ge(S[x + "_s0"], reached(x + "_s0"))
                dve.wait_ge(S[x + "_u"], at(l, x + "_u", TT))
                for c in range(NC):
                    t, par_ = divmod(c, 2)
                    rows = slice(par_ * C, (par_ + 1) * C)
                    dve.wait_ge(v_full, filled.next())
                    b = filled.bank()
                    v.tensor_tensor(un_z[rows, par_, :], V["up"][rows, t, :], b[rows, 0:4 * C], SUB).then_inc(S[x + "_ws"], 1)
                    dve.wait_ge(S[x + "_ws"], reached(x + "_ws"))
                    dve.wait_ge(v_full, filled.next())
                    b = filled.bank()
                    for h in range(H):
                        f, hp = divmod(h, 2)
                        hr = slice(hp * C, (hp + 1) * C)
                        ins = v.scalar_tensor_tensor(out=s_z[hr, f, hp, :], in0=s_z[hr, f, hp, :], scalar=pc[hr, f, c:c + 1],
                                                     in1=b[hr, f * C:(f + 1) * C], op0=MUL, op1=ADD)
                    ins.then_inc(S[x + "_s"], 1)
                    dve.wait_ge(S[x + "_s"], reached(x + "_s"))
                    if c in (1, 4):
                        fill()

            merged = [0]

            def merge(l, first=False):
                for _ in range(2):
                    n = merged[0]
                    m = n % 8
                    dve.wait_ge(v_full, filled.next())
                    b = filled.bank()
                    dve.wait_ge(S["mg_sig"], n + 1)
                    s = sg[:, n % 2, :]
                    if first:
                        v.tensor_tensor(mg[:, m, :], b[:], s, MUL).then_inc(S["mg_done"], 1)
                        dve.wait_ge(S["mg_done"], reached("mg_done"))
                    else:
                        tt(s, b[:], s, MUL)
                        v.tensor_tensor(mg[:, m, :], mg[:, m, :], s, ADD).then_inc(S["mg_done"], 1)
                        dve.wait_ge(S["mg_done"], reached("mg_done"))
                    merged[0] += 1

            def attention(l, x, V, scale, bias, slot):
                steps = [(qt, h) for qt in range(TT) for h in range(H)]
                for i in range(len(steps) + 2):
                    if i < len(steps):
                        qt, h = steps[i]
                        n = (qt + 1) * P
                        dve.wait_ge(v_full, filled.next())
                        b = filled.bank()
                        if i >= 2:
                            dve.wait_ge(S[x + "_pt"], at(l, x + "_pt", i - 1))
                        ss = V["ss"][:, i % 2, 0:n]
                        stt(ss, b[:, 0:n], scale, bias(qt), MUL, ADD)
                        v.tensor_reduce(sml[:, i % 2:i % 2 + 1], ss, AX_X, ALU.max, negate=True).then_inc(S[x + "_ss"], 1)
                        dve.wait_ge(S[x + "_ss"], reached(x + "_ss"))
                    if 1 <= i <= len(steps):
                        j = i - 1
                        qt, h = steps[j]
                        n = (qt + 1) * P
                        dve.wait_ge(S[x + "_p"], at(l, x + "_p", j + 1))
                        link(v.reciprocal(sml[:, 4 + j % 2:5 + j % 2], sml[:, 2 + j % 2:3 + j % 2]))
                        ss = V["ss"][:, j % 2, 0:n]
                        v.tensor_scalar(ss, ss, sml[:, 4 + j % 2:5 + j % 2], None, MUL).then_inc(S[x + "_pn"], 1)
                        dve.wait_ge(S[x + "_pn"], reached(x + "_pn"))
                    if i >= 2:
                        qt, h = steps[i - 2]
                        dve.wait_ge(v_full, filled.next())
                        b = filled.bank()
                        rows = slice((h % 2) * C, (h % 2 + 1) * C)
                        v.tensor_copy(yo[rows, slot, h // 2, qt * P:(qt + 1) * P], b[rows, 0:P]).then_inc(S[x + "_o"], 1)
                        dve.wait_ge(S[x + "_o"], reached(x + "_o"))

            link(v.memset(un_z[:], 0.0))
            link(v.memset(misc[:], 0.0))
            dve.wait_ge(const_here, 16)
            for k in range(KT):
                dve.wait_ge(v_full, filled.next())
                b = filled.bank()
                v.tensor_copy(xT[:, k, :], b[:]).then_inc(S["x_t"], 1)
                dve.wait_ge(S["x_t"], reached("x_t"))
            dve.wait_ge(pos_here, 16)
            link(v.tensor_copy(POS["f"], POS["i"]))
            for i, nm in enumerate(rotors):
                ts(POS["ang"], POS["f"], cst("freq_" + nm), None, MUL)
                ts(POS["k"], POS["ang"], float(1.0 / (2.0 * np.pi)), MAGIC, MUL, ADD)
                ts(POS["k"], POS["k"], MAGIC, None, SUB)
                red = POS["red"][:, i, :]
                stt(red, POS["k"], -TWO_PI[0], POS["ang"], MUL, ADD)
                stt(red, POS["k"], -TWO_PI[1], red, MUL, ADD)
                stt(red, POS["k"], -TWO_PI[2], red, MUL, ADD)
                v.tensor_scalar(red, red, 3.1415925, -3.1415925, ALU.min, ALU.max).then_inc(S["tab_arg"], 1)
                dve.wait_ge(S["tab_arg"], reached("tab_arg"))
            for i in range(2):
                dve.wait_ge(S["tab_sin"], i + 1)
                cos = POS["cos"][:, i, :]
                tt(cos, cos, cos, MUL)
                v.tensor_scalar(cos, cos, -2.0, 1.0, MUL, ADD).then_inc(S["tab"], 1)
                dve.wait_ge(S["tab"], reached("tab"))

            for l in range(L):
                dve.wait_ge(par_here, 16 * (l + 1))
                norm(2 * l, "mix_g")
                if l == 0:
                    dve.wait_ge(tab_out, 64)
                v.memset(R["rw"][:, :, 0:1], 0.0).then_inc(S["r_zero"], 1)
                dve.wait_ge(S["r_zero"], reached("r_zero"))
                ts(sml[:, 12:14], pr("k_a"), -1.0, 1.0, MUL, ADD)
                dve.wait_ge(S["r_in"], at(l, "r_in", 8))
                tt(R["rm"], R["rw"][:, :, 0:T], R["rw"][:, :, 1:T + 1], SUB)
                for i in range(8):
                    v.scalar_tensor_tensor(R["rm"][:, i, :], R["rm"][:, i, :], pr("mu", i), R["rw"][:, i, 1:T + 1], MUL, ADD).then_inc(S["r_mix"], 1)
                    dve.wait_ge(S["r_mix"], reached("r_mix"))
                r_, k_, v_ = R["rm"][:, 0:2, :], R["rm"][:, 2:4, :], R["rm"][:, 4:6, :]
                for f in range(2):
                    ts(R["kk"][:, f, :], k_[:, f, :], pr("k_k", f), None, MUL)
                v.tensor_tensor(R["tmp"], R["kk"], R["kk"], MUL).then_inc(S["r_sq"], 1)
                dve.wait_ge(S["r_sq"], reached("r_sq"))
                dve.wait_ge(x_away, 16 * (l + 1))
                dve.wait_ge(S["r_lora"], at(l, "r_lora", 2))
                for f in range(2):
                    for c in range(NC):
                        cs = slice(c * C, (c + 1) * C)
                        ins = v.tensor_tensor_scan(R["cs"][:, f, cs], cst("ones")[:, 0:C], R["sw"][:, f, cs], 0.0, MUL, ADD)
                ins.then_inc(S["r_cum"], 1)
                dve.wait_ge(S["r_cum"], reached("r_cum"))
                v.tensor_tensor(R["sw"], R["cs"], R["sw"], SUB).then_inc(S["r_ex"], 1)
                dve.wait_ge(S["r_ex"], reached("r_ex"))
                for f in range(2):
                    dve.wait_ge(v_full, filled.next())
                    b = filled.bank()
                    v.tensor_scalar(R["tmp"][:, f, :], b[:], EPS, None, ADD).then_inc(S["r_l2"], 1)
                    dve.wait_ge(S["r_l2"], reached("r_l2"))
                v.reciprocal(R["tmp"], R["tmp"]).then_inc(S["r_l2r"], 1)
                dve.wait_ge(S["r_l2r"], reached("r_l2r"))
                dve.wait_ge(S["r_l2s"], at(l, "r_l2s", 1))
                tt(R["kk"], R["kk"], R["tmp"], MUL)
                dve.wait_ge(S["r_lora"], at(l, "r_lora", 4))
                for f in range(2):
                    ts(R["tmp"][:, f, :], R["a"][:, f, :], pr("k_a", f), sml[:, 12 + f:13 + f], MUL, ADD)
                tt(k_, k_, R["tmp"], MUL)
                for f in range(2):
                    v.scalar_tensor_tensor(R["tmp"][:, f, :], k_[:, f, :], pr("r_k", f), r_[:, f, :], MUL, MUL).then_inc(S["r_bsq"], 1)
                    dve.wait_ge(S["r_bsq"], reached("r_bsq"))
                for f in range(2):
                    dve.wait_ge(v_full, filled.next())
                    b = filled.bank()
                    v.tensor_tensor(R["bon"][:, f, :], b[:], v_[:, f, :], MUL).then_inc(S["r_bon"], 1)
                    dve.wait_ge(S["r_bon"], reached("r_bon"))
                dve.wait_ge(S["r_dec"], at(l, "r_dec", 3))
                link(v.tensor_copy(pc[:], R["p"].rearrange("p f (c k) -> p f c k", k=C)[:, :, :, C - 1]))
                tt(R["et"], R["pe"], R["kk"], MUL)
                tt(R["rt"], R["p"], r_, MUL)
                tt(R["tmp"], R["kk"], R["a"], MUL)
                for hp in range(2):
                    stt(R["bz"][:, :, hp, :], R["pi"], hm[hp], R["tmp"], MUL, MUL)
                    stt(R["kz"][:, :, hp, :], R["pi"], hm[hp], k_, MUL, MUL)
                tt(R["bh"], R["tmp"], R["pi"], MUL)
                tt(R["kh"], k_, R["pi"], MUL)
                link(v.memset(R["k_tokz"], 0.0))
                for nm in ("bh", "kh"):
                    for f in range(2):
                        y = R[nm][:, f, :].rearrange("p (c k) -> p c k", k=C)
                        v.tensor_tensor(y, y, pc[:, f, :].unsqueeze(2).to_broadcast([P, NC, C]), MUL).then_inc(S["r_feat"], 1)
                        dve.wait_ge(S["r_feat"], reached("r_feat"))
                before = cst("before").unsqueeze(1).to_broadcast([P, H, P])
                upto = cst("upto").unsqueeze(1).to_broadcast([P, H, P])
                masked("r", R["u"], lambda t: before, 4)
                dve.wait_ge(S["r_tok"], at(l, "r_tok", 8))
                masked("r", R["akk"], lambda t: before, 4)
                masked("r", R["ark"], lambda t: upto, 4)
                masked("r", R["arb"], lambda t: upto, 4)
                invert(l, "r", R, lambda n: None)
                for t in range(TT):
                    dve.wait_ge(v_full, filled.next())
                    b = filled.bank()
                    for hp in range(2):
                        ins = v.tensor_scalar(own_half(R["y1"][:, t, :], 2, hp), own_half(b[:], 4, 3 * hp), -1.0, None, MUL)
                    ins.then_inc(S["r_y1"], 1)
                scan(l, "r", R, lambda: None)
                for f in range(2):
                    dve.wait_ge(v_full, filled.next())
                    b = filled.bank()
                    v.scalar_tensor_tensor(R["o"][:, f, :], b[:], -1.0 / C, R["o"][:, f, :], MUL, ADD).then_inc(S["r_mean"], 1)
                    dve.wait_ge(S["r_mean"], reached("r_mean"))
                v.tensor_tensor(R["sq"], R["o"], R["o"], MUL).then_inc(S["r_sq2"], 1)
                dve.wait_ge(S["r_sq2"], reached("r_sq2"))
                for f in range(2):
                    dve.wait_ge(v_full, filled.next())
                    b = filled.bank()
                    v.tensor_scalar(R["sq"][:, f, :], b[:], 1.0 / C, GN_EPS, MUL, ADD).then_inc(S["r_gv"], 1)
                    dve.wait_ge(S["r_gv"], reached("r_gv"))
                v.reciprocal(R["sq"], R["sq"]).then_inc(S["r_gr"], 1)
                dve.wait_ge(S["r_gr"], reached("r_gr"))
                dve.wait_ge(S["r_gs"], at(l, "r_gs", 1))
                tt(R["o"], R["o"], R["sq"], MUL)
                for f in range(2):
                    ts(R["o"][:, f, :], R["o"][:, f, :], pr("ln_w", f), pr("ln_b", f), MUL, ADD)
                tt(R["o"], R["o"], R["bon"], ADD)
                v.tensor_tensor(yo[:, 0, :, :], R["o"], R["g"], MUL).then_inc(S["r_out"], 1)
                dve.wait_ge(S["r_out"], reached("r_out"))

                v.memset(G["ci"][:, :, 0:3], 0.0).then_inc(S["g_pad"], 1)
                dve.wait_ge(S["g_pad"], reached("g_pad"))
                dve.wait_ge(S["ab_in"], at(l, "ab_in", 1))
                th = lambda i: gsm[:, i, :].rearrange("p (t h) -> p t h", h=H)
                tt(th(0), ab[:, :, 0:4], pr("dt").unsqueeze(1).to_broadcast([P, TT, H]), ADD)
                v.scalar_tensor_tensor(gsm[:, 1, :], gsm[:, 0, :], -1.0, gsm[:, 0, :], MUL, ALU.min).then_inc(S["g_t1"], 1)
                dve.wait_ge(S["g_t1"], reached("g_t1"))
                ts(ab[:, :, 8:16], ab[:, :, 8:16], float((8 * 64) ** -0.5), None, MUL)
                for i in range(6):
                    dve.wait_ge(S["g_in"], at(l, "g_in", i + 1))
                    ts(G["co"][:, i, :], G["ci"][:, i, 0:T], pr("conv", 4 * i), None, MUL)
                    for j in range(1, 3):
                        stt(G["co"][:, i, :], G["ci"][:, i, j:j + T], pr("conv", 4 * i + j), G["co"][:, i, :], MUL, ADD)
                    v.scalar_tensor_tensor(G["co"][:, i, :], G["ci"][:, i, 3:3 + T], pr("conv", 4 * i + 3), G["co"][:, i, :], MUL, ADD).then_inc(S["g_conv"], 1)
                    dve.wait_ge(S["g_conv"], reached("g_conv"))
                dve.wait_ge(S["g_sig"], at(l, "g_sig", 1))
                tt(G["co"], G["co"], G["sig"], MUL)
                v.tensor_tensor(G["sq"], G["co"][:, 0:4, :], G["co"][:, 0:4, :], MUL).then_inc(S["g_sq"], 1)
                dve.wait_ge(S["g_sq"], reached("g_sq"))
                stt(gsm[:, 2, :], gsm[:, 0, :], 0.0, gsm[:, 1, :], ALU.max, ADD)
                stt(th(4), th(2), -1.0, sml[:, 8:12].unsqueeze(1).to_broadcast([P, TT, H]), MUL, MUL)
                for i, nm in ((4, "g_wide"), (5, "b_wide")):
                    v.tensor_copy(G[nm].rearrange("p (m n) -> p m n", n=C), gsm[:, i, :].unsqueeze(2).to_broadcast([P, M, C])).then_inc(S["g_g"], 1)
                    dve.wait_ge(S["g_g"], reached("g_g"))
                dve.wait_ge(S["g_zs"], at(l, "g_zs", 1))
                tt(G["z"], G["z"], G["bh"], MUL)
                for i in range(4):
                    dve.wait_ge(v_full, filled.next())
                    b = filled.bank()
                    v.tensor_scalar(G["rs"][:, i, :], b[:], EPS, None, ADD).then_inc(S["g_l2"], 1)
                    dve.wait_ge(S["g_l2"], reached("g_l2"))
                v.reciprocal(G["rs"], G["rs"]).then_inc(S["g_l2r"], 1)
                dve.wait_ge(S["g_l2r"], reached("g_l2r"))
                dve.wait_ge(S["g_l2s"], at(l, "g_l2s", 1))
                stt(G["co"][:, 0:2, :], G["co"][:, 0:2, :], C ** -0.5, G["rs"][:, 0:2, :], MUL, MUL)
                v.tensor_tensor(G["co"][:, 2:4, :], G["co"][:, 2:4, :], G["rs"][:, 2:4, :], MUL).then_inc(S["g_qk"], 1)
                dve.wait_ge(S["g_qk"], reached("g_qk"))
                q_, k_, v_ = G["co"][:, 0:2, :], G["co"][:, 2:4, :], G["co"][:, 4:6, :]
                merge(l, True)
                dve.wait_ge(v_full, filled.next())
                b = filled.bank()
                v.tensor_copy(gsm[:, 3, :], b[:, 0:M]).then_inc(S["g_gc"], 1)
                dve.wait_ge(S["g_gc"], reached("g_gc"))
                for t in range(TT):
                    dve.wait_ge(v_full, filled.next())
                    b = filled.bank()
                    for h in range(H):
                        m = t * H + h
                        ins = v.tensor_scalar(G["d"][:, m, :], b[:, h * P:(h + 1) * P], gsm[:, 3, m:m + 1], 0.0, SUB, ALU.min)
                    ins.then_inc(S["g_row"], 1)
                    dve.wait_ge(S["g_row"], reached("g_row"))
                for t in range(TT):
                    dve.wait_ge(S["g_d"], at(l, "g_d", t + 1))
                    v.tensor_tensor(G["d"][:, t * H:(t + 1) * H, :], G["d"][:, t * H:(t + 1) * H, :], upto, MUL).then_inc(S["g_dm"], 1)
                    dve.wait_ge(S["g_dm"], reached("g_dm"))
                dve.wait_ge(S["g_feat"], at(l, "g_feat", 6))
                link(v.tensor_copy(pc[:], G["egc"].rearrange("p f (c k) -> p f c k", k=C)[:, :, :, C - 1]))
                tt(G["kb"], k_, G["beta"], MUL)
                tt(G["rt"], q_, G["egc"], MUL)
                tt(G["et"], G["kb"], G["egc"], MUL)
                tt(G["bh"], k_, G["ers"], MUL)
                tt(G["vb"], v_, G["beta"], MUL)
                for hp in range(2):
                    v.tensor_scalar(G["kz"][:, :, hp, :], k_, hm[hp], None, MUL).then_inc(S["g_prep"], 1)
                    dve.wait_ge(S["g_prep"], reached("g_prep"))
                masked("g", G["u"], lambda t: G["d"][:, t * H:(t + 1) * H, :], 4)
                masked("g", G["arb"], lambda t: G["d"][:, t * H:(t + 1) * H, :], 4)
                dve.wait_ge(S["g_tok"], at(l, "g_tok", 6))
                invert(l, "g", G, lambda n: merge(l, True) if n < 3 else None)
                scan(l, "g", G, lambda: None)
                dve.wait_ge(S["g_o"], at(l, "g_o", NC))
                v.tensor_tensor(G["sq2"], G["o"], G["o"], MUL).then_inc(S["g_sq2"], 1)
                dve.wait_ge(S["g_sq2"], reached("g_sq2"))
                for f in range(2):
                    dve.wait_ge(v_full, filled.next())
                    b = filled.bank()
                    v.tensor_scalar(G["sq2"][:, f, :], b[:], 1.0 / C, EPS, MUL, ADD).then_inc(S["g_gv"], 1)
                    dve.wait_ge(S["g_gv"], reached("g_gv"))
                v.reciprocal(G["sq2"], G["sq2"]).then_inc(S["g_gr"], 1)
                dve.wait_ge(S["g_gr"], reached("g_gr"))
                dve.wait_ge(S["g_gs"], at(l, "g_gs", 1))
                stt(G["o"], G["o"], pr("gdn_g", 0), G["sq2"], MUL, MUL)
                v.tensor_tensor(yo[:, 1, :, :], G["o"], G["z"], MUL).then_inc(S["g_out"], 1)
                dve.wait_ge(S["g_out"], reached("g_out"))

                dve.wait_ge(tab_d_here, 16 * (l + 1))
                cos, sin = Dv["tab"][:, 0, :], Dv["tab"][:, 1, :]
                link(v.memset(Dv["ikz"], 0.0))
                dve.wait_ge(v_full, filled.next())
                b = filled.bank()
                for hp in range(2):
                    hr = slice(hp * C, (hp + 1) * C)
                    ins = v.tensor_tensor(Dv["ikz"][hr, hp, :], b[hr, :], cos[hr, :], MUL)
                ins.then_inc(S["d_ik"], 1)
                dve.wait_ge(S["d_ik"], reached("d_ik"))
                dve.wait_ge(v_full, filled.next())
                b = filled.bank()
                v.tensor_tensor(Dv["tmp"], b[:], sin, MUL).then_inc(S["d_ik"], 1)
                dve.wait_ge(S["d_ik"], reached("d_ik"))
                for hp in range(2):
                    hr = slice(hp * C, (hp + 1) * C)
                    tt(Dv["ikz"][hr, hp, :], Dv["ikz"][hr, hp, :], Dv["tmp"][hr, :], ADD)
                for i in range(8):
                    x_ = Dv["iq"][:, i, :] if i < 4 else Dv["q"][:, i - 4, :] if i < 6 else Dv["k"][:, i - 6, :]
                    dve.wait_ge(v_full, filled.next())
                    b = filled.bank()
                    tt(Dv["tmp"], b[:], sin, MUL)
                    tt(x_, x_, cos, MUL)
                    v.tensor_tensor(x_, x_, Dv["tmp"], ADD).then_inc(S["d_rot"], 1)
                    dve.wait_ge(S["d_rot"], reached("d_rot"))
                for hp in range(2):
                    v.tensor_scalar(Dv["kz"][:, :, hp, :], Dv["k"], hm[hp], None, MUL).then_inc(S["d_kz"], 1)
                    dve.wait_ge(S["d_kz"], reached("d_kz"))
                i = 0
                for qt in range(1, TT):
                    n = (qt + 1) * P
                    sc, wk, gt, eq, cum = (Dv[x_][:, 0:n] for x_ in ("sc", "wk", "gt", "eq", "cum"))
                    for h in range(8):
                        dve.wait_ge(S["d_sc"], at(l, "d_sc", i + 1))
                        iw, rl = ab[:, qt, 8 + h:9 + h], Dv["rl"][:, i % 2, 0:n]
                        if h == 0:
                            v.tensor_scalar(sc, rl, iw, None, MUL).then_inc(S["d_acc"], 1)
                            dve.wait_ge(S["d_acc"], reached("d_acc"))
                        else:
                            v.scalar_tensor_tensor(sc, rl, iw, sc, MUL, ADD).then_inc(S["d_acc"], 1)
                            dve.wait_ge(S["d_acc"], reached("d_acc"))
                        i += 1
                    tt(sc[:, qt * P:n], sc[:, qt * P:n], cst("causal"), ADD)
                    src = sc
                    for r in range(TOPK // 8):
                        link(v.max(m8[:], src))
                        if r < TOPK // 8 - 1:
                            link(v.match_replace(wk, m8[:], src, -3e38))
                            src = wk
                    ts(gt, sc, m8[:, 7:8], None, ALU.is_gt)
                    link(v.tensor_reduce(sml[:, 6:7], gt, AX_X, ADD))
                    ts(sml[:, 7:8], sml[:, 6:7], -1.0, float(TOPK), MUL, ADD)
                    ts(eq, sc, m8[:, 7:8], None, ALU.is_equal)
                    link(v.tensor_tensor_scan(cum, eq, eq, 0.0, ADD, ALU.max))
                    stt(eq, cum, sml[:, 7:8], eq, ALU.is_le, MUL)
                    tt(gt, gt, eq, ADD)
                    v.tensor_scalar(Dv["bias"][:, qt, 0:n], gt, -NEG, NEG, MUL, ADD).then_inc(S["d_bias"], 1)
                    dve.wait_ge(S["d_bias"], reached("d_bias"))
                    merge(l)
                merge(l)
                attention(l, "d", Dv, C ** -0.5, lambda qt: Dv["bias"][:, qt, 0:(qt + 1) * P] if qt else cst("causal"), 0)

                dve.wait_ge(tab_m_here, 16 * (l + 1))
                rp = slice(64, 96)
                cos, sin = Mv["tab"][rp, 0, :], Mv["tab"][rp, 1, :]
                link(v.memset(Mv["bias"], 0.0))
                v.tensor_copy(Mv["bias"][:, 3 * P:T], cst("causal")).then_inc(S["m_bias"], 1)
                dve.wait_ge(S["m_bias"], reached("m_bias"))
                dve.wait_ge(S["m_in"], at(l, "m_in", 2))
                tt(Mv["sq"][:, 0:2, :], Mv["cq"], Mv["cq"], MUL)
                v.tensor_tensor(Mv["sq"][:, 2, :], misc[:, 0, :], misc[:, 0, :], MUL).then_inc(S["m_sq"], 1)
                dve.wait_ge(S["m_sq"], reached("m_sq"))
                merge(l)
                dve.wait_ge(v_full, filled.next())
                b = filled.bank()
                v.tensor_scalar(Mv["rs"][:, 0, :], b[:], 1.0 / 256, EPS, MUL, ADD).then_inc(S["m_nv"], 1)
                dve.wait_ge(S["m_nv"], reached("m_nv"))
                dve.wait_ge(v_full, filled.next())
                b = filled.bank()
                v.tensor_scalar(Mv["rs"][:, 1, :], b[:], 1.0 / 128, EPS, MUL, ADD).then_inc(S["m_nv"], 1)
                dve.wait_ge(S["m_nv"], reached("m_nv"))
                v.reciprocal(Mv["rs"], Mv["rs"]).then_inc(S["m_rec"], 1)
                dve.wait_ge(S["m_rec"], reached("m_rec"))
                dve.wait_ge(S["m_rs"], at(l, "m_rs", 1))
                for f in range(2):
                    stt(Mv["cq"][:, f, :], Mv["cq"][:, f, :], pr("q_g", f), Mv["rs"][:, 0, :], MUL, MUL)
                v.scalar_tensor_tensor(misc[:, 0, :], misc[:, 0, :], pr("kv_g", 0), Mv["rs"][:, 1, :], MUL, MUL).then_inc(S["m_c"], 1)
                dve.wait_ge(S["m_c"], reached("m_c"))
                merge(l)
                dve.wait_ge(v_full, filled.next())
                b = filled.bank()
                v.tensor_tensor(Mv["tmp"][rp, :], b[rp, :], sin, MUL).then_inc(S["m_krb"], 1)
                dve.wait_ge(S["m_krb"], reached("m_krb"))
                tt(Mv["kr"][rp, :], misc[rp, 1, :], cos, MUL)
                for h in range(H):
                    v.tensor_tensor(Mv["k"][rp, h, :], Mv["kr"][rp, :], Mv["tmp"][rp, :], ADD).then_inc(S["m_kr"], 1)
                    dve.wait_ge(S["m_kr"], reached("m_kr"))
                for h in range(H):
                    dve.wait_ge(v_full, filled.next())
                    b = filled.bank()
                    tt(Mv["tmp"][rp, :], b[rp, :], sin, MUL)
                    x_ = Mv["q"][rp, h, :]
                    tt(x_, x_, cos, MUL)
                    v.tensor_tensor(x_, x_, Mv["tmp"][rp, :], ADD).then_inc(S["m_rot"], 1)
                    dve.wait_ge(S["m_rot"], reached("m_rot"))
                merge(l)
                merge(l)
                attention(l, "m", Mv, 96 ** -0.5, lambda qt: Mv["bias"][:, (3 - qt) * P:T], 1)
                for i in range(5):
                    if i < 4:
                        merge(l)
                    if i >= 1:
                        for m in range(2 * i - 2, 2 * i):
                            dve.wait_ge(S["mg_hi"], at(l, "mg_hi", m + 1))
                            v.tensor_tensor(mg_lo[:, m, :], mg[:, m, :], mg_hi[:, m, :].bitcast(F32), SUB).then_inc(S["mg_lo"], 1)
                dve.wait_ge(x_back, 16 * (l + 1))
                for m in range(KT):
                    dve.wait_ge(v_full, filled.next())
                    b = filled.bank()
                    v.tensor_tensor(xT[:, m, :], xT[:, m, :], b[:], ADD).then_inc(S["wo_done"], 1)
                    dve.wait_ge(S["wo_done"], reached("wo_done"))
                norm(2 * l + 1, "mlp_g")
                for q in range(QUARTERS + 1):
                    if q < QUARTERS:
                        for i in range(8):
                            n = 8 * q + i
                            dve.wait_ge(S["up_relu"], at(l, "up_relu", n + 1))
                            v.tensor_tensor(relu2[:, n % 2, :], relu[:, n % 2, :], relu[:, n % 2, :], MUL).then_inc(S["up_sq"], 1)
                            dve.wait_ge(S["up_sq"], reached("up_sq"))
                            dve.wait_ge(S["up_hi"], at(l, "up_hi", n + 1))
                            v.tensor_tensor(up_lo[q % 2][:, i, :], relu2[:, n % 2, :], up_hi[q % 2][:, i, :].bitcast(F32), SUB).then_inc(S["up_done"], 1)
                            dve.wait_ge(S["up_done"], reached("up_done"))
                    if q >= 1:
                        for m in range(KT):
                            dve.wait_ge(v_full, filled.next())
                            b = filled.bank()
                            v.tensor_tensor(xT[:, m, :], xT[:, m, :], b[:], ADD).then_inc(S["down_done"], 1)
                            dve.wait_ge(S["down_done"], reached("down_done"))
            norm(2 * L, "fin_g", False)


def stream_layout(w):
    out = np.zeros((L * NU, P, SLOT), np.float32)
    w_outs = [w["w_out_gdn"], w["w_out_mla"], w["w_out_rwkv"], w["w_out_dsa"]]

    def tiles(a):
        return a.reshape(-1, P, a.shape[1]).transpose(1, 0, 2)

    for l in range(L):
        wi = w["w_in"][l]
        for u, unit in enumerate(UNITS):
            dst = out[l * NU + u].reshape(P, 10, P)
            kind, i = unit[0], unit[-1]
            if kind == "rw":
                dst[:, 0:8] = tiles(wi[:, RWK0 + P * i:RWK0 + P * (i + 1)])
            elif kind == "gd":
                c = GDN0 + P * i if i < 6 else GDN0 + 776 + P * (i - 6)
                dst[:, 0:8] = tiles(wi[:, c:c + P])
            elif kind == "misc":
                parts = ((MLA0 + 256, 128),) if i == 0 else ((DSA0 + 512, 64), (MLA0 + 384, 32), (GDN0 + 768, 8), (DSA0 + 576, 8))
                at = 0
                for c, n in parts:
                    dst[:, 0:8, at:at + n] = tiles(wi[:, c:c + n])
                    at += n
            elif kind == "ds":
                c = DSA0 + (P * i if i < 4 else 584 + P * (i - 4))
                dst[:, 0:8] = tiles(wi[:, c:c + P])
            elif kind == "cq":
                dst[:, 0:8] = tiles(wi[:, MLA0 + P * i:MLA0 + P * (i + 1)])
            elif kind == "merge":
                br = unit[1]
                c = GATE0 + D * br + P * i
                dst[:, 0:8] = tiles(wi[:, c:c + P])
                dst[:, 8:10] = tiles(w_outs[br][l][:, P * i:P * (i + 1)])
            elif kind == "wo":
                dst[:, 0:8] = tiles(w["w_o"][l][:, P * i:P * (i + 1)])
            elif kind == "up":
                dst[:, 0:8] = tiles(w["w_up"][l][:, P * i:P * (i + 1)])
            else:
                q = unit[1]
                dst[:, 0:8] = tiles(w["w_down"][l][D * q:D * (q + 1), P * i:P * (i + 1)])
    return out


def par_layout(w):
    out = np.zeros((L, P, NPAR), np.float32)

    def put(l, name, a):
        at, n = PAR[name]
        out[l, :, at:at + n] = a

    for l in range(L):
        col = lambda a: a.reshape(-1, P).T
        put(l, "mix_g", col(w["mix_norm_g"][l]))
        put(l, "mlp_g", col(w["mlp_norm_g"][l]))
        put(l, "fin_g", col(w["final_norm_g"]))
        put(l, "conv", w["gdn_conv_w"][l].reshape(4, 6, P).transpose(2, 1, 0).reshape(P, 24))
        put(l, "mu", col(w["rwkv_mu"][l]))
        for name, key in (("w0", "rwkv_w0"), ("a0", "rwkv_a0"), ("k_k", "rwkv_k_k"), ("k_a", "rwkv_k_a"),
                          ("ln_w", "rwkv_ln_w"), ("ln_b", "rwkv_ln_b"), ("q_g", "mla_q_norm_g"), ("kv_g", "mla_kv_norm_g")):
            put(l, name, col(w[key][l]))
        put(l, "r_k", col(w["rwkv_r_k"][l].reshape(-1)))
        put(l, "gdn_g", np.concatenate([w["gdn_norm_g"][l]] * 2)[:, None])
        put(l, "a_log", np.broadcast_to(w["gdn_a_log"][l], (P, H)))
        put(l, "dt", np.broadcast_to(w["gdn_dt_bias"][l], (P, H)))
        put(l, "wa2", np.concatenate([w["rwkv_w_w2"][l], w["rwkv_w_a2"][l]]))
        put(l, "g2", w["rwkv_w_g2"][l])
        put(l, "uq", w["mla_w_uq"][l].reshape(2, P, 384).transpose(1, 0, 2).reshape(P, 768))
        put(l, "ukv", w["mla_w_ukv"][l])
    return out


def kernel(**inputs):
    import concourse.bacc as bacc
    from concourse.bass_utils import run_bass_kernel_spmd as run

    w = {k: np.asarray(a) for k, a in inputs.items()}
    arrays = {
        "in_x": np.ascontiguousarray(w["x"][0]),
        "in_pos": np.ascontiguousarray(w["positions"][0]),
        "in_w": stream_layout(w),
        "in_par": par_layout(w),
        "in_const": CONST_ARRAY,
    }
    nc = bacc.Bacc("TRN2", target_bir_lowering=False, num_devices=1)
    aps = [nc.dram_tensor(n, a.shape, mybir.dt.from_np(a.dtype), kind="ExternalInput").ap() for n, a in arrays.items()]
    tabs = nc.dram_tensor("tabs", (2, 2, P, T), F32, kind="Internal").ap()
    x_dram = nc.dram_tensor("x_dram", (P, KT, T), F32, kind="Internal").ap()
    out = nc.dram_tensor("out_x", (T, D), F32, kind="ExternalOutput").ap()
    build(nc, *aps, tabs, x_dram, out)
    r = run(nc, [arrays], core_ids=[0])
    return r.results[0]["out_x"].reshape(1, T, D)
```

```python
from contextlib import ExitStack

import numpy as np

import concourse.bass as bass
from concourse import mybir

ALU = mybir.AluOpType
ACT = mybir.ActivationFunctionType
F32 = mybir.dt.float32
F32R = mybir.dt.float32r
I32 = mybir.dt.int32
AX_X = mybir.AxisListType.X

P = 128
T = 512
D = 1024
L = 2
KT = D // P
TT = T // P
C = 64
NC = T // C
H = 4
M = TT * H
FF = 4096
EPS = 1e-6
GN_EPS = 64e-5
TOPK = 128
NEG = -1e30
DECAY = float(np.exp(-0.5))
MAGIC = 12582912.0
TWO_PI = (6.28125, 0.0019350051879882812, 3.0199159819e-07)
RW_ORDER = (6, 7, 2, 3, 0, 1, 4, 5)
LEVELS = (2, 4, 8, 16, 32)

GDN0, MLA0, RWK0, DSA0, GATE0 = 0, 1032, 1448, 2472, 3824

SLOT = 10 * P
RING = 3
OUT_RING = 6
SPLIT = 2
QUARTERS = 4


def unit_list():
    u = [("rw", i) for i in range(8)] + [("misc", i) for i in range(2)]
    u += [("gd", i) for i in range(8)]
    u += [("merge", 2, i) for i in range(8)]
    u += [("ds", i) for i in range(10)]
    u += [("merge", 0, i) for i in range(4)]
    u += [("cq", i) for i in range(2)]
    u += [("merge", 0, i) for i in range(4, 8)]
    u += [("merge", 3, i) for i in range(8)]
    u += [("merge", 1, i) for i in range(8)]
    u += [("wo", i) for i in range(8)]
    for q in range(QUARTERS + 1):
        if q < QUARTERS:
            u += [("up", 8 * q + i) for i in range(8)]
        if q >= 1:
            u += [("down", q - 1, i) for i in range(8)]
    return u


UNITS = unit_list()
NU = len(UNITS)

GATE_STEPS = tuple(range(1, 13))

CONST = {}


def _constants():
    n = np.arange(P)
    blk = n[:, None] // C == n[None, :] // C
    parts = [
        ("ident", np.eye(P)),
        ("ones", np.ones((P, P))),
        ("blocks", blk),
        ("upto", blk & (n[:, None] <= n[None, :])),
        ("before", blk & (n[:, None] < n[None, :])),
        ("after", blk & (n[:, None] > n[None, :])),
    ]
    i, j = n[:, None], n[None, :]
    level = lambda s: (i // (2 * s) == j // (2 * s)) & (i % (2 * s) >= s) & (j % (2 * s) < s)
    parts.append(("first", -1.0 * level(1).T))
    for s in LEVELS:
        parts.append((f"level{s}", level(s)))
    parts.append(("causal", np.where(n[None, :] <= n[:, None], 0.0, NEG)))

    def rotate(dims, start, width):
        r = np.zeros((P, P))
        for b in range(start, P, width):
            for e in range(dims // 2):
                if b + dims <= P:
                    r[b + dims // 2 + e, b + e] = -1.0
                    r[b + e, b + dims // 2 + e] = 1.0
        return r

    rot_m = np.zeros((P, P))
    rot_m[64:96, 64:96] = rotate(32, 0, P)[:32, :32]
    rot_d = rotate(16, 0, C)
    dup = np.zeros((P, P))
    dup[:C, :] = (np.arange(C)[:, None] == (n % C)[None, :])
    parts += [("rot_m", rot_m), ("rot_d", rot_d), ("dup", dup), ("dup_rot", dup @ rot_d)]
    fm = np.zeros(P, np.float32)
    inv_m = (np.float32(500000.0) ** (-np.arange(0, 32, 2, dtype=np.float32) / np.float32(32))).astype(np.float32)
    fm[64:80] = inv_m
    fm[80:96] = inv_m
    fd = np.zeros(P, np.float32)
    inv_d = (np.float32(500000.0) ** (-np.arange(0, 16, 2, dtype=np.float32) / np.float32(16))).astype(np.float32)
    for b in (0, C):
        fd[b:b + 8] = inv_d
        fd[b + 8:b + 16] = inv_d
    parts += [("freq_d", fd[:, None]), ("freq_m", fm[:, None])]
    at, cols = 0, []
    for name, a in parts:
        a = np.asarray(a, np.float32)
        CONST[name] = (at, a.shape[1])
        at += a.shape[1]
        cols.append(a)
    return np.ascontiguousarray(np.concatenate(cols, axis=1))


CONST_ARRAY = _constants()
NCONST = CONST_ARRAY.shape[1]

PAR = {}
_at = 0
for _n, _w in (("mix_g", 8), ("mlp_g", 8), ("fin_g", 8), ("conv", 24), ("mu", 8), ("w0", 2), ("a0", 2), ("k_k", 2),
               ("k_a", 2), ("r_k", 2), ("ln_w", 2), ("ln_b", 2), ("gdn_g", 1), ("q_g", 2), ("kv_g", 1),
               ("a_log", 4), ("dt", 4), ("wa2", 256), ("g2", 256), ("uq", 768), ("ukv", 512)):
    PAR[_n] = (_at, _w)
    _at += _w
NPAR = _at


def build(nc, x_in, pos_in, wstream, par_in, const_in, tabs, x_dram, out):
    ctx = ExitStack()
    with ctx:
        def sb(name, shape, dt=F32):
            return ctx.enter_context(nc.sbuf_tensor(name, shape, dt))

        def sem(name):
            return ctx.enter_context(nc.semaphore(name))

        h_hi = sb("h_hi", [P, KT, T], F32R)
        h_lo = sb("h_lo", [P, KT, T], F32R)
        mg = sb("mg", [P, KT, T])
        ring = sb("ring", [P, RING, KT, P])
        out_ring = sb("out_ring", [P, OUT_RING, 2, P])
        w_hi = sb("w_hi", [P, SPLIT, KT, P], F32R)
        w_lo = sb("w_lo", [P, SPLIT, KT, P], F32R)
        consts = sb("consts", [P, NCONST])
        par = sb("par", [P, NPAR])
        yo = sb("yo", [P, 2, 2, T])
        misc = sb("misc", [P, 2, T])
        sg = sb("sg", [P, 2, T])
        s_z = sb("s_z", [P, 2, 2, C])
        un_z = sb("un_z", [P, 2, 4 * C])
        pc = sb("pc", [P, 2, NC])
        ab = sb("ab", [P, TT, 16])
        gsm = sb("gsm", [P, 6, M])
        m8 = sb("m8", [P, 8])
        sml = sb("sml", [P, 16])
        att = sb("att", [P, 3, 4])
        AQ = 45
        with nc.sbuf_tensor("arena", [P, AQ * T], F32) as arena:
            pass
        parts = sb("parts", [P, 4, KT, T], F32R)

        def ar(q, shape, at=0):
            n = int(np.prod(shape))
            v = arena[:, q * T + at:q * T + at + n]
            if len(shape) == 1:
                return v
            names = " ".join("abcd"[:len(shape)])
            return v.rearrange(f"p ({names}) -> p {names}", **{k: s for k, s in zip("abcd", shape)})

        xT = ar(AQ - KT, (KT, T))

        def cst(name):
            a, w = CONST[name]
            return consts[:, a:a + w]

        def pr(name, i=None):
            a, w = PAR[name]
            return par[:, a:a + w] if i is None else par[:, a + i:a + i + 1]

        bank_a = [ctx.enter_context(nc.psum_tensor(f"bank_a{i}", [P, T], F32)) for i in range(3)]
        bank_v = [ctx.enter_context(nc.psum_tensor(f"bank_v{i}", [P, T], F32)) for i in range(4)]

        bank_f = [ctx.enter_context(nc.psum_tensor("bank_f", [P, T], F32))]

        S, per = {}, {}

        def ev(name, n):
            S[name] = sem(name)
            per[name] = n

        a_full = sem("a_full")
        f_full = sem("f_full")
        v_full = sem("v_full")
        out_here = [sem(f"out_here{i}") for i in range(OUT_RING)]
        w_here = [sem(f"w_here{i}") for i in range(RING)]
        x_away = sem("x_away")
        x_back = sem("x_back")
        const_here = sem("const_here")
        more_here = sem("more_here")
        par_here = sem("par_here")
        x_here = [sem(f"x_here{i}") for i in range(2)]
        pos_here = sem("pos_here")
        tab_out = sem("tab_out")
        tab_d_here = sem("tab_d_here")
        tab_m_here = sem("tab_m_here")
        out_done = sem("out_done")
        dve_step = sem("dve_step")
        act_step = sem("act_step")
        for name, n in (
            ("split_hi", NU), ("split_lo", NU),
            ("n_sq", 16), ("n_var", 2), ("n_rec", 2), ("n_rs", 2), ("n_g", 16), ("n_hi", 16), ("n_h", 16),
            ("x_t", 0), ("o_tok", 0), ("tab", 0), ("tab_sin", 0), ("tab_arg", 0),
            ("r_in", 8), ("r_zero", 1), ("r_mix", 8), ("r_act", 2), ("r_lora", 6), ("r_cum", 1), ("r_dec", 3),
            ("r_ex", 1), ("r_sq", 1), ("r_l2", 2), ("r_l2r", 1), ("r_l2s", 1), ("r_bsq", 2), ("r_bon", 2), ("r_feat", 4),
            ("r_tok", 8), ("r_mat", 16), ("r_x1", TT), ("r_ti", TT), ("r_y", 5 * TT), ("r_t", 4 * TT), ("r_x", 5 * TT),
            ("r_wt", 2), ("r_y1", TT), ("r_u", TT), ("r_ws", NC), ("r_s", NC), ("r_o", NC),
            ("r_mean", 2), ("r_sq2", 1), ("r_gv", 2), ("r_gr", 1), ("r_gs", 1), ("r_out", 1),
            ("g_in", 6), ("g_z", 2), ("g_conv", 6), ("g_sig", 6), ("g_sq", 1), ("g_l2", 4),
            ("g_l2r", 1), ("g_l2s", 1), ("g_qk", 1), ("g_t1", 1), ("g_sp", 1), ("g_t2", 1), ("g_g", 2), ("g_feat", 6), ("g_gc", 1),
            ("g_row", 4), ("g_d", 4), ("g_prep", 2),
            ("g_tok", 6), ("g_mat", 8), ("g_x1", TT), ("g_ti", TT), ("g_y", 5 * TT), ("g_t", 4 * TT), ("g_x", 5 * TT),
            ("g_wt", 2), ("g_u", TT), ("g_ws", NC), ("g_s", NC), ("g_o", NC),
            ("g_sq2", 1), ("g_gv", 2), ("g_gr", 1), ("g_gs", 1), ("g_out", 1),
            ("misc_in", 2), ("ab_in", 1),
            ("d_in", 8), ("d_vf", 2), ("d_v", 2), ("d_ik", 2), ("d_rot", 8), ("d_sc", 24), ("d_acc", 24), ("d_bias", 4),
            ("d_ss", 16), ("d_p", 16), ("d_pn", 16), ("d_pt", 16), ("d_o", 16), ("d_kz", 2),
            ("m_in", 2), ("m_sq", 1), ("m_nv", 2), ("m_rec", 1), ("m_rs", 1), ("m_c", 1), ("m_q", 4), ("m_k", 4), ("m_v", 2),
            ("m_rot", 4), ("m_kr", 4), ("m_krb", 1),
            ("m_bias", 1),
            ("m_ss", 16), ("m_p", 16), ("m_pn", 16), ("m_pt", 16), ("m_o", 16),
            ("mg_sig", 32), ("mg_raw", 4), ("mg_done", 32), ("mg_hi", 8), ("mg_lo", 8), ("wo_done", 8), ("up_relu", 32), ("up_sq", 32), ("up_hi", 32), ("up_done", 32), ("g_zs", 1), ("r_s0", 1), ("g_s0", 1), ("down_done", 8 * QUARTERS),
        ):
            ev(name, n)

        def at(l, name, k):
            return l * per[name] + k

        class Banks:

            def __init__(self):
                self.pools = {"a": bank_a, "v": bank_v, "f": bank_f}
                self.used = {"a": 0, "v": 0, "f": 0}
                self.reader = {pool: [(const_here, 16)] * 4 for pool in "avf"}
                self.counts = {}

            def next(self, pool, done):
                i = self.used[pool] % len(self.pools[pool])
                self.used[pool] += 1
                sem_, value = self.reader[pool][i]
                self.counts[done] = self.counts.get(done, 0) + 1
                self.reader[pool][i] = (S[done], self.counts[done])
                return self.pools[pool][i], sem_, value

        class Filled:

            def __init__(self, banks):
                self.n, self.banks = 0, banks

            def next(self):
                self.n += 1
                return self.n

            def bank(self):
                return self.banks[(self.n - 1) % len(self.banks)]

        def own_half(view, parts, i):
            return view.rearrange("p (f x c) -> p f x c", f=2, x=parts)[:, :, i, :]

        def merges_to(g):
            return sum(UNITS[i % NU][0] == "merge" for i in range(g))

        block = ctx.enter_context(nc.Block())

        R = dict(
            rw=ar(0, (4, T + 1)), rm=ar(9, (8, T)), sw=ar(5, (2, T)), cs=ar(7, (2, T)), a=ar(35, (2, T)), g=ar(29, (2, T)),
            p=ar(17, (2, T)), pi=ar(19, (2, T)), pe=ar(21, (2, T)), kk=ar(23, (2, T)), tmp=ar(25, (2, T)),
            rt=ar(27, (2, T)), et=ar(0, (2, T)), bz=ar(31, (2, 2, T)), kz=ar(35, (2, 2, T)),
            bh=ar(39, (2, T)), kh=ar(41, (2, T)), bon=ar(43, (2, T)),
            e_tok=ar(17, (TT, 256)), v_tok=ar(19, (TT, 256)), b_tok=ar(21, (TT, 256)), k_tokz=ar(23, (TT, 2, 256)),
            u=ar(9, (M, P)), ark=ar(0, (M, P)), arb=ar(4, (M, P)), akk=ar(39, (M, P)),
            x_bd=ar(31, (M, P)), y_bd=ar(35, (M, P)), t_bd=ar(13, (M, P)),
            wt=ar(13, (2, T)), y1=ar(15, (TT, 256)), up=ar(17, (TT, 256)), o=ar(9, (2, T)), sq=ar(11, (2, T)),
        )
        G = dict(
            ci=mg[:, 0:6, :], zi=mg[:, 4:6, :], co=ar(31, (6, T)), z=ar(13, (2, T)), sig=ar(37, (6, T)), sq=ar(0, (4, T)), rs=ar(37, (4, T)),
            egc=ar(15, (2, T)), ers=ar(17, (2, T)), beta=ar(19, (2, T)), kb=ar(0, (2, T)), rt=ar(2, (2, T)), et=ar(4, (2, T)),
            bh=ar(21, (2, T)), vb=ar(23, (2, T)), kz=ar(25, (2, 2, T)), d=ar(7, (M, P)), u=ar(37, (M, P)), arb=ar(41, (M, P)),
            e_tok=ar(15, (TT, 256)), v_tok=ar(19, (TT, 256)), b_tok=ar(17, (TT, 256)),
            x_bd=ar(25, (M, P)), y_bd=ar(29, (M, P)), t_bd=ar(7, (M, P)),
            wt=ar(0, (2, T)), up=ar(4, (TT, 256)), o=ar(7, (2, T)), sq2=ar(9, (2, T)),
            g_wide=ar(41, (M * C,)), b_wide=ar(43, (M * C,)),
        )
        conv_out = lambda c: mg[:, (c + 6) % 8, :]
        Dv = dict(
            rl=ar(0, (2, T)), sc=ar(2, (T,)), wk=ar(3, (T,)), gt=ar(4, (T,)), eq=ar(5, (T,)), cum=ar(6, (T,)), bias=ar(7, (TT, T)),
            ss=ar(11, (4, T)), iq=ar(15, (4, T)), q=ar(19, (2, T)), k=ar(21, (2, T)), vf=ar(23, (2, T)), pt=ar(23, (2, TT, P)),
            v=ar(25, (TT, 256)), tab=ar(27, (2, T)), ikz=ar(29, (2, T)), kz=ar(31, (2, 2, T)), tmp=ar(35, (T,)),
        )
        Mv = dict(
            cq=ar(37, (2, T)), sq=ar(2, (3, T)), rs=ar(5, (2, T)), q=ar(7, (4, T)), k=ar(11, (4, T)), v=ar(15, (TT, 256)),
            tab=ar(17, (2, T)), tmp=ar(19, (T,)), bias=ar(20, (T,)), kr=ar(21, (T,)),
            ss=ar(22, (4, T)), pt=ar(26, (2, TT, P)),
        )
        xin = ar(0, (TT, D))
        xout = ar(0, (TT, D))
        mg_hi, mg_lo = parts[:, 0], parts[:, 1]
        up_hi = [parts[:, 0], parts[:, 2]]
        up_lo = [parts[:, 1], parts[:, 3]]
        relu = ar(32, (2, T))
        relu2 = ar(34, (2, T))
        squares = [ar(8, (KT, T)), ar(16, (KT, T))]
        POS = dict(i=ar(20, (T,)).bitcast(I32), f=ar(21, (T,)), ang=ar(22, (T,)), k=ar(23, (T,)), sin=ar(24, (2, T)), cos=ar(26, (2, T)),
                   red=ar(28, (2, T)))
        rotors = ("d", "m")

        @block.sync
        def _(sp):
            sp.dma_start(consts[:, 0:2 * P], const_in[:, 0:2 * P]).then_inc(const_here, 16)
            for half in range(2):
                cols = slice(half * D // 2, (half + 1) * D // 2)
                sp.dma_start(xin[:, :, cols], x_in.rearrange("(t p) d -> p t d", p=P)[:, :, cols]).then_inc(x_here[half], 16)
            sp.dma_start(consts[:, 2 * P:], const_in[:, 2 * P:]).then_inc(more_here, 16)
            sp.dma_start(POS["i"], pos_in.partition_broadcast(P)).then_inc(pos_here, 16)
            for g in range(L * NU):
                l, u = divmod(g, NU)
                if g >= RING:
                    sp.wait_ge(S["split_lo"], g - RING + 1)
                sp.dma_start(ring[:, g % RING, :, :], wstream[g, :, 0:KT * P].rearrange("p (k n) -> p k n", n=P)).then_inc(w_here[g % RING], 16)
                if UNITS[u][0] == "merge":
                    n = merges_to(g)
                    if n >= OUT_RING:
                        sp.wait_ge(S["mg_done"], n - OUT_RING + 1)
                    sp.dma_start(out_ring[:, n % OUT_RING, :, :], wstream[g, :, KT * P:].rearrange("p (k n) -> p k n", n=P)).then_inc(out_here[n % OUT_RING], 16)
                if UNITS[u] == ("rw", 4):
                    if l == 0:
                        sp.wait_ge(S["x_t"], 8)
                    else:
                        sp.wait_ge(S["down_done"], at(l - 1, "down_done", 8 * QUARTERS))
                    sp.dma_start(x_dram, xT).then_inc(x_away, 16)
                if UNITS[u] == ("merge", 1, 0):
                    sp.wait_ge(S["m_q"], at(l, "m_q", H))
                    sp.wait_ge(x_away, 16 * (l + 1))
                    sp.dma_start(xT, x_dram).then_inc(x_back, 16)
            for half in range(2):
                cols = slice(half * D // 2, (half + 1) * D // 2)
                sp.wait_ge(S["o_tok"], TT * (half + 1))
                sp.dma_start(out.rearrange("(t p) d -> p t d", p=P)[:, :, cols], xout[:, :, cols]).then_inc(out_done, 16)
            sp.wait_ge(out_done, 32)

        @block.gpsimd
        def _(pool):
            pool.dma_start(par[:], par_in[0]).then_inc(par_here, 16)
            for g in range(L * NU):
                l, u = divmod(g, NU)
                pool.wait_ge(S["split_hi"], g + 1)
                for half in range(2):
                    ks = slice(4 * half, 4 * half + 4)
                    raw = ring[:, g % RING, ks, :]
                    ins = nc.gpsimd.tensor_tensor(w_lo[:, g % SPLIT, ks, :], raw, w_hi[:, g % SPLIT, ks, :].bitcast(F32), ALU.subtract)
                ins.then_inc(S["split_lo"], 1)
                if g == 3:
                    for i in range(2):
                        pool.wait_ge(S["tab"], i + 1)
                        pool.dma_start(tabs[i, 0], POS["cos"][:, i, :]).then_inc(tab_out, 16)
                        pool.dma_start(tabs[i, 1], POS["sin"][:, i, :]).then_inc(tab_out, 16)
                if UNITS[u] == ("ds", 0):
                    pool.wait_ge(tab_out, 64)
                    pool.wait_ge(S["g_u"], at(l, "g_u", TT))
                    pool.dma_start(Dv["tab"], tabs[0].rearrange("k p t -> p k t")).then_inc(tab_d_here, 16)
                if UNITS[u] == ("merge", 3, 2):
                    pool.wait_ge(S["d_o"], at(l, "d_o", 16))
                    pool.dma_start(Mv["tab"], tabs[1].rearrange("k p t -> p k t")).then_inc(tab_m_here, 16)
                if UNITS[u] == ("up", 2) and l + 1 < L:
                    pool.wait_ge(S["n_g"], at(l, "n_g", 16))
                    pool.dma_start(par[:], par_in[l + 1]).then_inc(par_here, 16)

        @block.tensor
        def _(pe):
            mm = nc.tensor.matmul
            banks = Banks()
            unit = [0]

            def begin_unit(want, l):
                g = unit[0]
                assert UNITS[g % NU] == want and g // NU == l, (UNITS[g % NU], want)
                unit[0] += 1
                pe.wait_ge(S["split_hi"], g + 1)
                return g

            def split_product(g, b, hi, lo, sem_name=None, k0=0):
                s = g % SPLIT
                for k in range(KT):
                    if sem_name:
                        pe.wait_ge(S[sem_name], k0 + k + 1)
                    mm(b[:], w_hi[:, s, k, :], hi[:, k, :], start=k == 0, stop=False)
                    mm(b[:], w_hi[:, s, k, :], lo[:, k, :], start=False, stop=False)
                pe.wait_ge(S["split_lo"], g + 1)
                for k in range(KT):
                    ins = mm(b[:], w_lo[:, s, k, :], hi[:, k, :], start=False, stop=k == KT - 1)
                return ins

            def feat_group(want, l, hi, lo, pool, done, sem_name=None, k0=0):
                g = begin_unit(want, l)
                b, reader, emptied = banks.next(pool, done)
                pe.wait_ge(reader, emptied)
                split_product(g, b, hi, lo, sem_name, k0).then_inc(a_full if pool == "a" else v_full, 1)

            def norm_sum(n):
                b, reader, emptied = banks.next("v", "n_var")
                pe.wait_ge(reader, emptied)
                for k in range(KT):
                    pe.wait_ge(S["n_sq"], n * KT + k + 1)
                    ins = mm(b[:], cst("ones"), squares[n % 2][:, k, :], start=k == 0, stop=k == KT - 1)
                ins.then_inc(v_full, 1)

            def gates(l, br, i):
                numbers = []
                for j in range(2):
                    g = begin_unit(("merge", br, 2 * i + j), l)
                    numbers.append(merges_to(g))
                    b, reader, emptied = banks.next("a", "mg_sig")
                    pe.wait_ge(reader, emptied)
                    split_product(g, b, h_hi, h_lo).then_inc(a_full, 1)
                return numbers

            def merge(l, br, slot, i, output=None):
                numbers = gates(l, br, i)
                if output:
                    pe.wait_ge(S[output], at(l, output, per[output]))
                merge_outputs(slot, numbers)

            def merge_outputs(slot, numbers):
                for j in range(2):
                    b, reader, emptied = banks.next("v", "mg_done")
                    pe.wait_ge(reader, emptied)
                    n = numbers[j]
                    pe.wait_ge(out_here[n % OUT_RING], 16 * (n // OUT_RING + 1))
                    for k in range(2):
                        ins = mm(b[:], out_ring[:, n % OUT_RING, k, :], yo[:, slot, k, :], start=k == 0, stop=k == 1)
                    ins.then_inc(v_full, 1)

            def gate_pieces(l, br, i, numbers):
                for j in range(2):
                    g = begin_unit(("merge", br, 2 * i + j), l)
                    numbers.append(merges_to(g))
                    b, reader, emptied = banks.next("f", "mg_raw")
                    banks.counts["mg_sig"] += 1
                    pe.wait_ge(reader, emptied)
                    for k in range(KT):
                        mm(b[:], w_hi[:, g % SPLIT, k, :], h_hi[:, k, :], start=k == 0, stop=False)
                        mm(b[:], w_hi[:, g % SPLIT, k, :], h_lo[:, k, :], start=False, stop=False)
                        if k % 2 == 1:
                            yield
                    pe.wait_ge(S["split_lo"], g + 1)
                    for k in range(KT):
                        ins = mm(b[:], w_lo[:, g % SPLIT, k, :], h_hi[:, k, :], start=False, stop=k == KT - 1)
                        if k == 3:
                            yield
                    ins.then_inc(f_full, 1)
                    yield

            def transposes(srcs, x):
                for s in srcs:
                    for half in range(2):
                        b, reader, emptied = banks.next("a", x + "_tok")
                        pe.wait_ge(reader, emptied)
                        for t2 in range(2):
                            for f in range(2):
                                c = t2 * 256 + f * P
                                t = 2 * half + t2
                                ins = nc.tensor.transpose(b[:, c:c + P], s[:, f, t * P:(t + 1) * P], cst("ident"))
                        ins.then_inc(a_full, 1)

            def pair_matrices(lz, rhs, x):
                for t in range(TT):
                    b, reader, emptied = banks.next("v", x + "_mat")
                    pe.wait_ge(reader, emptied)
                    for h in range(H):
                        ins = mm(b[:, h * P:(h + 1) * P], lz[:, h // 2, h % 2, t * P:(t + 1) * P],
                                 rhs[:, h // 2, t * P:(t + 1) * P], start=True, stop=True)
                    ins.then_inc(v_full, 1)

            def block_products(pool, done, t, lhs, rhs):
                b, reader, emptied = banks.next(pool, done)
                pe.wait_ge(reader, emptied)
                for h in range(H):
                    m = t * H + h
                    ins = mm(b[:, h * P:(h + 1) * P], lhs[:, m, :], rhs(m), start=True, stop=True)
                ins.then_inc(v_full if pool == "v" else a_full, 1)

            def of_pair(src):
                return lambda m: src[:, m // H, (m % H) // 2 * P:((m % H) // 2 + 1) * P]

            def invert(l, x, V, fill):
                for t in range(TT):
                    b, reader, emptied = banks.next("a", x + "_ti")
                    pe.wait_ge(reader, emptied)
                    pe.wait_ge(S[x + "_x1"], at(l, x + "_x1", t + 1))
                    for h in range(H):
                        ins = nc.tensor.transpose(b[:, h * P:(h + 1) * P], V["x_bd"][:, t * H + h, :], cst("ident"))
                    ins.then_inc(a_full, 1)
                for n in range(len(LEVELS)):
                    for t in range(TT):
                        if n:
                            pe.wait_ge(S[x + "_t"], at(l, x + "_t", TT * (n - 1) + t + 1))
                        else:
                            pe.wait_ge(S[x + "_ti"], at(l, x + "_ti", t + 1))
                        block_products("v", x + "_y", t, V["u"], lambda m: V["t_bd"][:, m, :])
                    for t in range(TT):
                        pe.wait_ge(S[x + "_y"], at(l, x + "_y", TT * n + t + 1))
                        if n:
                            pe.wait_ge(S[x + "_x"], at(l, x + "_x", TT * (n - 1) + t + 1))
                        if n < len(LEVELS) - 1:
                            block_products("v", x + "_t", t, V["x_bd"], lambda m: V["y_bd"][:, m, :])
                    for t in range(TT):
                        block_products("v", x + "_x", t, V["y_bd"], lambda m: V["x_bd"][:, m, :])
                    fill(n)

            def through(l, x, V, rhs):
                pe.wait_ge(S[x + "_x"], at(l, x + "_x", TT * len(LEVELS)))
                for f in range(2):
                    b, reader, emptied = banks.next("a", x + "_wt")
                    pe.wait_ge(reader, emptied)
                    for t in range(TT):
                        for hp in range(2):
                            h = 2 * f + hp
                            ins = mm(b[hp * C:(hp + 1) * C, t * P:(t + 1) * P], V["e_tok"][:, t, h * C:(h + 1) * C],
                                     V["x_bd"][:, t * H + h, :], start=True, stop=True)
                    ins.then_inc(a_full, 1)
                for t in range(TT):
                    block_products("a", x + "_u", t, V["x_bd"], of_pair(rhs))

            def scan(l, x, V, fill):
                pe.wait_ge(S[x + "_s0"], at(l, x + "_s0", 1))
                pe.wait_ge(S[x + "_wt"], at(l, x + "_wt", 2))
                for c in range(NC):
                    t, par_ = divmod(c, 2)
                    rows = slice(par_ * C, (par_ + 1) * C)
                    if c:
                        pe.wait_ge(S[x + "_s"], at(l, x + "_s", c))
                    b, reader, emptied = banks.next("v", x + "_ws")
                    pe.wait_ge(reader, emptied)
                    for f in range(2):
                        ins = mm(b[rows, f * P:(f + 1) * P], V["wt"][:, f, c * C:(c + 1) * C],
                                 s_z[:, f, :, :], start=True, stop=True)
                    ins.then_inc(v_full, 1)
                    bo, reader, emptied = banks.next("a", x + "_o")
                    pe.wait_ge(reader, emptied)
                    bs, reader, emptied = banks.next("v", x + "_s")
                    pe.wait_ge(reader, emptied)
                    dst_o = [bo[h % 2 * C:(h % 2 + 1) * C, h // 2 * C:(h // 2 + 1) * C] for h in range(H)]
                    dst_s = [bs[h % 2 * C:(h % 2 + 1) * C, h // 2 * C:(h // 2 + 1) * C] for h in range(H)]
                    cols = [slice(h * C, (h + 1) * C) for h in range(H)]
                    for h in range(H):
                        mm(dst_o[h], s_z[:, h // 2, h % 2, :], V["rt"][:, h // 2, c * C:(c + 1) * C], start=h < 2, stop=False)
                        if "ark" in V:
                            mm(dst_o[h], V["v_tok"][:, t, cols[h]], V["ark"][:, t * H + h, rows], start=False, stop=False)
                            mm(dst_s[h], V["k_tokz"][:, t, par_, cols[h]], V["v_tok"][:, t, cols[h]], start=h < 2, stop=False)
                    pe.wait_ge(S[x + "_ws"], at(l, x + "_ws", c + 1))
                    for h in range(H):
                        ins = mm(dst_s[h], V["b_tok"][:, t, cols[h]], un_z[:, par_, cols[h]],
                                 start="ark" not in V, stop="ark" not in V or h >= 2)
                    ins.then_inc(v_full, 1)
                    for h in range(H):
                        ins = mm(dst_o[h], un_z[:, par_, cols[h]], V["arb"][:, t * H + h, rows], start=False, stop=h >= 2)
                    ins.then_inc(a_full, 1)
                    fill(c)

            def block_sums(l, need, k, src, tiles, done):
                pe.wait_ge(S[need], at(l, need, k))
                for i in range(tiles):
                    b, reader, emptied = banks.next("v", done)
                    pe.wait_ge(reader, emptied)
                    mm(b[:], cst("blocks"), src[:, i, :], start=True, stop=True).then_inc(v_full, 1)

            def attention(l, x, q_of, k_of, v, fill):
                steps = [(qt, h) for qt in range(TT) for h in range(H)]
                for i in range(len(steps) + 3):
                    if i < len(steps):
                        qt, h = steps[i]
                        b, reader, emptied = banks.next("v", x + "_ss")
                        pe.wait_ge(reader, emptied)
                        mm(b[:, 0:(qt + 1) * P], q_of(h, qt), k_of(h, (qt + 1) * P), start=True, stop=True).then_inc(v_full, 1)
                    if 2 <= i < len(steps) + 2:
                        j = i - 2
                        qt, h = steps[j]
                        b, reader, emptied = banks.next("a", x + "_pt")
                        pe.wait_ge(reader, emptied)
                        pe.wait_ge(S[x + "_pn"], at(l, x + "_pn", j + 1))
                        for k in range(qt + 1):
                            ins = nc.tensor.transpose(b[:, k * P:(k + 1) * P], V_ss(x)[:, j % 4, k * P:(k + 1) * P], cst("ident"))
                        ins.then_inc(a_full, 1)
                    if i >= 3:
                        j = i - 3
                        qt, h = steps[j]
                        b, reader, emptied = banks.next("v", x + "_o")
                        pe.wait_ge(reader, emptied)
                        pe.wait_ge(S[x + "_pt"], at(l, x + "_pt", j + 1))
                        rows = slice((h % 2) * C, (h % 2 + 1) * C)
                        for k in range(qt + 1):
                            ins = mm(b[rows, 0:P], v[:, k, h * C:(h + 1) * C], V_pt(x)[:, j % 2, k, :],
                                     start=k == 0, stop=k == qt)
                        ins.then_inc(v_full, 1)
                    fill(i)

            def V_ss(x):
                return (Dv if x == "d" else Mv)["ss"]

            def V_pt(x):
                return (Dv if x == "d" else Mv)["pt"]

            pe.wait_ge(const_here, 16)
            for k in range(KT):
                pe.wait_ge(x_here[k // 4], 16)
                b, reader, emptied = banks.next("v", "x_t")
                pe.wait_ge(reader, emptied)
                for t in range(TT):
                    ins = nc.tensor.transpose(b[:, t * P:(t + 1) * P], xin[:, t, k * P:(k + 1) * P], cst("ident"))
                ins.then_inc(v_full, 1)

            for l in range(L):
                norm_sum(2 * l)
                if l == 0:
                    pe.wait_ge(more_here, 16)
                rw = iter(range(8))

                def project_rw(count):
                    for _ in range(count):
                        i = next(rw)
                        if i == 0:
                            feat_group(("rw", i), l, h_hi, h_lo, "a", "r_in", "n_h", at(l, "n_h", 0))
                        else:
                            feat_group(("rw", i), l, h_hi, h_lo, "a", "r_in")

                def low_rank(weights, act_tile):
                    for f in range(2):
                        b, reader, emptied = banks.next("a", "r_lora")
                        pe.wait_ge(reader, emptied)
                        mm(b[:], weights[:, f * P:(f + 1) * P], act_tile, start=True, stop=True).then_inc(a_full, 1)

                project_rw(4)
                pe.wait_ge(S["r_act"], at(l, "r_act", 1))
                low_rank(pr("wa2")[0:64, :], R["rm"][0:64, 6, :])
                low_rank(pr("wa2")[64:128, :], R["rm"][64:128, 6, :])
                project_rw(1)
                block_sums(l, "r_sq", 1, R["tmp"], 2, "r_l2")
                pe.wait_ge(S["r_act"], at(l, "r_act", 2))
                low_rank(pr("g2"), R["rm"][:, 7, :])
                project_rw(3)
                for i in range(2):
                    feat_group(("misc", i), l, h_hi, h_lo, "a", "misc_in")
                b, reader, emptied = banks.next("a", "ab_in")
                pe.wait_ge(reader, emptied)
                pe.wait_ge(S["misc_in"], at(l, "misc_in", 2))
                for t in range(TT):
                    ins = nc.tensor.transpose(b[:, t * P:(t + 1) * P], misc[:, 1, t * P:(t + 1) * P], cst("ident"))
                ins.then_inc(a_full, 1)
                feat_group(("gd", 0), l, h_hi, h_lo, "a", "g_in")
                block_sums(l, "r_bsq", 2, R["tmp"], 2, "r_bon")
                for i in range(1, 6):
                    feat_group(("gd", i), l, h_hi, h_lo, "a", "g_in")
                pe.wait_ge(S["r_feat"], at(l, "r_feat", 4))
                transposes((R["et"], R["rm"][:, 4:6, :], R["bh"], R["kh"]), "r")
                pair_matrices(R["bz"], R["et"], "r")
                pair_matrices(R["kz"], R["et"], "r")
                pair_matrices(R["kz"], R["rt"], "r")
                pair_matrices(R["bz"], R["rt"], "r")
                invert(l, "r", R, lambda n: None)
                pe.wait_ge(S["r_tok"], at(l, "r_tok", 8))
                for t in range(TT):
                    block_products("v", "r_y1", t, R["akk"], of_pair(R["v_tok"]))
                pe.wait_ge(S["r_y1"], at(l, "r_y1", TT))
                through(l, "r", R, R["y1"])
                scan(l, "r", R, lambda c: None)
                feat_group(("gd", 6), l, h_hi, h_lo, "a", "g_z")
                block_sums(l, "r_o", NC, R["o"], 2, "r_mean")
                feat_group(("gd", 7), l, h_hi, h_lo, "a", "g_z")
                block_sums(l, "r_sq2", 1, R["sq"], 2, "r_gv")

                block_sums(l, "g_sq", 1, G["sq"], 4, "g_l2")
                numbers = gates(l, 2, 0)
                more = gates(l, 2, 1)
                pe.wait_ge(S["r_out"], at(l, "r_out", 1))
                merge_outputs(0, numbers)
                merge_outputs(0, more)
                pe.wait_ge(S["g_g"], at(l, "g_g", 2))
                for src, rhs in (("g", "upto"), ("g", "after"), ("b", "ident")):
                    for f in range(2):
                        b, reader, emptied = banks.next("a", "g_feat")
                        pe.wait_ge(reader, emptied)
                        for t in range(TT):
                            m = t * H + 2 * f
                            wide = G["g_wide" if src == "g" else "b_wide"][:, m * C:(m + 2) * C]
                            ins = mm(b[:, t * P:(t + 1) * P], wide, cst(rhs), start=True, stop=True)
                        ins.then_inc(a_full, 1)
                b, reader, emptied = banks.next("v", "g_gc")
                pe.wait_ge(reader, emptied)
                mm(b[:, 0:M], cst("upto"), gsm[:, 4, :], start=True, stop=True).then_inc(v_full, 1)
                for t in range(TT):
                    b, reader, emptied = banks.next("v", "g_row")
                    pe.wait_ge(reader, emptied)
                    for h in range(H):
                        ins = mm(b[:, h * P:(h + 1) * P], gsm[:, 4, t * H + h:t * H + h + 1].to_broadcast([P, P]), cst("upto"),
                                 start=True, stop=True)
                    ins.then_inc(v_full, 1)
                merge(l, 2, 0, 2)
                merge(l, 2, 0, 3)
                pe.wait_ge(S["g_prep"], at(l, "g_prep", 2))
                transposes((G["et"], G["vb"], G["bh"]), "g")
                pair_matrices(G["kz"], G["kb"], "g")
                pair_matrices(G["kz"], G["co"][:, 0:2, :], "g")
                invert(l, "g", G, lambda n: None)
                pe.wait_ge(S["g_tok"], at(l, "g_tok", 6))
                through(l, "g", G, G["v_tok"])
                scan(l, "g", G, lambda c: None)
                def index_scores(qt):
                    for h in range(8):
                        b, reader, emptied = banks.next("a", "d_sc")
                        pe.wait_ge(reader, emptied)
                        mm(b[:, 0:(qt + 1) * P], Dv["iq"][:, h // 2, qt * P:(qt + 1) * P], Dv["ikz"][:, h % 2, 0:(qt + 1) * P],
                           start=True, stop=True).then_inc(a_full, 1)

                for i in range(10):
                    if i == 7:
                        pe.wait_ge(S["d_rot"], at(l, "d_rot", 4))
                        index_scores(1)
                    if i == 1:
                        block_sums(l, "g_sq2", 1, G["sq2"], 2, "g_gv")
                    feat_group(("ds", i), l, h_hi, h_lo, "a", "d_in" if i < 8 else "d_vf")
                    if i == 1:
                        for nm in ("dup", "dup_rot"):
                            b, reader, emptied = banks.next("v", "d_ik")
                            pe.wait_ge(reader, emptied)
                            mm(b[:], cst(nm), misc[:, 1, :], start=True, stop=True).then_inc(v_full, 1)
                    if 2 <= i:
                        j = i - 2
                        src = Dv["iq"][:, j, :] if j < 4 else Dv["q"][:, j - 4, :] if j < 6 else Dv["k"][:, j - 6, :]
                        b, reader, emptied = banks.next("v", "d_rot")
                        pe.wait_ge(reader, emptied)
                        pe.wait_ge(S["d_in"], at(l, "d_in", j + 1))
                        mm(b[:], cst("rot_d"), src, start=True, stop=True).then_inc(v_full, 1)
                pe.wait_ge(S["d_vf"], at(l, "d_vf", 2))
                for half in range(2):
                    b, reader, emptied = banks.next("a", "d_v")
                    pe.wait_ge(reader, emptied)
                    for t2 in range(2):
                        for f in range(2):
                            t = 2 * half + t2
                            ins = nc.tensor.transpose(b[:, t2 * 256 + f * P:t2 * 256 + (f + 1) * P], Dv["vf"][:, f, t * P:(t + 1) * P], cst("ident"))
                    ins.then_inc(a_full, 1)
                for qt in range(1, TT):
                    if qt > 1:
                        index_scores(qt)
                    merge(l, 0, 1, qt - 1)
                    if qt == 2:
                        for i in range(2):
                            feat_group(("cq", i), l, h_hi, h_lo, "a", "m_in")
                merge(l, 0, 1, 3)
                numbers = []
                pieces = gate_pieces(l, 3, 0, numbers)
                pe.wait_ge(S["d_rot"], at(l, "d_rot", 8))
                pe.wait_ge(S["d_kz"], at(l, "d_kz", 2))
                attention(l, "d", lambda h, qt: Dv["q"][:, h // 2, qt * P:(qt + 1) * P],
                          lambda h, n: Dv["kz"][:, h // 2, h % 2, 0:n], Dv["v"], lambda i: next(pieces) if i in GATE_STEPS else None)

                more = gates(l, 3, 1)
                pe.wait_ge(S["d_o"], at(l, "d_o", 16))
                merge_outputs(0, numbers)
                merge_outputs(0, more)
                pe.wait_ge(S["m_sq"], at(l, "m_sq", 1))
                b, reader, emptied = banks.next("v", "m_nv")
                pe.wait_ge(reader, emptied)
                for k in range(2):
                    ins = mm(b[:], cst("ones"), Mv["sq"][:, k, :], start=k == 0, stop=k == 1)
                ins.then_inc(v_full, 1)
                b, reader, emptied = banks.next("v", "m_nv")
                pe.wait_ge(reader, emptied)
                mm(b[:], cst("ones"), Mv["sq"][:, 2, :], start=True, stop=True).then_inc(v_full, 1)
                merge(l, 3, 0, 2)
                pe.wait_ge(S["m_c"], at(l, "m_c", 1))
                for h in range(H):
                    b, reader, emptied = banks.next("a", "m_q")
                    pe.wait_ge(reader, emptied)
                    for k in range(2):
                        ins = mm(b[0:96, :], pr("uq")[:, k * 384 + h * 96:k * 384 + (h + 1) * 96], Mv["cq"][:, k, :], start=k == 0, stop=k == 1)
                    ins.then_inc(a_full, 1)
                for h in range(H):
                    b, reader, emptied = banks.next("a", "m_k")
                    pe.wait_ge(reader, emptied)
                    mm(b[0:64, :], pr("ukv")[:, h * P:h * P + C], misc[:, 0, :], start=True, stop=True).then_inc(a_full, 1)
                for half in range(2):
                    b, reader, emptied = banks.next("a", "m_v")
                    pe.wait_ge(reader, emptied)
                    for t2 in range(2):
                        t = 2 * half + t2
                        ins = mm(b[:, t2 * 256:(t2 + 1) * 256], misc[:, 0, t * P:(t + 1) * P],
                                 pr("ukv").rearrange("p (h n) -> p h n", n=P)[:, :, C:P], start=True, stop=True)
                    ins.then_inc(a_full, 1)
                b, reader, emptied = banks.next("v", "m_krb")
                pe.wait_ge(reader, emptied)
                mm(b[0:96, :], cst("rot_m")[64:96, 0:96], misc[64:96, 1, :], start=True, stop=True).then_inc(v_full, 1)
                for h in range(H):
                    b, reader, emptied = banks.next("v", "m_rot")
                    pe.wait_ge(reader, emptied)
                    pe.wait_ge(S["m_q"], at(l, "m_q", h + 1))
                    mm(b[0:96, :], cst("rot_m")[0:96, 0:96], Mv["q"][0:96, h, :], start=True, stop=True).then_inc(v_full, 1)
                merge(l, 3, 0, 3)
                pe.wait_ge(S["m_rot"], at(l, "m_rot", 4))
                pe.wait_ge(S["m_kr"], at(l, "m_kr", 4))
                pe.wait_ge(S["m_k"], at(l, "m_k", 4))
                pe.wait_ge(S["m_v"], at(l, "m_v", 2))
                numbers = []
                pieces = gate_pieces(l, 1, 0, numbers)
                attention(l, "m", lambda h, qt: Mv["q"][0:96, h, qt * P:(qt + 1) * P],
                          lambda h, n: Mv["k"][0:96, h, 0:n], Mv["v"], lambda i: next(pieces) if i in GATE_STEPS else None)
                more = gates(l, 1, 1)
                pe.wait_ge(S["m_o"], at(l, "m_o", 16))
                merge_outputs(1, numbers)
                merge_outputs(1, more)
                for i in range(2, 4):
                    merge(l, 1, 1, i)

                for i in range(8):
                    if i == 0:
                        feat_group(("wo", i), l, mg_hi, mg_lo, "v", "wo_done", "mg_lo", at(l, "mg_lo", 0))
                    else:
                        feat_group(("wo", i), l, mg_hi, mg_lo, "v", "wo_done")
                norm_sum(2 * l + 1)
                for q in range(QUARTERS + 1):
                    if q < QUARTERS:
                        for i in range(8):
                            if q == 0 and i == 0:
                                feat_group(("up", i), l, h_hi, h_lo, "a", "up_relu", "n_h", at(l, "n_h", 8))
                            else:
                                feat_group(("up", 8 * q + i), l, h_hi, h_lo, "a", "up_relu")
                    if q >= 1:
                        for i in range(8):
                            hi, lo = up_hi[(q - 1) % 2], up_lo[(q - 1) % 2]
                            if i == 0:
                                feat_group(("down", q - 1, i), l, hi, lo, "v", "down_done", "up_done", at(l, "up_done", 8 * (q - 1)))
                            else:
                                feat_group(("down", q - 1, i), l, hi, lo, "v", "down_done")
            norm_sum(2 * L)
            for half in range(2):
                for t in range(TT):
                    b, reader, emptied = banks.next("a", "o_tok")
                    pe.wait_ge(reader, emptied)
                    if t == 0:
                        pe.wait_ge(S["n_g"], 16 * L + 4 * (half + 1))
                    for k in range(4):
                        ins = nc.tensor.transpose(b[:, k * P:(k + 1) * P], mg[:, 4 * half + k, t * P:(t + 1) * P], cst("ident"))
                    ins.then_inc(a_full, 1)

        @block.scalar
        def _(act):
            act_fn = nc.scalar.activation
            filled = Filled(bank_a)
            filled_f = Filled(bank_f)

            def invert(l, x, V, fill):
                for t in range(TT):
                    act.wait_ge(a_full, filled.next())
                    b = filled.bank()
                    act_fn(V["t_bd"][:, t * H:(t + 1) * H, :], b[:].rearrange("p (m n) -> p m n", n=P), ACT.Copy).then_inc(S[x + "_ti"], 1)
                for n in range(len(LEVELS)):
                    fill(n)

            def tok(l, x, V, names):
                for nm in names:
                    for half in range(2):
                        act.wait_ge(a_full, filled.next())
                        b = filled.bank()
                        if nm == "k_tokz":
                            for p in range(2):
                                rows = slice(p * C, (p + 1) * C)
                                last = act_fn(V[nm][rows, 2 * half:2 * half + 2, p, :],
                                              b[rows, :].rearrange("p (t n) -> p t n", n=256), ACT.Copy)
                        else:
                            last = act_fn(V[nm][:, 2 * half:2 * half + 2, :], b[:].rearrange("p (t n) -> p t n", n=256), ACT.Copy)
                        last.then_inc(S[x + "_tok"], 1)

            def after_inverse(l, x, V):
                for f in range(2):
                    act.wait_ge(a_full, filled.next())
                    b = filled.bank()
                    act_fn(V["wt"][:, f, :], b[:], ACT.Copy).then_inc(S[x + "_wt"], 1)
                for t in range(TT):
                    act.wait_ge(a_full, filled.next())
                    b = filled.bank()
                    for hp in range(2):
                        last = act_fn(own_half(V["up"][:, t, :], 2, hp), own_half(b[:], 4, 3 * hp), ACT.Copy)
                    last.then_inc(S[x + "_u"], 1)

            def outputs(l, x, V, fill):
                for c in range(NC):
                    act.wait_ge(a_full, filled.next())
                    b = filled.bank()
                    act_fn(V["o"][:, :, c * C:(c + 1) * C], b[:, 0:P].rearrange("p (f n) -> p f n", n=C), ACT.Copy).then_inc(S[x + "_o"], 1)
                    fill(c)

            sigs = [0]

            def merge_sig(l):
                for _ in range(2):
                    act.wait_ge(a_full, filled.next())
                    b = filled.bank()
                    n = sigs[0]
                    if n >= 2:
                        act.wait_ge(S["mg_done"], n - 1)
                    act_fn(sg[:, n % 2, :], b[:], ACT.Sigmoid).then_inc(S["mg_sig"], 1)
                    sigs[0] += 1
                    split_next()

            def piecewise_sig(l, i):
                if i in (GATE_STEPS[5], GATE_STEPS[11]):
                    act.wait_ge(f_full, filled_f.next())
                    n = sigs[0] + (i == GATE_STEPS[11])
                    if n >= 2:
                        act.wait_ge(S["mg_done"], n - 1)
                    act_fn(sg[:, n % 2, :], filled_f.bank()[:], ACT.Copy).then_inc(S["mg_raw"], 1)
                    split_next()

            def late_sig(l):
                act.wait_ge(S["mg_raw"], filled_f.n)
                for _ in range(2):
                    n = sigs[0]
                    act_fn(sg[:, n % 2, :], sg[:, n % 2, :], ACT.Sigmoid).then_inc(S["mg_sig"], 1)
                    sigs[0] += 1

            units = [0]

            def split_next():
                g = units[0]
                if g < L * NU:
                    act.wait_ge(w_here[g % RING], 16 * (g // RING + 1))
                    act_fn(w_hi[:, g % SPLIT, :, :], ring[:, g % RING, :, :],
                           ACT.Copy).then_inc(S["split_hi"], 1)
                    units[0] += 1

            def norm_squares(n, need, k0):
                for k in range(KT):
                    act.wait_ge(S[need], k0 + k + 1)
                    act_fn(squares[n % 2][:, k, :], xT[:, k, :], ACT.Square).then_inc(S["n_sq"], 1)

            def norm_root(n, parts=True):
                act.wait_ge(S["n_rec"], n + 1)
                act_fn(sg[:, 0, :], sg[:, 0, :], ACT.Sqrt).then_inc(S["n_rs"], 1)
                if parts:
                    for k in range(KT):
                        act.wait_ge(S["n_g"], n * KT + k + 1)
                        act_fn(h_hi[:, k, :], mg[:, k, :], ACT.Copy).then_inc(S["n_hi"], 1)

            def attention(l, x, V, fill):
                steps = [(qt, h) for qt in range(TT) for h in range(H)]
                for i in range(len(steps) + 3):
                    if i < len(steps):
                        qt, h = steps[i]
                        n = (qt + 1) * P
                        act.wait_ge(S[x + "_ss"], at(l, x + "_ss", i + 1))
                        act_fn(V["ss"][:, i % 4, 0:n], V["ss"][:, i % 4, 0:n], ACT.Exp, bias=att[:, 0, i % 4:i % 4 + 1], accum_out=att[:, 1, i % 4:i % 4 + 1]).then_inc(S[x + "_p"], 1)
                    if 2 <= i < len(steps) + 2:
                        j = i - 2
                        qt, h = steps[j]
                        act.wait_ge(a_full, filled.next())
                        b = filled.bank()
                        if j >= 2:
                            act.wait_ge(S[x + "_o"], at(l, x + "_o", j - 1))
                        act_fn(V["pt"][:, j % 2, 0:qt + 1, :], b[:, 0:(qt + 1) * P].rearrange("p (k n) -> p k n", n=P), ACT.Copy).then_inc(S[x + "_pt"], 1)
                    fill(i)

            split_next()
            split_next()
            for l in range(L):
                if l == 0:
                    norm_squares(0, "x_t", 0)
                norm_root(2 * l)
                if l == 0:
                    for i in range(2):
                        act.wait_ge(S["tab_arg"], i + 1)
                        act_fn(POS["sin"][:, i, :], POS["red"][:, i, :], ACT.Sin)
                        act_fn(POS["cos"][:, i, :], POS["red"][:, i, :], ACT.Sin, scale=0.5).then_inc(S["tab_sin"], 1)

                def take_rw(i):
                    act.wait_ge(a_full, filled.next())
                    b = filled.bank()
                    if i >= 4:
                        act.wait_ge(S["r_mix"], at(l, "r_mix", i - 3))
                    act_fn(R["rw"][:, i % 4, 1:T + 1], b[:], ACT.Copy).then_inc(S["r_in"], 1)
                    split_next()

                def take_low_rank(name, bias):
                    for f in range(2):
                        act.wait_ge(a_full, filled.next())
                        b = filled.bank()
                        if bias:
                            act_fn(R[name][:, f, :], b[:], ACT.Sigmoid, bias=pr(bias, f)).then_inc(S["r_lora"], 1)
                        else:
                            act_fn(R[name][:, f, :], b[:], ACT.Copy).then_inc(S["r_lora"], 1)

                for i in range(3):
                    take_rw(i)
                act.wait_ge(S["r_mix"], at(l, "r_mix", 1))
                act_fn(R["rm"][0:64, 6, :], R["rm"][0:64, 6, :], ACT.Tanh).then_inc(S["r_act"], 1)
                act.wait_ge(S["r_mix"], at(l, "r_mix", 2))
                act_fn(R["rm"][:, 7, :], R["rm"][:, 7, :], ACT.Sigmoid).then_inc(S["r_act"], 1)
                take_rw(3)
                act.wait_ge(par_here, 16 * (l + 1))
                take_low_rank("sw", "w0")
                take_low_rank("a", "a0")
                take_rw(4)
                take_low_rank("g", None)
                take_rw(5)
                act.wait_ge(S["r_l2r"], at(l, "r_l2r", 1))
                act_fn(R["tmp"], R["tmp"], ACT.Sqrt).then_inc(S["r_l2s"], 1)
                take_rw(6)
                act.wait_ge(S["r_cum"], at(l, "r_cum", 1))
                act_fn(R["p"], R["cs"], ACT.Exp, scale=-DECAY).then_inc(S["r_dec"], 1)
                act_fn(R["pi"], R["cs"], ACT.Exp, scale=DECAY).then_inc(S["r_dec"], 1)
                act.wait_ge(S["r_ex"], at(l, "r_ex", 1))
                act_fn(R["pe"], R["sw"], ACT.Exp, scale=-DECAY).then_inc(S["r_dec"], 1)
                take_rw(7)
                for i in range(2):
                    act.wait_ge(a_full, filled.next())
                    b = filled.bank()
                    act_fn(misc[:, i, :], b[:], ACT.Copy).then_inc(S["misc_in"], 1)
                    split_next()
                act.wait_ge(a_full, filled.next())
                b = filled.bank()
                act_fn(ab[:, :, :], b[:].rearrange("p (t n) -> p t n", n=P)[:, :, 96:112], ACT.Copy).then_inc(S["ab_in"], 1)
                for i in range(6):
                    act.wait_ge(a_full, filled.next())
                    b = filled.bank()
                    act_fn(G["ci"][:, i, :], b[:], ACT.Copy).then_inc(S["g_in"], 1)
                    split_next()
                act.wait_ge(S["r_feat"], at(l, "r_feat", 4))
                tok(l, "r", R, ("e_tok", "v_tok", "b_tok", "k_tokz"))
                invert(l, "r", R, lambda n: None)
                after_inverse(l, "r", R)

                def conv_sigmoid(c):
                    if 2 <= c:
                        act.wait_ge(S["g_conv"], at(l, "g_conv", c - 1))
                        act_fn(G["sig"][:, c - 2, :], conv_out(c - 2), ACT.Sigmoid).then_inc(S["g_sig"], 1)

                outputs(l, "r", R, conv_sigmoid)
                for i in range(2):
                    act.wait_ge(a_full, filled.next())
                    b = filled.bank()
                    act_fn(G["zi"][:, i, :], b[:], ACT.Copy).then_inc(S["g_z"], 1)
                    split_next()
                act_fn(gsm[:, 5, :], ab[:, :, 4:8], ACT.Sigmoid)
                act.wait_ge(S["g_z"], at(l, "g_z", 2))
                act_fn(G["bh"], G["zi"], ACT.Sigmoid).then_inc(S["g_zs"], 1)
                act.wait_ge(S["r_gr"], at(l, "r_gr", 1))
                act_fn(R["sq"], R["sq"], ACT.Sqrt).then_inc(S["r_gs"], 1)

                merge_sig(l)
                merge_sig(l)
                act.wait_ge(S["g_t1"], at(l, "g_t1", 1))
                act_fn(gsm[:, 1, :], gsm[:, 1, :], ACT.Exp).then_inc(act_step, 1)
                act_fn(sml[:, 8:12], pr("a_log"), ACT.Exp).then_inc(S["g_t2"], 1)
                act.wait_ge(act_step, l + 1)
                act_fn(gsm[:, 1, :], gsm[:, 1, :], ACT.Ln, bias=1.0).then_inc(S["g_sp"], 1)
                for i in range(6):
                    act.wait_ge(a_full, filled.next())
                    b = filled.bank()
                    f = i % 2
                    dst = (G["egc"], G["ers"], G["beta"])[i // 2][:, f, :]
                    act_fn(dst, b[:], ACT.Exp if i < 4 else ACT.Copy).then_inc(S["g_feat"], 1)
                for t in range(TT):
                    act.wait_ge(S["g_row"], at(l, "g_row", t + 1))
                    act_fn(G["d"][:, t * H:(t + 1) * H, :], G["d"][:, t * H:(t + 1) * H, :], ACT.Exp).then_inc(S["g_d"], 1)
                act.wait_ge(S["g_l2r"], at(l, "g_l2r", 1))
                act_fn(G["rs"], G["rs"], ACT.Sqrt).then_inc(S["g_l2s"], 1)
                merge_sig(l)
                merge_sig(l)
                act.wait_ge(S["g_prep"], at(l, "g_prep", 2))
                tok(l, "g", G, ("e_tok", "v_tok", "b_tok"))
                invert(l, "g", G, lambda n: None)
                after_inverse(l, "g", G)
                outputs(l, "g", G, lambda c: None)

                def rectify(qt):
                    n = (qt + 1) * P
                    for h in range(8):
                        i = 8 * (qt - 1) + h
                        act.wait_ge(a_full, filled.next())
                        b = filled.bank()
                        if i >= 2:
                            act.wait_ge(S["d_acc"], at(l, "d_acc", i - 1))
                        act_fn(Dv["rl"][:, i % 2, 0:n], b[:, 0:n], ACT.Relu).then_inc(S["d_sc"], 1)

                for i in range(8):
                    if i == 7:
                        rectify(1)
                    if i == 2:
                        act.wait_ge(S["g_gr"], at(l, "g_gr", 1))
                        act_fn(G["sq2"], G["sq2"], ACT.Sqrt).then_inc(S["g_gs"], 1)
                    act.wait_ge(a_full, filled.next())
                    b = filled.bank()
                    dst = Dv["iq"][:, i, :] if i < 4 else Dv["q"][:, i - 4, :] if i < 6 else Dv["k"][:, i - 6, :]
                    act_fn(dst, b[:], ACT.Copy).then_inc(S["d_in"], 1)
                    split_next()
                for f in range(2):
                    act.wait_ge(a_full, filled.next())
                    b = filled.bank()
                    act_fn(Dv["vf"][:, f, :], b[:], ACT.Copy).then_inc(S["d_vf"], 1)
                    split_next()
                for half in range(2):
                    act.wait_ge(a_full, filled.next())
                    b = filled.bank()
                    act_fn(Dv["v"][:, 2 * half:2 * half + 2, :], b[:].rearrange("p (t n) -> p t n", n=256), ACT.Copy).then_inc(S["d_v"], 1)
                for qt in range(1, TT):
                    if qt > 1:
                        rectify(qt)
                    merge_sig(l)
                    if qt == 2:
                        for j in range(2):
                            act.wait_ge(a_full, filled.next())
                            b = filled.bank()
                            act_fn(Mv["cq"][:, j, :], b[:], ACT.Copy).then_inc(S["m_in"], 1)
                            split_next()
                merge_sig(l)
                attention(l, "d", Dv, lambda i: piecewise_sig(l, i))
                late_sig(l)

                merge_sig(l)
                act.wait_ge(S["m_rec"], at(l, "m_rec", 1))
                act_fn(Mv["rs"], Mv["rs"], ACT.Sqrt).then_inc(S["m_rs"], 1)
                merge_sig(l)
                for h in range(H):
                    act.wait_ge(a_full, filled.next())
                    b = filled.bank()
                    act_fn(Mv["q"][0:96, h, :], b[0:96, :], ACT.Copy).then_inc(S["m_q"], 1)
                for h in range(H):
                    act.wait_ge(a_full, filled.next())
                    b = filled.bank()
                    act_fn(Mv["k"][0:64, h, :], b[0:64, :], ACT.Copy).then_inc(S["m_k"], 1)
                for half in range(2):
                    act.wait_ge(a_full, filled.next())
                    b = filled.bank()
                    act_fn(Mv["v"][:, 2 * half:2 * half + 2, :], b[:].rearrange("p (t n) -> p t n", n=256), ACT.Copy).then_inc(S["m_v"], 1)
                merge_sig(l)
                attention(l, "m", Mv, lambda i: piecewise_sig(l, i))
                late_sig(l)
                mg_tile = 0
                for i in range(4):
                    if i:
                        merge_sig(l)
                    for m in range(mg_tile, mg_tile + 2):
                        act.wait_ge(S["mg_done"], at(l, "mg_done", 24 + m + 1))
                        act_fn(mg_hi[:, m, :], mg[:, m, :], ACT.Copy).then_inc(S["mg_hi"], 1)
                    mg_tile += 2
                act.wait_ge(x_back, 16 * (l + 1))
                for m in range(8):
                    act.wait_ge(S["wo_done"], at(l, "wo_done", m + 1))
                    split_next()
                    act_fn(squares[1][:, m, :], xT[:, m, :], ACT.Square).then_inc(S["n_sq"], 1)
                norm_root(2 * l + 1)
                for q in range(QUARTERS + 1):
                    if q < QUARTERS:
                        for i in range(8):
                            n = 8 * q + i
                            act.wait_ge(a_full, filled.next())
                            b = filled.bank()
                            if n >= 2:
                                act.wait_ge(S["up_sq"], at(l, "up_sq", n - 1))
                            act_fn(relu[:, n % 2, :], b[:], ACT.Relu).then_inc(S["up_relu"], 1)
                            act.wait_ge(S["up_relu"], at(l, "up_relu", n + 1))
                            act_fn(up_hi[q % 2][:, i, :], relu[:, n % 2, :], ACT.Square).then_inc(S["up_hi"], 1)
                            split_next()
                    if q >= 1:
                        for m in range(8):
                            act.wait_ge(S["down_done"], at(l, "down_done", 8 * (q - 1) + m + 1))
                            split_next()
                            if q == QUARTERS:
                                act_fn(squares[0][:, m, :], xT[:, m, :], ACT.Square).then_inc(S["n_sq"], 1)
            norm_root(2 * L, False)
            for half in range(2):
                for t in range(TT):
                    act.wait_ge(a_full, filled.next())
                    b = filled.bank()
                    act_fn(xout[:, t, half * T:(half + 1) * T], b[:], ACT.Copy).then_inc(S["o_tok"], 1)

        @block.vector
        def _(dve):
            v = nc.vector
            filled = Filled(bank_v)
            counts = {}

            def reached(name):
                counts[name] = counts.get(name, 0) + 1
                return counts[name]

            def link(ins):
                ins.then_inc(dve_step, 1)
                dve.wait_ge(dve_step, reached("step"))

            def tt(out_, a, b, op):
                link(v.tensor_tensor(out_, a, b, op))

            def ts(out_, a, s1, s2, op0, op1=ALU.bypass):
                link(v.tensor_scalar(out_, a, s1, s2, op0, op1))

            def stt(out_, a, s, b, op0, op1):
                link(v.scalar_tensor_tensor(out_, a, s, b, op0, op1))

            MUL, ADD, SUB = ALU.mult, ALU.add, ALU.subtract
            hm = (cst("blocks")[:, 0:1], cst("blocks")[:, C:C + 1])

            def norm(n, gain, parts=True):
                dve.wait_ge(v_full, filled.next())
                b = filled.bank()
                v.tensor_scalar(sg[:, 0, :], b[:], 1.0 / D, EPS, MUL, ADD).then_inc(S["n_var"], 1)
                dve.wait_ge(S["n_var"], reached("n_var"))
                v.reciprocal(sg[:, 0, :], sg[:, 0, :]).then_inc(S["n_rec"], 1)
                dve.wait_ge(S["n_rec"], reached("n_rec"))
                dve.wait_ge(S["n_rs"], n + 1)
                for k in range(KT + 1):
                    if k < KT:
                        v.scalar_tensor_tensor(mg[:, k, :], xT[:, k, :], pr(gain, k), sg[:, 0, :], MUL, MUL).then_inc(S["n_g"], 1)
                    if parts and k >= 1:
                        dve.wait_ge(S["n_hi"], n * KT + k)
                        v.tensor_tensor(h_lo[:, k - 1, :], mg[:, k - 1, :], h_hi[:, k - 1, :].bitcast(F32), SUB).then_inc(S["n_h"], 1)

            def bank3(b, n):
                return b[:].rearrange("p (m n) -> p m n", n=n)

            def masked(x, dst, mask, count):
                for t in range(TT):
                    dve.wait_ge(v_full, filled.next())
                    b = filled.bank()
                    m = mask(t)
                    v.tensor_tensor(dst[:, t * H:(t + 1) * H, :], bank3(b, P), m, MUL).then_inc(S[x + "_mat"], 1)
                    dve.wait_ge(S[x + "_mat"], reached(x + "_mat"))

            def invert(l, x, V, fill):
                first = cst("first").unsqueeze(1).to_broadcast([P, H, P])
                eye = cst("ident").unsqueeze(1).to_broadcast([P, H, P])
                for t in range(TT):
                    ms = slice(t * H, (t + 1) * H)
                    tt(V["x_bd"][:, ms, :], V["u"][:, ms, :], first, MUL)
                    v.tensor_tensor(V["x_bd"][:, ms, :], V["x_bd"][:, ms, :], eye, ADD).then_inc(S[x + "_x1"], 1)
                    dve.wait_ge(S[x + "_x1"], reached(x + "_x1"))
                for n, s in enumerate(LEVELS):
                    lev = cst(f"level{s}").unsqueeze(1).to_broadcast([P, H, P])
                    for t in range(TT):
                        dve.wait_ge(v_full, filled.next())
                        b = filled.bank()
                        v.tensor_tensor(V["y_bd"][:, t * H:(t + 1) * H, :], bank3(b, P), lev, MUL).then_inc(S[x + "_y"], 1)
                    if n < len(LEVELS) - 1:
                        for t in range(TT):
                            ms = slice(t * H, (t + 1) * H)
                            dve.wait_ge(v_full, filled.next())
                            b = filled.bank()
                            v.tensor_tensor(V["t_bd"][:, ms, :], V["t_bd"][:, ms, :], bank3(b, P), SUB).then_inc(S[x + "_t"], 1)
                    for t in range(TT):
                        ms = slice(t * H, (t + 1) * H)
                        dve.wait_ge(v_full, filled.next())
                        b = filled.bank()
                        v.tensor_tensor(V["x_bd"][:, ms, :], V["x_bd"][:, ms, :], bank3(b, P), SUB).then_inc(S[x + "_x"], 1)
                    fill(n)

            def scan(l, x, V, fill):
                v.memset(s_z[:], 0.0).then_inc(S[x + "_s0"], 1)
                dve.wait_ge(S[x + "_s0"], reached(x + "_s0"))
                dve.wait_ge(S[x + "_u"], at(l, x + "_u", TT))
                for c in range(NC):
                    t, par_ = divmod(c, 2)
                    rows = slice(par_ * C, (par_ + 1) * C)
                    dve.wait_ge(v_full, filled.next())
                    b = filled.bank()
                    v.tensor_tensor(un_z[rows, par_, :], V["up"][rows, t, :], b[rows, 0:4 * C], SUB).then_inc(S[x + "_ws"], 1)
                    dve.wait_ge(S[x + "_ws"], reached(x + "_ws"))
                    dve.wait_ge(v_full, filled.next())
                    b = filled.bank()
                    for h in range(H):
                        f, hp = divmod(h, 2)
                        hr = slice(hp * C, (hp + 1) * C)
                        ins = v.scalar_tensor_tensor(out=s_z[hr, f, hp, :], in0=s_z[hr, f, hp, :], scalar=pc[hr, f, c:c + 1],
                                                     in1=b[hr, f * C:(f + 1) * C], op0=MUL, op1=ADD)
                    ins.then_inc(S[x + "_s"], 1)
                    dve.wait_ge(S[x + "_s"], reached(x + "_s"))
                    fill(c)

            merged = [0]

            def merge(l, first=False):
                for _ in range(2):
                    n = merged[0]
                    m = n % 8
                    dve.wait_ge(v_full, filled.next())
                    b = filled.bank()
                    dve.wait_ge(S["mg_sig"], n + 1)
                    s = sg[:, n % 2, :]
                    if first:
                        v.tensor_tensor(mg[:, m, :], b[:], s, MUL).then_inc(S["mg_done"], 1)
                        dve.wait_ge(S["mg_done"], reached("mg_done"))
                    else:
                        tt(s, b[:], s, MUL)
                        v.tensor_tensor(mg[:, m, :], mg[:, m, :], s, ADD).then_inc(S["mg_done"], 1)
                        dve.wait_ge(S["mg_done"], reached("mg_done"))
                    merged[0] += 1

            def attention(l, x, V, scale, bias, slot, fill):
                steps = [(qt, h) for qt in range(TT) for h in range(H)]
                for i in range(len(steps) + 3):
                    if i < len(steps):
                        qt, h = steps[i]
                        n = (qt + 1) * P
                        dve.wait_ge(v_full, filled.next())
                        b = filled.bank()
                        if i >= 4:
                            dve.wait_ge(S[x + "_pt"], at(l, x + "_pt", i - 3))
                        ss = V["ss"][:, i % 4, 0:n]
                        stt(ss, b[:, 0:n], scale, bias(qt), MUL, ADD)
                        v.tensor_reduce(att[:, 0, i % 4:i % 4 + 1], ss, AX_X, ALU.max, negate=True).then_inc(S[x + "_ss"], 1)
                        reached(x + "_ss")
                    if 1 <= i <= len(steps):
                        j = i - 1
                        qt, h = steps[j]
                        n = (qt + 1) * P
                        dve.wait_ge(S[x + "_p"], at(l, x + "_p", j + 1))
                        link(v.reciprocal(att[:, 2, j % 4:j % 4 + 1], att[:, 1, j % 4:j % 4 + 1]))
                        ss = V["ss"][:, j % 4, 0:n]
                        v.tensor_scalar(ss, ss, att[:, 2, j % 4:j % 4 + 1], None, MUL).then_inc(S[x + "_pn"], 1)
                        reached(x + "_pn")
                    if i >= 3:
                        qt, h = steps[i - 3]
                        dve.wait_ge(v_full, filled.next())
                        b = filled.bank()
                        rows = slice((h % 2) * C, (h % 2 + 1) * C)
                        v.tensor_copy(yo[rows, slot, h // 2, qt * P:(qt + 1) * P], b[rows, 0:P]).then_inc(S[x + "_o"], 1)
                        dve.wait_ge(S[x + "_o"], reached(x + "_o"))
                    fill(i)

            link(v.memset(un_z[:], 0.0))
            link(v.memset(misc[:], 0.0))
            dve.wait_ge(const_here, 16)
            for k in range(KT):
                dve.wait_ge(v_full, filled.next())
                b = filled.bank()
                v.tensor_copy(xT[:, k, :], b[:]).then_inc(S["x_t"], 1)
                dve.wait_ge(S["x_t"], reached("x_t"))

            for l in range(L):
                dve.wait_ge(par_here, 16 * (l + 1))
                norm(2 * l, "mix_g")
                if l == 0:
                    dve.wait_ge(more_here, 16)
                    dve.wait_ge(pos_here, 16)
                    link(v.tensor_copy(POS["f"], POS["i"]))
                    for i, nm in enumerate(rotors):
                        ts(POS["ang"], POS["f"], cst("freq_" + nm), None, MUL)
                        ts(POS["k"], POS["ang"], float(1.0 / (2.0 * np.pi)), MAGIC, MUL, ADD)
                        ts(POS["k"], POS["k"], MAGIC, None, SUB)
                        red = POS["red"][:, i, :]
                        stt(red, POS["k"], -TWO_PI[0], POS["ang"], MUL, ADD)
                        stt(red, POS["k"], -TWO_PI[1], red, MUL, ADD)
                        stt(red, POS["k"], -TWO_PI[2], red, MUL, ADD)
                        v.tensor_scalar(red, red, 3.1415925, -3.1415925, ALU.min, ALU.max).then_inc(S["tab_arg"], 1)
                        dve.wait_ge(S["tab_arg"], reached("tab_arg"))
                    for i in range(2):
                        dve.wait_ge(S["tab_sin"], i + 1)
                        cos = POS["cos"][:, i, :]
                        tt(cos, cos, cos, MUL)
                        v.tensor_scalar(cos, cos, -2.0, 1.0, MUL, ADD).then_inc(S["tab"], 1)
                        dve.wait_ge(S["tab"], reached("tab"))
                v.memset(R["rw"][:, :, 0:1], 0.0).then_inc(S["r_zero"], 1)
                dve.wait_ge(S["r_zero"], reached("r_zero"))
                ts(sml[:, 12:14], pr("k_a"), -1.0, 1.0, MUL, ADD)

                def mix(k):
                    i = RW_ORDER[k]
                    dve.wait_ge(S["r_in"], at(l, "r_in", k + 1))
                    tt(R["rm"][:, i, :], R["rw"][:, k % 4, 0:T], R["rw"][:, k % 4, 1:T + 1], SUB)
                    v.scalar_tensor_tensor(R["rm"][:, i, :], R["rm"][:, i, :], pr("mu", i), R["rw"][:, k % 4, 1:T + 1], MUL, ADD).then_inc(S["r_mix"], 1)
                    dve.wait_ge(S["r_mix"], reached("r_mix"))

                r_, k_, v_ = R["rm"][:, 0:2, :], R["rm"][:, 2:4, :], R["rm"][:, 4:6, :]
                for k in range(4):
                    mix(k)
                if l == 0:
                    dve.wait_ge(tab_out, 64)
                for f in range(2):
                    ts(R["kk"][:, f, :], k_[:, f, :], pr("k_k", f), None, MUL)
                v.tensor_tensor(R["tmp"], R["kk"], R["kk"], MUL).then_inc(S["r_sq"], 1)
                dve.wait_ge(S["r_sq"], reached("r_sq"))
                dve.wait_ge(S["r_lora"], at(l, "r_lora", 2))
                for f in range(2):
                    for c in range(NC):
                        cs = slice(c * C, (c + 1) * C)
                        ins = v.tensor_tensor_scan(R["cs"][:, f, cs], cst("ones")[:, 0:C], R["sw"][:, f, cs], 0.0, MUL, ADD)
                ins.then_inc(S["r_cum"], 1)
                dve.wait_ge(S["r_cum"], reached("r_cum"))
                v.tensor_tensor(R["sw"], R["cs"], R["sw"], SUB).then_inc(S["r_ex"], 1)
                dve.wait_ge(S["r_ex"], reached("r_ex"))
                mix(4)
                for f in range(2):
                    dve.wait_ge(v_full, filled.next())
                    b = filled.bank()
                    v.tensor_scalar(R["tmp"][:, f, :], b[:], EPS, None, ADD).then_inc(S["r_l2"], 1)
                    dve.wait_ge(S["r_l2"], reached("r_l2"))
                v.reciprocal(R["tmp"], R["tmp"]).then_inc(S["r_l2r"], 1)
                dve.wait_ge(S["r_l2r"], reached("r_l2r"))
                mix(5)
                dve.wait_ge(S["r_l2s"], at(l, "r_l2s", 1))
                tt(R["kk"], R["kk"], R["tmp"], MUL)
                dve.wait_ge(S["r_lora"], at(l, "r_lora", 4))
                for f in range(2):
                    ts(R["tmp"][:, f, :], R["a"][:, f, :], pr("k_a", f), sml[:, 12 + f:13 + f], MUL, ADD)
                tt(k_, k_, R["tmp"], MUL)
                mix(6)
                for f in range(2):
                    v.scalar_tensor_tensor(R["tmp"][:, f, :], k_[:, f, :], pr("r_k", f), r_[:, f, :], MUL, MUL).then_inc(S["r_bsq"], 1)
                    dve.wait_ge(S["r_bsq"], reached("r_bsq"))
                mix(7)
                dve.wait_ge(x_away, 16 * (l + 1))
                dve.wait_ge(S["r_dec"], at(l, "r_dec", 3))
                link(v.tensor_copy(pc[:], R["p"].rearrange("p f (c k) -> p f c k", k=C)[:, :, :, C - 1]))
                tt(R["et"], R["pe"], R["kk"], MUL)
                tt(R["rt"], R["p"], r_, MUL)
                for f in range(2):
                    dve.wait_ge(v_full, filled.next())
                    b = filled.bank()
                    v.tensor_tensor(R["bon"][:, f, :], b[:], v_[:, f, :], MUL).then_inc(S["r_bon"], 1)
                    dve.wait_ge(S["r_bon"], reached("r_bon"))
                tt(R["tmp"], R["kk"], R["a"], MUL)
                for hp in range(2):
                    stt(R["bz"][:, :, hp, :], R["pi"], hm[hp], R["tmp"], MUL, MUL)
                    stt(R["kz"][:, :, hp, :], R["pi"], hm[hp], k_, MUL, MUL)
                tt(R["bh"], R["tmp"], R["pi"], MUL)
                tt(R["kh"], k_, R["pi"], MUL)
                link(v.memset(R["k_tokz"], 0.0))
                for nm in ("bh", "kh"):
                    for f in range(2):
                        y = R[nm][:, f, :].rearrange("p (c k) -> p c k", k=C)
                        v.tensor_tensor(y, y, pc[:, f, :].unsqueeze(2).to_broadcast([P, NC, C]), MUL).then_inc(S["r_feat"], 1)
                        dve.wait_ge(S["r_feat"], reached("r_feat"))
                def conv(c):
                    y = conv_out(c)
                    dve.wait_ge(S["g_in"], at(l, "g_in", c + 1))
                    ts(y, G["ci"][:, c, :], pr("conv", 4 * c + 3), None, MUL)
                    for j in range(1, 3):
                        stt(y[:, j:T], G["ci"][:, c, 0:T - j], pr("conv", 4 * c + 3 - j), y[:, j:T], MUL, ADD)
                    v.scalar_tensor_tensor(y[:, 3:T], G["ci"][:, c, 0:T - 3], pr("conv", 4 * c), y[:, 3:T], MUL, ADD).then_inc(S["g_conv"], 1)
                    dve.wait_ge(S["g_conv"], reached("g_conv"))

                for c in range(6):
                    conv(c)
                before = cst("before").unsqueeze(1).to_broadcast([P, H, P])
                upto = cst("upto").unsqueeze(1).to_broadcast([P, H, P])
                masked("r", R["u"], lambda t: before, 4)
                dve.wait_ge(S["r_tok"], at(l, "r_tok", 8))
                masked("r", R["akk"], lambda t: before, 4)
                masked("r", R["ark"], lambda t: upto, 4)
                masked("r", R["arb"], lambda t: upto, 4)
                invert(l, "r", R, lambda n: None)
                for t in range(TT):
                    dve.wait_ge(v_full, filled.next())
                    b = filled.bank()
                    for hp in range(2):
                        ins = v.tensor_scalar(own_half(R["y1"][:, t, :], 2, hp), own_half(b[:], 4, 3 * hp), -1.0, None, MUL)
                    ins.then_inc(S["r_y1"], 1)

                scan(l, "r", R, lambda c: None)
                for f in range(2):
                    dve.wait_ge(v_full, filled.next())
                    b = filled.bank()
                    v.scalar_tensor_tensor(R["o"][:, f, :], b[:], -1.0 / C, R["o"][:, f, :], MUL, ADD).then_inc(S["r_mean"], 1)
                    dve.wait_ge(S["r_mean"], reached("r_mean"))
                v.tensor_tensor(R["sq"], R["o"], R["o"], MUL).then_inc(S["r_sq2"], 1)
                dve.wait_ge(S["r_sq2"], reached("r_sq2"))
                dve.wait_ge(S["g_sig"], at(l, "g_sig", 6))
                tt(G["co"][:, 0:2, :], mg[:, 6:8, :], G["sig"][:, 0:2, :], MUL)
                tt(G["co"][:, 2:6, :], mg[:, 0:4, :], G["sig"][:, 2:6, :], MUL)
                v.tensor_tensor(G["sq"], G["co"][:, 0:4, :], G["co"][:, 0:4, :], MUL).then_inc(S["g_sq"], 1)
                dve.wait_ge(S["g_sq"], reached("g_sq"))
                for f in range(2):
                    dve.wait_ge(v_full, filled.next())
                    b = filled.bank()
                    v.tensor_scalar(R["sq"][:, f, :], b[:], 1.0 / C, GN_EPS, MUL, ADD).then_inc(S["r_gv"], 1)
                    dve.wait_ge(S["r_gv"], reached("r_gv"))
                v.reciprocal(R["sq"], R["sq"]).then_inc(S["r_gr"], 1)
                dve.wait_ge(S["r_gr"], reached("r_gr"))
                for i in range(4):
                    dve.wait_ge(v_full, filled.next())
                    b = filled.bank()
                    v.tensor_scalar(G["rs"][:, i, :], b[:], EPS, None, ADD).then_inc(S["g_l2"], 1)
                    dve.wait_ge(S["g_l2"], reached("g_l2"))
                dve.wait_ge(S["r_gs"], at(l, "r_gs", 1))
                tt(R["o"], R["o"], R["sq"], MUL)
                for f in range(2):
                    ts(R["o"][:, f, :], R["o"][:, f, :], pr("ln_w", f), pr("ln_b", f), MUL, ADD)
                tt(R["o"], R["o"], R["bon"], ADD)
                v.tensor_tensor(yo[:, 0, :, :], R["o"], R["g"], MUL).then_inc(S["r_out"], 1)
                dve.wait_ge(S["r_out"], reached("r_out"))

                link(v.reciprocal(G["rs"][:, 2:4, :], G["rs"][:, 2:4, :]))
                merge(l, True)
                merge(l, True)
                dve.wait_ge(S["ab_in"], at(l, "ab_in", 1))
                th = lambda i: gsm[:, i, :].rearrange("p (t h) -> p t h", h=H)
                tt(th(0), ab[:, :, 0:4], pr("dt").unsqueeze(1).to_broadcast([P, TT, H]), ADD)
                v.scalar_tensor_tensor(gsm[:, 1, :], gsm[:, 0, :], -1.0, gsm[:, 0, :], MUL, ALU.min).then_inc(S["g_t1"], 1)
                dve.wait_ge(S["g_t1"], reached("g_t1"))
                ts(ab[:, :, 8:16], ab[:, :, 8:16], float((8 * 64) ** -0.5), None, MUL)
                dve.wait_ge(S["g_sp"], at(l, "g_sp", 1))
                stt(gsm[:, 2, :], gsm[:, 0, :], 0.0, gsm[:, 1, :], ALU.max, ADD)
                stt(th(4), th(2), -1.0, sml[:, 8:12].unsqueeze(1).to_broadcast([P, TT, H]), MUL, MUL)
                for i, nm in ((4, "g_wide"), (5, "b_wide")):
                    v.tensor_copy(G[nm].rearrange("p (m n) -> p m n", n=C), gsm[:, i, :].unsqueeze(2).to_broadcast([P, M, C])).then_inc(S["g_g"], 1)
                    dve.wait_ge(S["g_g"], reached("g_g"))
                dve.wait_ge(S["g_zs"], at(l, "g_zs", 1))
                tt(G["z"], G["zi"], G["bh"], MUL)
                q_, k_, v_ = G["co"][:, 0:2, :], G["co"][:, 2:4, :], G["co"][:, 4:6, :]
                dve.wait_ge(v_full, filled.next())
                b = filled.bank()
                v.tensor_copy(gsm[:, 3, :], b[:, 0:M]).then_inc(S["g_gc"], 1)
                dve.wait_ge(S["g_gc"], reached("g_gc"))
                for t in range(TT):
                    dve.wait_ge(v_full, filled.next())
                    b = filled.bank()
                    for h in range(H):
                        m = t * H + h
                        ins = v.tensor_scalar(G["d"][:, m, :], b[:, h * P:(h + 1) * P], gsm[:, 3, m:m + 1], 0.0, SUB, ALU.min)
                    ins.then_inc(S["g_row"], 1)
                    dve.wait_ge(S["g_row"], reached("g_row"))
                v.reciprocal(G["rs"][:, 0:2, :], G["rs"][:, 0:2, :]).then_inc(S["g_l2r"], 1)
                dve.wait_ge(S["g_l2r"], reached("g_l2r"))
                for t in range(TT):
                    dve.wait_ge(S["g_d"], at(l, "g_d", t + 1))
                    tt(G["d"][:, t * H:(t + 1) * H, :], G["d"][:, t * H:(t + 1) * H, :], upto, MUL)
                dve.wait_ge(S["g_l2s"], at(l, "g_l2s", 1))
                stt(G["co"][:, 0:2, :], G["co"][:, 0:2, :], C ** -0.5, G["rs"][:, 0:2, :], MUL, MUL)
                v.tensor_tensor(G["co"][:, 2:4, :], G["co"][:, 2:4, :], G["rs"][:, 2:4, :], MUL).then_inc(S["g_qk"], 1)
                dve.wait_ge(S["g_qk"], reached("g_qk"))
                dve.wait_ge(S["g_feat"], at(l, "g_feat", 6))
                link(v.tensor_copy(pc[:], G["egc"].rearrange("p f (c k) -> p f c k", k=C)[:, :, :, C - 1]))
                tt(G["kb"], k_, G["beta"], MUL)
                tt(G["rt"], q_, G["egc"], MUL)
                tt(G["et"], G["kb"], G["egc"], MUL)
                tt(G["bh"], k_, G["ers"], MUL)
                tt(G["vb"], v_, G["beta"], MUL)
                for hp in range(2):
                    v.tensor_scalar(G["kz"][:, :, hp, :], k_, hm[hp], None, MUL).then_inc(S["g_prep"], 1)
                    dve.wait_ge(S["g_prep"], reached("g_prep"))
                merge(l, True)
                merge(l, True)
                masked("g", G["u"], lambda t: G["d"][:, t * H:(t + 1) * H, :], 4)
                masked("g", G["arb"], lambda t: G["d"][:, t * H:(t + 1) * H, :], 4)
                dve.wait_ge(S["g_tok"], at(l, "g_tok", 6))
                invert(l, "g", G, lambda n: None)
                scan(l, "g", G, lambda c: None)
                dve.wait_ge(S["g_o"], at(l, "g_o", NC))
                v.tensor_tensor(G["sq2"], G["o"], G["o"], MUL).then_inc(S["g_sq2"], 1)
                dve.wait_ge(S["g_sq2"], reached("g_sq2"))
                for f in range(2):
                    dve.wait_ge(v_full, filled.next())
                    b = filled.bank()
                    v.tensor_scalar(G["sq2"][:, f, :], b[:], 1.0 / C, EPS, MUL, ADD).then_inc(S["g_gv"], 1)
                    dve.wait_ge(S["g_gv"], reached("g_gv"))
                v.reciprocal(G["sq2"], G["sq2"]).then_inc(S["g_gr"], 1)
                dve.wait_ge(S["g_gr"], reached("g_gr"))
                dve.wait_ge(S["g_gs"], at(l, "g_gs", 1))
                stt(G["o"], G["o"], pr("gdn_g", 0), G["sq2"], MUL, MUL)
                v.tensor_tensor(yo[:, 1, :, :], G["o"], G["z"], MUL).then_inc(S["g_out"], 1)
                dve.wait_ge(S["g_out"], reached("g_out"))

                dve.wait_ge(tab_d_here, 16 * (l + 1))
                cos, sin = Dv["tab"][:, 0, :], Dv["tab"][:, 1, :]
                link(v.memset(Dv["ikz"], 0.0))
                dve.wait_ge(v_full, filled.next())
                b = filled.bank()
                for hp in range(2):
                    hr = slice(hp * C, (hp + 1) * C)
                    ins = v.tensor_tensor(Dv["ikz"][hr, hp, :], b[hr, :], cos[hr, :], MUL)
                ins.then_inc(S["d_ik"], 1)
                dve.wait_ge(S["d_ik"], reached("d_ik"))
                dve.wait_ge(v_full, filled.next())
                b = filled.bank()
                v.tensor_tensor(Dv["tmp"], b[:], sin, MUL).then_inc(S["d_ik"], 1)
                dve.wait_ge(S["d_ik"], reached("d_ik"))
                for hp in range(2):
                    hr = slice(hp * C, (hp + 1) * C)
                    tt(Dv["ikz"][hr, hp, :], Dv["ikz"][hr, hp, :], Dv["tmp"][hr, :], ADD)
                def select(qt):
                    i = 8 * (qt - 1)
                    n = (qt + 1) * P
                    sc, wk, gt, eq, cum = (Dv[x_][:, 0:n] for x_ in ("sc", "wk", "gt", "eq", "cum"))
                    for h in range(8):
                        dve.wait_ge(S["d_sc"], at(l, "d_sc", i + 1))
                        iw, rl = ab[:, qt, 8 + h:9 + h], Dv["rl"][:, i % 2, 0:n]
                        if h == 0:
                            v.tensor_scalar(sc, rl, iw, None, MUL).then_inc(S["d_acc"], 1)
                            dve.wait_ge(S["d_acc"], reached("d_acc"))
                        else:
                            v.scalar_tensor_tensor(sc, rl, iw, sc, MUL, ADD).then_inc(S["d_acc"], 1)
                            dve.wait_ge(S["d_acc"], reached("d_acc"))
                        i += 1
                    tt(sc[:, qt * P:n], sc[:, qt * P:n], cst("causal"), ADD)
                    src = sc
                    for r in range(TOPK // 8):
                        link(v.max(m8[:], src))
                        if r < TOPK // 8 - 1:
                            link(v.match_replace(wk, m8[:], src, -3e38))
                            src = wk
                    ts(gt, sc, m8[:, 7:8], None, ALU.is_gt)
                    link(v.tensor_reduce(sml[:, 6:7], gt, AX_X, ADD))
                    ts(sml[:, 7:8], sml[:, 6:7], -1.0, float(TOPK), MUL, ADD)
                    ts(eq, sc, m8[:, 7:8], None, ALU.is_equal)
                    link(v.tensor_tensor_scan(cum, eq, eq, 0.0, ADD, ALU.max))
                    stt(eq, cum, sml[:, 7:8], eq, ALU.is_le, MUL)
                    tt(gt, gt, eq, ADD)
                    v.tensor_scalar(Dv["bias"][:, qt, 0:n], gt, -NEG, NEG, MUL, ADD).then_inc(S["d_bias"], 1)
                    dve.wait_ge(S["d_bias"], reached("d_bias"))

                for i in range(8):
                    if i == 4:
                        select(1)
                    x_ = Dv["iq"][:, i, :] if i < 4 else Dv["q"][:, i - 4, :] if i < 6 else Dv["k"][:, i - 6, :]
                    dve.wait_ge(v_full, filled.next())
                    b = filled.bank()
                    tt(Dv["tmp"], b[:], sin, MUL)
                    tt(x_, x_, cos, MUL)
                    v.tensor_tensor(x_, x_, Dv["tmp"], ADD).then_inc(S["d_rot"], 1)
                    dve.wait_ge(S["d_rot"], reached("d_rot"))
                for hp in range(2):
                    v.tensor_scalar(Dv["kz"][:, :, hp, :], Dv["k"], hm[hp], None, MUL).then_inc(S["d_kz"], 1)
                    dve.wait_ge(S["d_kz"], reached("d_kz"))
                for qt in range(1, TT):
                    if qt > 1:
                        select(qt)
                    merge(l)
                merge(l)
                attention(l, "d", Dv, C ** -0.5, lambda qt: Dv["bias"][:, qt, 0:(qt + 1) * P] if qt else cst("causal"), 0, lambda i: None)

                dve.wait_ge(tab_m_here, 16 * (l + 1))
                rp = slice(64, 96)
                cos, sin = Mv["tab"][rp, 0, :], Mv["tab"][rp, 1, :]
                link(v.memset(Mv["bias"], 0.0))
                v.tensor_copy(Mv["bias"][:, 3 * P:T], cst("causal")).then_inc(S["m_bias"], 1)
                dve.wait_ge(S["m_bias"], reached("m_bias"))
                dve.wait_ge(S["m_in"], at(l, "m_in", 2))
                tt(Mv["sq"][:, 0:2, :], Mv["cq"], Mv["cq"], MUL)
                v.tensor_tensor(Mv["sq"][:, 2, :], misc[:, 0, :], misc[:, 0, :], MUL).then_inc(S["m_sq"], 1)
                dve.wait_ge(S["m_sq"], reached("m_sq"))
                merge(l)
                merge(l)
                dve.wait_ge(v_full, filled.next())
                b = filled.bank()
                v.tensor_scalar(Mv["rs"][:, 0, :], b[:], 1.0 / 256, EPS, MUL, ADD).then_inc(S["m_nv"], 1)
                dve.wait_ge(S["m_nv"], reached("m_nv"))
                dve.wait_ge(v_full, filled.next())
                b = filled.bank()
                v.tensor_scalar(Mv["rs"][:, 1, :], b[:], 1.0 / 128, EPS, MUL, ADD).then_inc(S["m_nv"], 1)
                dve.wait_ge(S["m_nv"], reached("m_nv"))
                v.reciprocal(Mv["rs"], Mv["rs"]).then_inc(S["m_rec"], 1)
                dve.wait_ge(S["m_rec"], reached("m_rec"))
                dve.wait_ge(S["m_rs"], at(l, "m_rs", 1))
                for f in range(2):
                    stt(Mv["cq"][:, f, :], Mv["cq"][:, f, :], pr("q_g", f), Mv["rs"][:, 0, :], MUL, MUL)
                v.scalar_tensor_tensor(misc[:, 0, :], misc[:, 0, :], pr("kv_g", 0), Mv["rs"][:, 1, :], MUL, MUL).then_inc(S["m_c"], 1)
                dve.wait_ge(S["m_c"], reached("m_c"))
                merge(l)
                dve.wait_ge(v_full, filled.next())
                b = filled.bank()
                v.tensor_tensor(Mv["tmp"][rp, :], b[rp, :], sin, MUL).then_inc(S["m_krb"], 1)
                dve.wait_ge(S["m_krb"], reached("m_krb"))
                tt(Mv["kr"][rp, :], misc[rp, 1, :], cos, MUL)
                for h in range(H):
                    v.tensor_tensor(Mv["k"][rp, h, :], Mv["kr"][rp, :], Mv["tmp"][rp, :], ADD).then_inc(S["m_kr"], 1)
                    dve.wait_ge(S["m_kr"], reached("m_kr"))
                for h in range(H):
                    dve.wait_ge(v_full, filled.next())
                    b = filled.bank()
                    tt(Mv["tmp"][rp, :], b[rp, :], sin, MUL)
                    x_ = Mv["q"][rp, h, :]
                    tt(x_, x_, cos, MUL)
                    v.tensor_tensor(x_, x_, Mv["tmp"][rp, :], ADD).then_inc(S["m_rot"], 1)
                    dve.wait_ge(S["m_rot"], reached("m_rot"))
                merge(l)
                attention(l, "m", Mv, 96 ** -0.5, lambda qt: Mv["bias"][:, (3 - qt) * P:T], 1, lambda i: None)
                for i in range(5):
                    if i < 4:
                        merge(l)
                    if i >= 1:
                        for m in range(2 * i - 2, 2 * i):
                            dve.wait_ge(S["mg_hi"], at(l, "mg_hi", m + 1))
                            v.tensor_tensor(mg_lo[:, m, :], mg[:, m, :], mg_hi[:, m, :].bitcast(F32), SUB).then_inc(S["mg_lo"], 1)
                dve.wait_ge(x_back, 16 * (l + 1))
                for m in range(KT):
                    dve.wait_ge(v_full, filled.next())
                    b = filled.bank()
                    v.tensor_tensor(xT[:, m, :], xT[:, m, :], b[:], ADD).then_inc(S["wo_done"], 1)
                    dve.wait_ge(S["wo_done"], reached("wo_done"))
                norm(2 * l + 1, "mlp_g")
                for q in range(QUARTERS + 1):
                    if q < QUARTERS:
                        for i in range(8):
                            n = 8 * q + i
                            dve.wait_ge(S["up_relu"], at(l, "up_relu", n + 1))
                            v.tensor_tensor(relu2[:, n % 2, :], relu[:, n % 2, :], relu[:, n % 2, :], MUL).then_inc(S["up_sq"], 1)
                            dve.wait_ge(S["up_sq"], reached("up_sq"))
                            dve.wait_ge(S["up_hi"], at(l, "up_hi", n + 1))
                            v.tensor_tensor(up_lo[q % 2][:, i, :], relu2[:, n % 2, :], up_hi[q % 2][:, i, :].bitcast(F32), SUB).then_inc(S["up_done"], 1)
                            dve.wait_ge(S["up_done"], reached("up_done"))
                    if q >= 1:
                        for m in range(KT):
                            dve.wait_ge(v_full, filled.next())
                            b = filled.bank()
                            v.tensor_tensor(xT[:, m, :], xT[:, m, :], b[:], ADD).then_inc(S["down_done"], 1)
                            dve.wait_ge(S["down_done"], reached("down_done"))
            norm(2 * L, "fin_g", False)


def stream_layout(w):
    out = np.zeros((L * NU, P, SLOT), np.float32)
    w_outs = [w["w_out_gdn"], w["w_out_mla"], w["w_out_rwkv"], w["w_out_dsa"]]

    def tiles(a):
        return a.reshape(-1, P, a.shape[1]).transpose(1, 0, 2)

    for l in range(L):
        wi = w["w_in"][l]
        for u, unit in enumerate(UNITS):
            dst = out[l * NU + u].reshape(P, 10, P)
            kind, i = unit[0], unit[-1]
            if kind == "rw":
                dst[:, 0:8] = tiles(wi[:, RWK0 + P * RW_ORDER[i]:RWK0 + P * (RW_ORDER[i] + 1)])
            elif kind == "gd":
                c = GDN0 + P * i if i < 6 else GDN0 + 776 + P * (i - 6)
                dst[:, 0:8] = tiles(wi[:, c:c + P])
            elif kind == "misc":
                parts = ((MLA0 + 256, 128),) if i == 0 else ((DSA0 + 512, 64), (MLA0 + 384, 32), (GDN0 + 768, 8), (DSA0 + 576, 8))
                at = 0
                for c, n in parts:
                    dst[:, 0:8, at:at + n] = tiles(wi[:, c:c + n])
                    at += n
            elif kind == "ds":
                c = DSA0 + (P * i if i < 4 else 584 + P * (i - 4))
                dst[:, 0:8] = tiles(wi[:, c:c + P])
            elif kind == "cq":
                dst[:, 0:8] = tiles(wi[:, MLA0 + P * i:MLA0 + P * (i + 1)])
            elif kind == "merge":
                br = unit[1]
                c = GATE0 + D * br + P * i
                dst[:, 0:8] = tiles(wi[:, c:c + P])
                dst[:, 8:10] = tiles(w_outs[br][l][:, P * i:P * (i + 1)])
            elif kind == "wo":
                dst[:, 0:8] = tiles(w["w_o"][l][:, P * i:P * (i + 1)])
            elif kind == "up":
                dst[:, 0:8] = tiles(w["w_up"][l][:, P * i:P * (i + 1)])
            else:
                q = unit[1]
                dst[:, 0:8] = tiles(w["w_down"][l][D * q:D * (q + 1), P * i:P * (i + 1)])
    return out


def par_layout(w):
    out = np.zeros((L, P, NPAR), np.float32)

    def put(l, name, a):
        at, n = PAR[name]
        out[l, :, at:at + n] = a

    for l in range(L):
        col = lambda a: a.reshape(-1, P).T
        put(l, "mix_g", col(w["mix_norm_g"][l]))
        put(l, "mlp_g", col(w["mlp_norm_g"][l]))
        put(l, "fin_g", col(w["final_norm_g"]))
        put(l, "conv", w["gdn_conv_w"][l].reshape(4, 6, P).transpose(2, 1, 0).reshape(P, 24))
        put(l, "mu", col(w["rwkv_mu"][l]))
        for name, key in (("w0", "rwkv_w0"), ("a0", "rwkv_a0"), ("k_k", "rwkv_k_k"), ("k_a", "rwkv_k_a"),
                          ("ln_w", "rwkv_ln_w"), ("ln_b", "rwkv_ln_b"), ("q_g", "mla_q_norm_g"), ("kv_g", "mla_kv_norm_g")):
            put(l, name, col(w[key][l]))
        put(l, "r_k", col(w["rwkv_r_k"][l].reshape(-1)))
        put(l, "gdn_g", np.concatenate([w["gdn_norm_g"][l]] * 2)[:, None])
        put(l, "a_log", np.broadcast_to(w["gdn_a_log"][l], (P, H)))
        put(l, "dt", np.broadcast_to(w["gdn_dt_bias"][l], (P, H)))
        put(l, "wa2", np.concatenate([w["rwkv_w_w2"][l], w["rwkv_w_a2"][l]]))
        put(l, "g2", w["rwkv_w_g2"][l])
        put(l, "uq", w["mla_w_uq"][l].reshape(2, P, 384).transpose(1, 0, 2).reshape(P, 768))
        put(l, "ukv", w["mla_w_ukv"][l])
    return out


def kernel(**inputs):
    import concourse.bacc as bacc
    from concourse.bass_utils import run_bass_kernel_spmd as run

    w = {k: np.asarray(a) for k, a in inputs.items()}
    arrays = {
        "in_x": np.ascontiguousarray(w["x"][0]),
        "in_pos": np.ascontiguousarray(w["positions"][0]),
        "in_w": stream_layout(w),
        "in_par": par_layout(w),
        "in_const": CONST_ARRAY,
    }
    nc = bacc.Bacc("TRN2", target_bir_lowering=False, num_devices=1)
    aps = [nc.dram_tensor(n, a.shape, mybir.dt.from_np(a.dtype), kind="ExternalInput").ap() for n, a in arrays.items()]
    tabs = nc.dram_tensor("tabs", (2, 2, P, T), F32, kind="Internal").ap()
    x_dram = nc.dram_tensor("x_dram", (P, KT, T), F32, kind="Internal").ap()
    out = nc.dram_tensor("out_x", (T, D), F32, kind="ExternalOutput").ap()
    build(nc, *aps, tabs, x_dram, out)
    r = run(nc, [arrays], core_ids=[0])
    return r.results[0]["out_x"].reshape(1, T, D)
```
